# Optimizing a Trainium2 kernel written in Bass

```python
import jax, jax.numpy as jnp
from jax import lax
import numpy as np

D_MODEL = 1024
BATCH = 1
SEQ = 512
DEPTH = 1

GLA_HEADS = 4
GLA_DK = 64
GLA_DV = 128
GLA_LOWRANK = 16
GLA_GATE_NORM = 16.0
GLA_CHUNK = 64
SWA_HEADS = 8
SWA_KV_HEADS = 2
SWA_HD = 64
WINDOW = 128
ROPE_THETA = 500000.0
ROPE_DIMS = SWA_HD // 4
N_GROUPS = 4
EXPERTS_PER_GROUP = 8
TOP_K_IN_GROUP = 2
D_EXPERT = 256

EPS = 1e-6
GLA_WIDTH = GLA_HEADS * GLA_DV
SWA_WIDTH = SWA_HEADS * SWA_HD
MIX_WIDTH = GLA_WIDTH + SWA_WIDTH
IN_SIZES = (GLA_HEADS * GLA_DK,
            GLA_HEADS * GLA_DK,
            GLA_WIDTH,
            GLA_WIDTH,
            GLA_LOWRANK,
            SWA_WIDTH,
            SWA_KV_HEADS * SWA_HD,
            SWA_KV_HEADS * SWA_HD)
IN_WIDTH = sum(IN_SIZES)

kernel_name = "hymba_gla_swa_sink_hier_moe_adaln"

def rmsnorm(x, g):
    x32 = x.astype(jnp.float32)
    y = x32 * lax.rsqrt(jnp.mean(x32 * x32, axis=-1, keepdims=True) + EPS)
    return y.astype(x.dtype) * g

def rope_tables(positions):
    inv_freq = ROPE_THETA ** (-jnp.arange(0, ROPE_DIMS, 2, dtype=jnp.float32) / ROPE_DIMS)
    ang = positions.astype(jnp.float32)[..., None] * inv_freq
    return jnp.cos(ang)[:, :, None, :], jnp.sin(ang)[:, :, None, :]

def partial_rope(x, cos, sin):
    half = ROPE_DIMS // 2
    x32 = x.astype(jnp.float32)
    x1, x2, rest = x32[..., :half], x32[..., half:ROPE_DIMS], x32[..., ROPE_DIMS:]
    out = jnp.concatenate([x1 * cos - x2 * sin, x2 * cos + x1 * sin, rest], axis=-1)
    return out.astype(x.dtype)

def gla_mixer(q, k, v, g_out, a_low, w_a2, b_a2, gn_gain):
    B, S = q.shape[:2]
    nc, C, H, dk, dv = S // GLA_CHUNK, GLA_CHUNK, GLA_HEADS, GLA_DK, GLA_DV
    f32 = jnp.float32
    log_a = jax.nn.log_sigmoid((a_low @ w_a2 + b_a2).astype(f32)) / GLA_GATE_NORM
    log_a = log_a.reshape(B, nc, C, H, dk)
    qc = q.astype(f32).reshape(B, nc, C, H, dk) * (dk ** -0.5)
    kc = k.astype(f32).reshape(B, nc, C, H, dk)
    vc = v.astype(f32).reshape(B, nc, C, H, dv)
    b = jnp.cumsum(log_a, axis=2)
    b_last = b[:, :, -1:]
    q_dec = qc * jnp.exp(b)
    k_dec = kc * jnp.exp(-b)
    causal = jnp.tril(jnp.ones((C, C), dtype=bool))
    scores = jnp.einsum('bnthd,bnshd->bnhts', q_dec, k_dec)
    scores = jnp.where(causal, scores, 0.0)
    o_intra = jnp.einsum('bnhts,bnshe->bnthe', scores, vc)
    kv = jnp.einsum('bnshd,bnshe->bnhde', kc * jnp.exp(b_last - b), vc)
    decay = jnp.exp(b_last[:, :, 0])

    def step(state, inp):
        kv_n, dec_n = inp
        return dec_n[..., None] * state + kv_n, state

    s0 = jnp.zeros((B, H, dk, dv), f32)
    _, s_prev = lax.scan(step, s0, (jnp.moveaxis(kv, 1, 0), jnp.moveaxis(decay, 1, 0)))
    s_prev = jnp.moveaxis(s_prev, 0, 1)
    o_inter = jnp.einsum('bnthd,bnhde->bnthe', q_dec, s_prev)
    o = (o_intra + o_inter).reshape(B, S, H, dv)
    o = rmsnorm(o, gn_gain)
    o = o * jax.nn.silu(g_out.astype(f32).reshape(B, S, H, dv))
    return o.reshape(B, S, H * dv).astype(q.dtype)

def swa_sink_mixer(q, k, v, sinks, cos, sin):
    B, S = q.shape[:2]
    W, hd, Hkv = WINDOW, SWA_HD, SWA_KV_HEADS
    G = SWA_HEADS // Hkv
    nb = S // W
    q = partial_rope(q.reshape(B, S, SWA_HEADS, hd), cos, sin)
    k = partial_rope(k.reshape(B, S, Hkv, hd), cos, sin)
    qb = q.reshape(B, nb, W, Hkv, G, hd) * (hd ** -0.5)
    kb = k.reshape(B, nb, W, Hkv, hd)
    vb = v.reshape(B, nb, W, Hkv, hd)
    pad = ((0, 0), (1, 0), (0, 0), (0, 0), (0, 0))
    kk = jnp.concatenate([jnp.pad(kb, pad)[:, :-1], kb], axis=2)
    vv = jnp.concatenate([jnp.pad(vb, pad)[:, :-1], vb], axis=2)
    scores = jnp.einsum('bnqkgd,bnskd->bnkgqs', qb, kk).astype(jnp.float32)
    q_pos = jnp.arange(W)[:, None] + W
    k_pos = jnp.arange(2 * W)[None, :]
    rel = q_pos - k_pos
    band = (rel >= 0) & (rel < W)
    blk = jnp.arange(nb)[:, None, None]
    valid = band[None] & ((blk > 0) | (k_pos[None] >= W))
    scores = jnp.where(valid[None, :, None, None], scores, -jnp.inf)
    sink = jnp.broadcast_to(sinks.astype(jnp.float32).reshape(Hkv, G)[None, None, :, :, None, None],
                            scores.shape[:-1] + (1,))
    probs = jax.nn.softmax(jnp.concatenate([scores, sink], axis=-1), axis=-1)[..., :-1]
    out = jnp.einsum('bnkgqs,bnskd->bnqkgd', probs.astype(vv.dtype), vv)
    return out.reshape(B, S, SWA_HEADS * hd)

def hier_moe(h, w_grp, b_grp, w_exp, b_exp, w_gate, w_up, w_down):
    T = h.shape[0]
    grp_logits = (h @ w_grp + b_grp).astype(jnp.float32)
    grp_prob = jax.nn.softmax(grp_logits, axis=-1)
    grp_idx = jnp.argmax(grp_logits, axis=-1)
    grp_gate = jnp.take_along_axis(grp_prob, grp_idx[:, None], axis=1)[:, 0]
    exp_logits = (h @ w_exp + b_exp).astype(jnp.float32).reshape(T, N_GROUPS, EXPERTS_PER_GROUP)
    sel_logits = jnp.take_along_axis(exp_logits, grp_idx[:, None, None], axis=1)[:, 0]
    top_vals, top_idx = lax.top_k(sel_logits, TOP_K_IN_GROUP)
    top_w = jax.nn.softmax(top_vals, axis=-1) * grp_gate[:, None]
    within = jnp.sum(jax.nn.one_hot(top_idx, EXPERTS_PER_GROUP, dtype=jnp.float32) * top_w[..., None], axis=1)
    combine = (jax.nn.one_hot(grp_idx, N_GROUPS, dtype=jnp.float32)[:, :, None] * within[:, None, :]).astype(h.dtype)
    out = jnp.zeros_like(h)
    for gi in range(N_GROUPS):
        a = jnp.einsum('td,edf->tef', h, w_gate[gi])
        u = jnp.einsum('td,edf->tef', h, w_up[gi])
        act = jax.nn.silu(a) * u * combine[:, gi, :, None]
        out = out + jnp.einsum('tef,efd->td', act, w_down[gi])
    return out

def setup_inputs(seed: int = 0) -> dict:
    key = jax.random.key(seed)
    ks = jax.random.split(key, 24)
    D, L = D_MODEL, DEPTH
    nrm = lambda k, shape, s: jax.random.normal(k, shape, jnp.float32) * s
    return {
        "x": nrm(ks[0], (BATCH, SEQ, D), 1.0),
        "c": nrm(ks[1], (BATCH, D), 1.0),
        "positions": (jnp.arange(SEQ, dtype=jnp.int32)[None, :]
                      + jax.random.randint(ks[2], (BATCH, 1), 0, 1024, dtype=jnp.int32)),
        "ada_w": nrm(ks[3], (L, D, 6 * D), D ** -0.5),
        "ada_b": nrm(ks[4], (L, 6 * D), 0.02),
        "norm_mix_g": 1.0 + nrm(ks[5], (L, D), 0.02),
        "w_in": nrm(ks[6], (L, D, IN_WIDTH), D ** -0.5),
        "gla_w_a2": nrm(ks[7], (L, GLA_LOWRANK, GLA_HEADS * GLA_DK), GLA_LOWRANK ** -0.5),
        "gla_b_a2": nrm(ks[8], (L, GLA_HEADS * GLA_DK), 0.02),
        "gla_norm_g": 1.0 + nrm(ks[9], (L, GLA_HEADS, GLA_DV), 0.02),
        "swa_sinks": nrm(ks[10], (L, SWA_HEADS), 0.5),
        "w_out": nrm(ks[11], (L, MIX_WIDTH, D), MIX_WIDTH ** -0.5),
        "norm_ffn_g": 1.0 + nrm(ks[12], (L, D), 0.02),
        "w_grp": nrm(ks[13], (L, D, N_GROUPS), D ** -0.5),
        "b_grp": nrm(ks[14], (L, N_GROUPS), 0.01),
        "w_exp": nrm(ks[15], (L, D, N_GROUPS * EXPERTS_PER_GROUP), D ** -0.5),
        "b_exp": nrm(ks[16], (L, N_GROUPS * EXPERTS_PER_GROUP), 0.01),
        "w_gate": nrm(ks[17], (L, N_GROUPS, EXPERTS_PER_GROUP, D, D_EXPERT), D ** -0.5),
        "w_up": nrm(ks[18], (L, N_GROUPS, EXPERTS_PER_GROUP, D, D_EXPERT), D ** -0.5),
        "w_down": nrm(ks[19], (L, N_GROUPS, EXPERTS_PER_GROUP, D_EXPERT, D), D_EXPERT ** -0.5),
        "final_norm_g": 1.0 + nrm(ks[20], (D,), 0.02),
    }

def reference(x, c, positions, ada_w, ada_b, norm_mix_g, w_in, gla_w_a2, gla_b_a2, gla_norm_g,
              swa_sinks, w_out, norm_ffn_g, w_grp, b_grp, w_exp, b_exp, w_gate, w_up, w_down,
              final_norm_g):
    B, S, D = x.shape
    cos, sin = rope_tables(positions)
    c_act = jax.nn.silu(c)
    split_pts = [int(p) for p in np.cumsum(IN_SIZES)[:-1]]
    for l in range(DEPTH):
        mod = (c_act @ ada_w[l] + ada_b[l])[:, None, :]
        sh_a, sc_a, gt_a, sh_f, sc_f, gt_f = jnp.split(mod, 6, axis=-1)
        h = rmsnorm(x, norm_mix_g[l]) * (1.0 + sc_a) + sh_a
        proj = h @ w_in[l]
        g_q, g_k, g_v, g_g, g_a, s_q, s_k, s_v = jnp.split(proj, split_pts, axis=-1)
        o_gla = gla_mixer(g_q, g_k, g_v, g_g, g_a, gla_w_a2[l], gla_b_a2[l], gla_norm_g[l])
        o_swa = swa_sink_mixer(s_q, s_k, s_v, swa_sinks[l], cos, sin)
        mix = jnp.concatenate([o_gla, o_swa], axis=-1) @ w_out[l]
        x = x + gt_a * mix
        h = rmsnorm(x, norm_ffn_g[l]) * (1.0 + sc_f) + sh_f
        y = hier_moe(h.reshape(B * S, D), w_grp[l], b_grp[l], w_exp[l], b_exp[l],
                     w_gate[l], w_up[l], w_down[l]).reshape(B, S, D)
        x = x + gt_f * y
    return rmsnorm(x, final_norm_g)


_drawn_inputs = setup_inputs


def setup_inputs(seed=0):
    import zlib

    import numpy as np

    out = dict(_drawn_inputs(seed))
    spreads = {}
    factors = {'gla_b_a2': 5.789,
     'gla_norm_g': 7.24,
     'swa_sinks': 17.935,
     'b_grp': 20.055,
     'b_exp': 20.404,
     'final_norm_g': 9.08,
     'norm_ffn_g': 4.301}
    for name, (base, spread) in spreads.items():
        noise = np.random.default_rng([zlib.crc32(name.encode()), seed]).standard_normal(out[name].shape)
        drawn = base * np.exp(spread * noise) if base else spread * noise
        out[name] = __import__('jax').numpy.asarray(drawn.astype(out[name].dtype))
    for name, factor in factors.items():
        out[name] = (out[name] * factor).astype(out[name].dtype)
    return out
```

```python
from contextlib import ExitStack

import numpy as np
import concourse.bass as bass
from concourse import mybir

P = 128
SEQ, D = 512, 1024
NB = SEQ // P
KD = D // P
GH, DK, DV, RANK = 4, 64, 128, 16
CHUNK = 64
SH, SKV, HD = 8, 2, 64
ROPE = HD // 4
HALF = ROPE // 2
THETA = 500000.0
NG, EPG = 4, 8
NE = NG * EPG
F = 256
FC = F // P
EPS = 1e-6
CQ, CK, CV, CG = 0, GH * DK, 2 * GH * DK, 2 * GH * DK + GH * DV
CA = CG + GH * DV
CSQ = CA + RANK
CSK = CSQ + SH * HD
CSV = CSK + SKV * HD
WIN = CSV + SKV * HD
CHUNKS = [(CA, CA + 512), (CA + 512, WIN), (CQ, CV), (CV, CG), (CG, CA)]
NCH = len(CHUNKS)
PARTS = [1, 0, 2, 4, 3, 5]
PC = 512
NPC = 2 * len(PARTS)
KH = KD // 2
CAP = 96
EXTRA = -(-SEQ // CAP) - 1
ROWS = (EXTRA + 1) * CAP
PAD = 8192
BIG = 1.0e30
SLOTS = 4

F32, I32, U32 = mybir.dt.float32, mybir.dt.int32, mybir.dt.uint32
ALU = mybir.AluOpType
ACT = mybir.ActivationFunctionType
AX = mybir.AxisListType.X

MIXER_ORDER = (
    [("proj", 0, b) for b in range(NB)] + [("proj", 1, b) for b in range(NB)]
    + [("rope",), ("proj", 2, 0), ("mod", 4), ("ga",), ("sA", 0), ("proj", 2, 1), ("mod", 5), ("sB", 0),
       ("proj", 2, 2), ("sD", 0), ("proj", 2, 3), ("sA", 1), ("sE", 0),
       ("proj", 3, 0), ("mod", 6), ("sB", 1), ("proj", 3, 1), ("mod", 7), ("sD", 1),
       ("proj", 3, 2), ("sA", 2), ("sE", 1), ("proj", 3, 3), ("mod", 8), ("sB", 2), ("gC", 0),
       ("proj", 4, 0), ("mod", 9), ("sD", 2), ("gD", 0), ("proj", 4, 1), ("sA", 3), ("sE", 2), ("gE", 0),
       ("proj", 4, 2), ("sB", 3), ("gF", 0), ("gC", 1), ("proj", 4, 3), ("sD", 3), ("gD", 1),
       ("mod", 10), ("mod", 11), ("sE", 3), ("gate",), ("gE", 1), ("gF", 1),
       ("gC", 2), ("gD", 2), ("gE", 2), ("gF", 2), ("gC", 3), ("gD", 3), ("gE", 3), ("gF", 3)]
)
CONSTS = 38

TURN = {s: n for n, s in enumerate(s for s in MIXER_ORDER if s[0] in ("proj", "mod"))}


def layer_kernel(nc, x, c, positions, ada_w, ada_b, norm_mix_g, w_in, gla_w_a2, gla_b_a2, gla_norm_g,
                 swa_sinks, w_out, norm_ffn_g, w_grp, b_grp, w_exp, b_exp, w_gate, w_up, w_down,
                 final_norm_g, out):
    h_rows = nc.dram_tensor("h_rows", [SEQ, D], F32, kind="Internal").ap()
    y_rows = nc.dram_tensor("y_rows", [2 * SEQ, D], F32, kind="Internal").ap()
    table = nc.dram_tensor("pair_table", [ROWS * NE, 1], I32, kind="Internal").ap()

    with ExitStack() as ctx:
        def sb(name, shape, dt=F32):
            return ctx.enter_context(nc.sbuf_tensor(name, shape, dt))

        def sem(name):
            return ctx.enter_context(nc.semaphore(name))

        CW = [hi - lo for lo, hi in CHUNKS]
        ring = sb("ring", [P, KD * WIN])
        at_c = {}
        off = 0
        for ch in (3, 4, 2, 0, 1):
            at_c[ch] = off
            off += KD * CW[ch]
        win_sb = [ring[:, at_c[ch]:at_c[ch] + KD * CW[ch]].rearrange("p (k n) -> p k n", k=KD)
                  for ch in range(NCH)]
        wide = sb("wide", [P, KD * D])
        ada_sb = [wide[:, i * KH * PC:(i + 1) * KH * PC].rearrange("p (k n) -> p k n", k=KH) for i in range(3)]
        o_ = 3 * KH * PC
        acc = wide[:, o_:o_ + 2 * PC].rearrange("p (a n) -> p a n", a=2)
        brow = wide[0:1, o_ + 2 * PC:o_ + 3 * PC]
        wout_sb = wide[:, :].rearrange("p (k n) -> p k n", k=KD)
        xres = sb("xres", [P, NB, D])
        hreg = sb("hreg", [P, KD * SEQ])
        hT = hreg[:, :].rearrange("p (k t) -> p k t", k=KD)
        proj = sb("proj", [P, NB, WIN])
        pflat = proj[:, :, :].rearrange("p b n -> p (b n)")
        scm = proj[:, :, 0:D]

        def shared(ch, start, size):
            return ring[:, at_c[ch] + start:at_c[ch] + start + size]

        probs = shared(0, 0, SH * 2 * P).rearrange("p (h s) -> p h s", h=SH)
        probsT = shared(0, SH * 2 * P, SH * 2 * P).rearrange("p (h c q) -> p h c q", h=SH, c=2)
        ropet = shared(0, 0, 4 * NB * 10 * HALF).rearrange("p (f b h d) -> p f b h d", f=4, b=NB, h=10)
        loga = shared(1, 0, NB * GH * DK).rearrange("p (b n) -> p b n", b=NB)
        lexp = shared(1, NB * GH * DK, NB * GH * DK).rearrange("p (b n) -> p b n", b=NB)
        gqT = shared(1, 1024, 512).rearrange("p (h t) -> p h t", h=GH)
        gqTm = shared(1, 1536, 512).rearrange("p (h t) -> p h t", h=GH)
        ebr = shared(2, 0, 512)
        enb = shared(2, 512, 256)
        krem = shared(2, 768, 256)
        qdup = shared(2, 1024, 512).rearrange("p (h c d) -> p h c d", h=GH, c=2)
        krm = shared(2, 1536, 512).rearrange("p (h c d) -> p h c d", h=GH, c=2)
        gkT = shared(2, 2048, 256).rearrange("p (h t) -> p h t", h=2)
        aT = shared(2, 2304, 512).rearrange("p (h t) -> p h t", h=GH)
        state = shared(2, 2816, 512).rearrange("p (h v) -> p h v", h=GH)
        kdec = shared(2, 3328, 256)
        osq = shared(2, 3584, 128)

        gt_a = sb("gt_a", [P, D])
        amp_f = sb("amp_f", [P, D])
        sh_f = sb("sh_f", [P, D])
        gt_f = sb("gt_f", [P, D])
        gla_g = sb("gla_g", [P, GH * DV])
        sqT = sb("sqT", [P, 4, P])
        skT = sb("skT", [P, SKV, NB, P])
        lowT = sb("lowT", [32, SEQ])
        wa2 = sb("wa2", [RANK + 1, GH * DK])
        fin_g = amp_f

        ident = sb("ident", [P, P])
        causal = sb("causal", [P, P])
        u16 = sb("u16", [P, P])
        r16 = sb("r16", [P, P])
        ind16 = sb("ind16", [P, 2])
        blockm = sb("blockm", [P, P])
        band = sb("band", [P, 2 * P])
        ones = sb("ones", [P, P])

        ccol = sb("ccol", [P, KD])
        csil = sb("csil", [P, KD])
        mcol = sb("mcol", [P, 4, KD])
        ssq = sb("ssq", [P, 16])
        rstd = sb("rstd", [P, 16])
        halfm = sb("halfm", [P, 4])
        posi = sb("posi", [P, NB], I32)
        freq = sb("freq", [P, HALF])
        ang = sb("ang", [P, 3, NB * HALF])
        trig = sb("trig", [P, 2, NB * HALF])
        sinks = sb("sinks", [P, SH])
        sm = sb("sm", [P, 6, SH])
        dec = sb("dec", [P, 8])

        ps = [ctx.enter_context(nc.psum_tensor(f"ps{i}", [P, 512], F32)) for i in range(8)]

        consts, low_ready, c_in, x_in0, x_in1, x_in2 = (
            sem(n) for n in ('consts', 'low_ready', 'c_in', 'x_in0', 'x_in1', 'x_in2'))
        x_in3, small_in, ada_in0, ada_in1, ada_in2, brow_in = (
            sem(n) for n in ('x_in3', 'small_in', 'ada_in0', 'ada_in1', 'ada_in2', 'brow_in'))
        wi0, wi1, wi2, wi3, wi4, wo_in = (
            sem(n) for n in ('wi0', 'wi1', 'wi2', 'wi3', 'wi4', 'wo_in'))
        fg_in, pos_in, silu_e, ssq_ready, mean_ready, pow_ready = (
            sem(n) for n in ('fg_in', 'pos_in', 'silu_e', 'ssq_ready', 'mean_ready', 'pow_ready'))
        xs_ready, ada_used, acc_ready, mod_col, col_vec, x_turned = (
            sem(n) for n in ('xs_ready', 'ada_used', 'acc_ready', 'mod_col', 'col_vec', 'x_turned'))
        h_dve, h_act, turn_ready, turn_free, rope_done, ang_ready = (
            sem(n) for n in ('h_dve', 'h_act', 'turn_ready', 'turn_free', 'rope_done', 'ang_ready'))
        trig_ready, low_t, low_z, z_ready, nz_ready, e_ready = (
            sem(n) for n in ('trig_ready', 'low_t', 'low_z', 'z_ready', 'nz_ready', 'e_ready'))
        l_ready, loga_ready, sq_t, sq_c, s_sc, s_masked = (
            sem(n) for n in ('l_ready', 'loga_ready', 'sq_t', 'sq_c', 's_sc', 's_masked'))
        s_max, s_exp, s_norm, s_pt, s_pc, s_pv = (
            sem(n) for n in ('s_max', 's_exp', 's_norm', 's_pt', 's_pc', 's_pv'))
        s_out, gb, gexp, gops, gq_t, gq_c = (
            sem(n) for n in ('s_out', 'gb', 'gexp', 'gops', 'gq_t', 'gq_c'))
        gk_c, g_a, g_kv, g_am, g_st, g_o = (
            sem(n) for n in ('gk_c', 'g_a', 'g_kv', 'g_am', 'g_st', 'g_o'))
        g_osq, g_mean, g_pow, g_out, gate_ready, gate_scaled = (
            sem(n) for n in ('g_osq', 'g_mean', 'g_pow', 'g_out', 'gate_ready', 'gate_scaled'))
        mt, mt_c, mo, x1_done, sq2, mean2 = (
            sem(n) for n in ('mt', 'mt_c', 'mo', 'x1_done', 'sq2', 'mean2'))
        pow2, h_dve2, h_ready, h_st0, h_st1, h_st2 = (
            sem(n) for n in ('pow2', 'h_dve2', 'h_ready', 'h_st0', 'h_st1', 'h_st2'))
        h_st3, h_turned, h_col, r_log, chain, r_dve = (
            sem(n) for n in ('h_st3', 'h_turned', 'h_col', 'r_log', 'chain', 'r_dve'))
        r_exp, r_cnt, r_pos, table_set, table_out, slot_ready = (
            sem(n) for n in ('r_exp', 'r_cnt', 'r_pos', 'table_set', 'table_out', 'slot_ready'))
        ids_out, tab_in, tok_ready, w_in0, w_in1, w_in2 = (
            sem(n) for n in ('ids_out', 'tab_in', 'tok_ready', 'w_in0', 'w_in1', 'w_in2'))
        w_in3, wd_in0, wd_in1, wd_in2, wd_in3, gath0 = (
            sem(n) for n in ('w_in3', 'wd_in0', 'wd_in1', 'wd_in2', 'wd_in3', 'gath0'))
        gath1, gath2, gath3, scat0, scat1, scat2 = (
            sem(n) for n in ('gath1', 'gath2', 'gath3', 'scat0', 'scat1', 'scat2'))
        scat3, idx_ready, e_turned, e_ta, e_td, e_gu = (
            sem(n) for n in ('scat3', 'idx_ready', 'e_turned', 'e_ta', 'e_td', 'e_gu'))
        e_silu, e_act, e_down, e_oa, e_od, hg_init = (
            sem(n) for n in ('e_silu', 'e_act', 'e_down', 'e_oa', 'e_od', 'hg_init'))
        ov_w, ov_idx, ov_tok, ov_hg, ov_t, ov_tc = (
            sem(n) for n in ('ov_w', 'ov_idx', 'ov_tok', 'ov_hg', 'ov_t', 'ov_tc'))
        ov_gu, ov_si, ov_ac, ov_dn, ov_oc, ov_sc = (
            sem(n) for n in ('ov_gu', 'ov_si', 'ov_ac', 'ov_dn', 'ov_oc', 'ov_sc'))
        ov_done, ov_free, dma_let, y_in0, y_in1, y_in2 = (
            sem(n) for n in ('ov_done', 'ov_free', 'dma_let', 'y_in0', 'y_in1', 'y_in2'))
        y_in3, y1s, yfin, ysq, ymean, ypow = (
            sem(n) for n in ('y_in3', 'y1s', 'yfin', 'ysq', 'ymean', 'ypow'))
        ynorm, out_done = (
            sem(n) for n in ('ynorm', 'out_done'))

        w_in_v = w_in.rearrange("l (k p) n -> p (l k) n", p=P)
        w_out_v = w_out.rearrange("l (k p) n -> p (l k) n", p=P)
        ada_v = ada_w.rearrange("l (p k) n -> p (l k) n", k=KD)
        x_v = x.rearrange("a (b p) d -> (a b) p d", p=P)
        out_v = out.rearrange("a (b p) d -> (a b) p d", p=P)
        gate_v = w_gate.rearrange("l g e (p k) f -> (l g e) p (k f)", k=KD)
        up_v = w_up.rearrange("l g e (p k) f -> (l g e) p (k f)", k=KD)
        down_v = w_down.rearrange("l g e (k p) d -> (l g e) p k d", p=P)
        SLOT = 2 * KD * F + FC * D
        slot = [ring[:, i * SLOT:(i + 1) * SLOT] for i in range(3)] + [wide[:, 0:SLOT]]
        wg_sb = [t[:, 0:KD * F].rearrange("p (k f) -> p k f", k=KD) for t in slot]
        wu_sb = [t[:, KD * F:2 * KD * F].rearrange("p (k f) -> p k f", k=KD) for t in slot]
        wd_sb = [t[:, 2 * KD * F:SLOT].rearrange("p (k d) -> p k d", k=FC) for t in slot]
        w_sem = [w_in0, w_in1, w_in2, w_in3]
        wd_sem = [wd_in0, wd_in1, wd_in2, wd_in3]
        h_stored = [h_st0, h_st1, h_st2, h_st3]
        gath = [gath0, gath1, gath2, gath3]
        scat = [scat0, scat1, scat2, scat3]

        hb = hreg[:, 0:2 * D].rearrange("p (a d) -> p a d", a=2)
        hcT = hreg[:, 2 * D:3 * D].rearrange("p (k t) -> p k t", k=KD)
        rt = hreg[:, 3 * D:4 * D]
        mixT = ring[:, at_c[0]:at_c[0] + D].rearrange("p (k t) -> p k t", k=KD)
        sq2t = ring[:, at_c[0] + D:at_c[0] + 2 * D]
        NR = NG + NE
        wr = sb("wr", [P, KD, NR])
        br = sb("br", [P, NR])
        lg = sb("lg", [P, NB, NR])
        topw = sb("topw", [P, 2, NB])
        ustrict = sb("ustrict", [P, P])
        eidx = sb("eidx", [P, NE])
        gkey = sb("gkey", [P, NG])
        ekey = sb("ekey", [P, NE])
        slot_i = sb("slot_i", [P, 2 * NB], I32)
        pair_i = sb("pair_i", [P, 2 * NB], I32)
        steps = sb("steps", [P, EXTRA])
        extra_i = sb("extra_i", [P, 1], I32)
        tabs = rt[0:CAP, 704:704 + 2 * NE].bitcast(I32).rearrange("p (a e) -> p a e", a=2)
        tabf = rt[0:CAP, 768:768 + NE]
        now = rt[0:CAP, 800:808].bitcast(I32).rearrange("p (u a) -> p u a", u=4)

        EOFF = [0]

        def take(n):
            EOFF[0] += n
            return pflat[:, EOFF[0] - n:EOFF[0]]
        hg = [take(D)[0:CAP, :] for i in range(4)]
        heT = [take(KD * CAP).rearrange("p (k t) -> p k t", k=KD) for i in range(2)]
        eo = [take(D)[0:CAP, :] for i in range(2)]
        sg = [take(FC * CAP) for i in range(2)]
        eact = [take(FC * CAP).rearrange("p (c t) -> p c t", c=FC) for i in range(2)]
        assert EOFF[0] <= NB * WIN
        padt = pflat[:, 0:ROWS * NE // P].bitcast(I32)

        block = ctx.enter_context(nc.Block())

        def bc(ap, shape):
            return ap.broadcast_to(shape)

        def score_place(h):
            return 3 + h % 2 + 2 * (h // 4), (h // 2 % 2) * 256

        def trig_b(i):
            return trig[:, i, :].rearrange("p (b d) -> p b d", b=NB).unsqueeze(2).broadcast_to([P, NB, 10, HALF])

        @block.sync
        def _(sp):
            sp.dma_start(ccol[:, :], c.rearrange("a (p k) -> (a p) k", k=KD)).then_inc(c_in, 16)
            for b in range(NB):
                sp.dma_start(xres[:, b, :], x_v[b]).then_inc([x_in0, x_in1, x_in2, x_in3][b], 16)
            ada_sem = [ada_in0, ada_in1, ada_in2]

            def piece(i):
                col = PARTS[i // 2] * D + (i % 2) * PC
                for kh in range(2):
                    q = 2 * i + kh
                    if q >= 3:
                        sp.wait_ge(ada_used, q - 2)
                    sp.dma_start(ada_sb[q % 3], ada_v[:, kh * KH:(kh + 1) * KH, col:col + PC])\
                        .then_inc(ada_sem[q % 3], 16)
                if i >= 1:
                    sp.wait_ge(acc_ready, i)
                sp.dma_start(brow, ada_b[0:1, col:col + PC]).then_inc(brow_in, 16)

            def win(ch):
                lo, hi = CHUNKS[ch]
                sp.dma_start(win_sb[ch], w_in_v[:, :, lo:hi]).then_inc([wi0, wi1, wi2, wi3, wi4][ch], 16)

            for i in range(4):
                piece(i)
            win(0)
            win(1)
            piece(4)
            piece(5)
            win(2)
            piece(6)
            piece(7)
            win(3)
            piece(8)
            piece(9)
            win(4)
            piece(10)
            piece(11)
            sp.wait_ge(turn_ready, len(TURN))
            sp.dma_start(wout_sb, w_out_v).then_inc(wo_in, 16)

            def expert(e, u):
                sp.dma_start(slot[u][:, 0:KD * F], gate_v[e]).then_inc(w_sem[u], 16)
                sp.dma_start(slot[u][:, KD * F:2 * KD * F], up_v[e]).then_inc(w_sem[u], 16)
                sp.dma_start(wd_sb[u], down_v[e]).then_inc(wd_sem[u], 16)

            sp.wait_ge(turn_ready, len(TURN))
            sp.wait_ge(mo, 1)
            expert(0, 0)
            expert(1, 1)
            for b in range(NB):
                sp.wait_ge(h_ready, b + 1)
                sp.dma_start(h_rows[b * P:(b + 1) * P, :], hb[:, b % 2, :]).then_inc(h_stored[b], 16)
            sp.wait_ge(mo, NB)
            sp.wait_ge(sq2, NB)
            expert(2, 2)
            expert(3, 3)
            sp.wait_ge(ids_out, 16 * 2 * NB)
            sp.dma_start(tabs[:, 1, :], table[0:CAP * NE, :].rearrange("(q e) o -> q (e o)", e=NE))\
                .then_inc(tab_in, 16)

            def refill(j):
                for u in range(SLOTS):
                    sp.wait_ge(e_down, SLOTS * (j - 1) + u + 1)
                    expert(SLOTS * j + u, u)
            with sp.Fori(1, NE // SLOTS) as j:
                refill(j)

            sp.wait_ge(r_dve, 3)
            extra = sp.value_load(extra_i[0:1, 0:1], min_val=0, max_val=EXTRA)
            with sp.If(extra > 0):
                sp.wait_ge(e_down, NE)
                with sp.Fori(0, extra) as m:
                    with sp.Fori(0, NE) as e:
                        sp.wait_ge(ov_free, m * NE + e + 1)
                        sp.dma_start(slot[0][:, 0:KD * F], gate_v[e]).then_inc(ov_w, 16)
                        sp.dma_start(slot[0][:, KD * F:2 * KD * F], up_v[e]).then_inc(ov_w, 16)
                        sp.dma_start(wd_sb[0], down_v[e]).then_inc(ov_w, 16)
                        with nc.allow_non_contiguous_dma("one id a place"):
                            sp.dma_start(now[:, 0, 1:2], table[bass.ds((m + 1) * CAP * NE, CAP * NE), :]
                                         .rearrange("(q e) o -> q (e o)", e=NE)[:, bass.ds(e, 1)]).then_inc(ov_idx, 16)
                sp.wait_ge(ov_free, extra * NE + 1)
                sp.sem_inc(ov_done, 1)
            for i in range(4):
                sp.wait_ge(scat[i], 16 * (NE // 4))
            yl = [y_in0, y_in1, y_in2, y_in3]
            for b in range(NB):
                if b >= 2:
                    sp.wait_ge(yfin, b - 1)
                sp.dma_start(ring[:, (2 * (b % 2)) * D:(2 * (b % 2) + 1) * D], y_rows[b * P:(b + 1) * P, :])\
                    .then_inc(yl[b], 16)
                sp.dma_start(ring[:, (2 * (b % 2) + 1) * D:(2 * (b % 2) + 2) * D],
                             y_rows[SEQ + b * P:SEQ + (b + 1) * P, :]).then_inc(yl[b], 16)
            for b in range(NB):
                sp.wait_ge(ynorm, b + 1)
                sp.dma_start(out_v[b], xres[:, b, :]).then_inc(out_done, 16)
            sp.wait_ge(out_done, 16 * NB)

        @block.gpsimd
        def _(pool):
            n_const = [0]

            def made(ins, wait=True):
                n_const[0] += 1
                ins.then_inc(consts, 1)
                if wait:
                    pool.wait_ge(consts, n_const[0])
            made(pool.memset(halfm[:, :], -0.5))
            made(pool.memset(ones[:, :], 1.0))
            made(pool.memset(ident[:, :], 0.0))
            made(pool.affine_select(out=ident[:, :], in_=ident[:, :], compare_op=ALU.not_equal, fill=1.0, base=0,
                                    pattern=[[-1, P]], channel_multiplier=1))
            for i in range(HALF):
                made(pool.memset(freq[:, i:i + 1], float(np.float32(THETA) ** np.float32(-2.0 * i / ROPE))), False)
            made(pool.memset(lowT[:, :], 1.0), False)
            for t, v in ((causal, 1.0), (u16, 1.0 / 16), (r16, 1.0 / 16), (blockm, 0.0), (ind16, 0.0),
                         (band, 0.0), (ustrict, 1.0)):
                made(pool.memset(t[:, :], v))
            for t in (causal, u16):
                made(pool.affine_select(out=t[:, :], in_=t[:, :], compare_op=ALU.is_ge, fill=0.0, base=0,
                                        pattern=[[1, P]], channel_multiplier=-1))
                made(pool.memset(t[0:CHUNK, CHUNK:P], 0.0))
            made(pool.affine_select(out=r16[:, :], in_=r16[:, :], compare_op=ALU.is_ge, fill=0.0, base=-1,
                                    pattern=[[-1, P]], channel_multiplier=1))
            made(pool.memset(r16[CHUNK:P, 0:CHUNK], 0.0))
            made(pool.affine_select(out=ustrict[:, :], in_=ustrict[:, :], compare_op=ALU.is_ge, fill=0.0, base=-1,
                                    pattern=[[1, P]], channel_multiplier=-1))
            made(pool.memset(blockm[0:CHUNK, 0:CHUNK], 1.0))
            made(pool.memset(blockm[CHUNK:P, CHUNK:P], 1.0))
            made(pool.memset(ind16[0:CHUNK, 0:1], 1.0 / 16))
            made(pool.memset(ind16[CHUNK:P, 1:2], 1.0 / 16))
            made(pool.affine_select(out=band[:, 0:P], in_=band[:, 0:P], compare_op=ALU.is_ge, fill=-BIG, base=-1,
                                    pattern=[[1, P]], channel_multiplier=-1))
            made(pool.affine_select(out=band[:, P:2 * P], in_=band[:, P:2 * P], compare_op=ALU.is_ge, fill=-BIG,
                                    base=0, pattern=[[-1, P]], channel_multiplier=1))
            imp = dict(allow_small_or_imprecise_dtypes=True)
            made(pool.iota(eidx[:, :], pattern=[[1, NE]], base=0, channel_multiplier=0, **imp))
            made(pool.iota(ekey[:, :], pattern=[[-1, NE]], base=NE, channel_multiplier=0, **imp))
            made(pool.iota(gkey[:, :], pattern=[[-1, NG]], base=NG, channel_multiplier=0, **imp))
            made(pool.iota(steps[:, :], pattern=[[CAP, EXTRA]], base=CAP, channel_multiplier=0, **imp))
            made(pool.iota(pair_i[:, :], pattern=[[P, 2 * NB]], base=0, channel_multiplier=1))
            assert n_const[0] == CONSTS, n_const[0]

            def power(o, i, ready, n, done):
                pool.wait_ge(ready, n)
                pool.tensor_tensor(rstd[:, o:o + i], ssq[:, o:o + i], halfm[:, 0:i], ALU.pow).then_inc(done, 1)
            power(0, 4, mean_ready, 1, pow_ready)
            for st in MIXER_ORDER:
                if st[0] == "gF":
                    power(4, 4, g_mean, st[1] + 1, g_pow)
            for b in range(NB):
                power(8 + b, 1, mean2, b + 1, pow2)

            pool.wait_ge(mt_c, 2 * NB)
            pool.memset(padt, PAD).then_inc(table_set, 1)
            pool.wait_ge(table_set, 1)
            pool.dma_start(table.rearrange("(p n) o -> p (n o)", p=P), padt).then_inc(table_out, 16)
            pool.wait_ge(table_out, 16)
            for i in range(4):
                pool.memset(hg[i], 0.0).then_inc(hg_init, 1)
            pool.wait_ge(slot_ready, 1)
            for i in range(2 * NB):
                pool.indirect_dma_start(out=table, out_offset=bass.IndirectOffsetOnAxis(ap=slot_i[:, i:i + 1], axis=0),
                                        in_=pair_i[:, i:i + 1], in_offset=None).then_inc(ids_out, 16)
            for b in range(NB):
                pool.wait_ge(h_stored[b], 16)
            pool.wait_ge(hg_init, 4)
            pool.wait_ge(tok_ready, 1)

            last_token = pool.to_reg(SEQ - 1)
            last_pair = pool.to_reg(2 * SEQ - 1)

            def hold():
                pool.sem_inc(dma_let, 1)

            def pick(e, u):
                pool.tensor_copy(now[:, u, :].unsqueeze(2), tabs[:, :, bass.ds(e, 1)]).then_inc(idx_ready, 1)

            def gather(e, u):
                pool.wait_ge(idx_ready, e + 1)
                hold()
                pool.indirect_dma_start(out=hg[u], out_offset=None, in_=h_rows,
                                        in_offset=bass.IndirectOffsetOnAxis(ap=now[:, u, 0:1], axis=0),
                                        bounds_check=last_token, oob_is_err=False).then_inc(gath[u], 16)

            def scatter(e, u, src, done):
                pool.indirect_dma_start(out=y_rows, out_offset=bass.IndirectOffsetOnAxis(ap=now[:, u, 1:2], axis=0),
                                        in_=src, in_offset=None, bounds_check=last_pair, oob_is_err=False)\
                    .then_inc(done, 16)

            for e in range(3):
                pick(e, e)
                gather(e, e)

            def step(e, u, j, first=False, last=False):
                if not (last and u >= 1):
                    ahead = e + 3 if isinstance(e, int) else pool.snap(e + 3)
                    if not (first and u == 0):
                        pool.wait_ge(e_turned, e)
                        pool.wait_ge(scat[(u + 3) % 4], 16 * (j if u == 0 else j + 1))
                    pick(ahead, (u + 3) % 4)
                    gather(e + 3, (u + 3) % 4)
                pool.wait_ge(e_oa, e + 1)
                pool.wait_ge(e_od, e + 1)
                hold()
                scatter(e, u, eo[u % 2], scat[u])

            for u in range(SLOTS):
                step(u, u, 0, first=True)
            with pool.Fori(1, NE // SLOTS - 1) as j:
                for u in range(SLOTS):
                    step(SLOTS * j + u, u, j)
            for u in range(SLOTS):
                step(NE - SLOTS + u, u, NE // SLOTS - 1, last=True)

            pool.wait_ge(r_dve, 3)
            extra = pool.value_load(extra_i[0:1, 0:1], min_val=0, max_val=EXTRA)
            with pool.If(extra > 0):
                for i in range(4):
                    pool.wait_ge(scat[i], 16 * (NE // 4))
                pool.sem_inc(ov_free, 1)
                with pool.Fori(0, extra) as m:
                    with pool.Fori(0, NE) as e:
                        n = m * NE + e
                        pool.wait_ge(ov_tok, n + 1)
                        hold()
                        pool.indirect_dma_start(out=hg[0], out_offset=None, in_=h_rows,
                                                in_offset=bass.IndirectOffsetOnAxis(ap=now[:, 0, 0:1], axis=0),
                                                bounds_check=last_token, oob_is_err=False).then_inc(ov_hg, 16)
                        pool.wait_ge(ov_oc, (n + 1) * 2)
                        hold()
                        scatter(e, 0, eo[0], ov_sc)
                        pool.wait_ge(ov_sc, (n + 1) * 16)
                        pool.sem_inc(ov_free, 1)
            for b in range(NB):
                power(12 + b, 1, ymean, b + 1, ypow)

        @block.scalar
        def _(act):
            def few(o, i):
                act.dma_start(o, i).then_inc(small_in, 16)
            with nc.allow_non_contiguous_dma("column and broadcast loads of small vectors"):
                act.dma_start(posi[:, :], positions.rearrange("a (b p) -> p (a b)", p=P)).then_inc(pos_in, 16)
                few(mcol[:, 2, :], norm_mix_g.rearrange("l (k p) -> p (l k)", p=P))
                few(sinks[:, :], swa_sinks[0:1, :].broadcast_to([P, SH]))
                few(gla_g[:, :], gla_norm_g.rearrange("l h v -> l (h v)").broadcast_to([P, GH * DV]))
                few(wa2[0:RANK, :], gla_w_a2[0])
                few(wa2[RANK:RANK + 1, :], gla_b_a2)
                few(amp_f[:, :], norm_ffn_g[0:1, :].broadcast_to([P, D]))
                few(wr[:, :, 0:NG], w_grp.rearrange("l (k p) n -> p (l k) n", p=P))
                few(wr[:, :, NG:], w_exp.rearrange("l (k p) n -> p (l k) n", p=P))
                few(br[:, 0:NG], b_grp[0:1, :].broadcast_to([P, NG]))
                few(br[:, NG:], b_exp[0:1, :].broadcast_to([P, NE]))
            act.wait_ge(ang_ready, 1)
            act.activation(trig[:, 0, :], ang[:, 0, :], ACT.Sin).then_inc(trig_ready, 1)
            act.activation(trig[:, 1, :], ang[:, 1, :], ACT.Sin).then_inc(trig_ready, 1)
            act.wait_ge(c_in, 16)
            act.activation(csil[:, :], ccol[:, :], ACT.Exp, scale=-1.0).then_inc(silu_e, 1)
            for b in range(NB):
                act.wait_ge([x_in0, x_in1, x_in2, x_in3][b], 16)
                act.activation(scm[:, b, :], xres[:, b, :], ACT.Square, accum_out=ssq[:, b:b + 1]).then_inc(ssq_ready, 1)
            act.wait_ge(pow_ready, 1)
            act.wait_ge(ssq_ready, NB)
            for b in range(NB):
                act.activation(scm[:, b, :], xres[:, b, :], ACT.Identity, scale=rstd[:, b:b + 1]).then_inc(xs_ready, 1)
            act.wait_ge(col_vec, 2)
            for k in range(1, KD, 2):
                act.wait_ge(x_turned, k + 1)
                act.activation(hT[:, k, :], ps[k % 6][:, :], ACT.Identity, scale=mcol[:, 3, k:k + 1],
                               bias=mcol[:, 1, k:k + 1]).then_inc(h_act, 1)

            mod_dst = {2: gt_a, 4: None, 3: sh_f, 5: gt_f}
            for st in MIXER_ORDER:
                kind = st[0]
                if kind in ("proj", "mod"):
                    r = TURN[st]
                    act.wait_ge(turn_ready, r + 1)
                    if kind == "proj":
                        lo, hi = CHUNKS[st[1]]
                        if r == 0:
                            act.wait_ge(x_turned, KD)
                        act.activation(proj[:, st[2], lo:hi], ps[r % 2][:, 0:hi - lo], ACT.Copy).then_inc(turn_free, 1)
                    else:
                        i = st[1]
                        part, cols = PARTS[i // 2], slice((i % 2) * PC, (i % 2 + 1) * PC)
                        dst = {2: gt_a, 4: sh_f, 3: sh_f, 5: gt_f}[part]
                        if part == 4:
                            act.activation(gt_f[:, cols], ps[r % 2][:, :], ACT.Copy).then_inc(turn_free, 1)
                        else:
                            if part == 5:
                                act.wait_ge(h_dve2, 2)
                            act.activation(dst[:, cols], ps[r % 2][:, :], ACT.Copy).then_inc(turn_free, 1)
                elif kind == "ga":
                    act.wait_ge(low_z, 1)
                    act.activation(loga[:, 0:2, :], ps[2][:, :].rearrange("p (b n) -> p b n", b=2), ACT.Copy).then_inc(z_ready, 1)
                    act.activation(loga[:, 2:4, :], ps[7][:, :].rearrange("p (b n) -> p b n", b=2), ACT.Copy).then_inc(z_ready, 1)
                    act.wait_ge(nz_ready, 1)
                    act.activation(lexp[:, :, :], lexp[:, :, :], ACT.Exp).then_inc(e_ready, 1)
                    act.wait_ge(e_ready, 1)
                    act.activation(lexp[:, :, :], lexp[:, :, :], ACT.Ln, bias=1.0).then_inc(l_ready, 1)
                elif kind == "sA":
                    n = st[1]
                    act.wait_ge(sq_t, n + 1)
                    act.activation(sqT[:, :, :], ps[3][:, :].rearrange("p (h t) -> p h t", h=4), ACT.Copy).then_inc(sq_c, 1)
                    for kv in range(SKV):
                        for half in range(2):
                            act.activation(skT[half * HD:(half + 1) * HD, kv, n, :], ps[4][kv * HD:(kv + 1) * HD, 0:P],
                                           ACT.Copy).then_inc(sq_c, 1)
                elif kind == "sB":
                    n = st[1]
                    act.wait_ge(s_max, n + 1)
                    lo = 0 if n else P
                    for h in range(SH):
                        act.activation(probs[:, h, lo:], probs[:, h, lo:], ACT.Exp, bias=sm[:, 1, h:h + 1],
                                       scale=HD ** -0.5, accum_out=sm[:, 2, h:h + 1]).then_inc(s_exp, 1)
                    act.activation(sm[:, 3, :], sm[:, 3, :], ACT.Exp).then_inc(s_exp, 1)
                elif kind == "sD":
                    n = st[1]
                    for i in range(1, 4, 2):
                        act.wait_ge(s_pt, 4 * n + i + 1)
                        if n == 0:
                            act.activation(probsT[:, 2 * i:2 * i + 2, 1, :],
                                           ps[3 + i][:, :].rearrange("p (h c q) -> p h c q", h=2, c=2)[:, :, 1, :],
                                           ACT.Copy).then_inc(s_pc, 1)
                        else:
                            act.activation(probsT[:, 2 * i:2 * i + 2, :, :],
                                           ps[3 + i][:, :].rearrange("p (h c q) -> p h c q", h=2, c=2),
                                           ACT.Copy).then_inc(s_pc, 1)
                elif kind == "gC":
                    n = st[1]
                    act.wait_ge(gb, n + 1)
                    if n >= 1:
                        act.wait_ge(gops, n)
                        act.wait_ge(g_st, 2 * n * GH)
                    else:
                        act.wait_ge(turn_ready, TURN[("proj", 2, 3)] + 1)
                    act.activation(ebr, ps[2][:, :], ACT.Exp).then_inc(gexp, 1)
                    act.activation(enb, ps[2][:, 0:256], ACT.Exp, scale=-1.0).then_inc(gexp, 1)
                    src = ps[7][:, 0:4].rearrange("p (i c) -> p i c", c=2)
                    for odd in range(2):
                        for ch in range(2):
                            act.activation(dec[ch * DK:(ch + 1) * DK, :].rearrange("p (i o c) -> p i o c", i=2, o=2)
                                           [:, :, odd, ch], src[odd * DK:(odd + 1) * DK, :, ch], ACT.Exp)\
                                .then_inc(gexp, 1)
                elif kind == "gD":
                    n = st[1]
                    act.wait_ge(gq_t, n + 1)
                    if n >= 1:
                        act.wait_ge(g_o, n)
                    act.activation(gqT[:, :, :], ps[2][:, :].rearrange("p (h t) -> p h t", h=GH), ACT.Copy,
                                   scale=DK ** -0.5).then_inc(gq_c, 1)
                elif kind == "gate":
                    act.wait_ge(turn_free, len(TURN))
                    act.activation(proj[:, :, CG:CA], proj[:, :, CG:CA], ACT.Silu).then_inc(gate_ready, 1)
                elif kind == "gF":
                    n = st[1]
                    act.wait_ge(g_o, n + 1)
                    for h in range(GH):
                        if n or h:
                            act.wait_ge(g_osq, GH * n + h)
                        act.activation(osq, ps[2][:, h * DV:(h + 1) * DV], ACT.Square,
                                       accum_out=ssq[:, 4 + h:5 + h]).then_inc(g_osq, 1)
            def h_column(b):
                for i in range(2):
                    act.wait_ge(h_turned, 2 * b + i + 1)
                    act.activation(hcT[:, 4 * i:4 * i + 4, :], ps[i][:, :].rearrange("p (k t) -> p k t", k=4),
                                   ACT.Copy).then_inc(h_col, 1)

            for b in range(NB):
                act.wait_ge(mt, 2 * b + 2)
                act.activation(mixT[:, 4:8, :], ps[4][:, :].rearrange("p (k t) -> p k t", k=4), ACT.Copy).then_inc(mt_c, 1)
                act.wait_ge(x1_done, 2 * b + 2)
                act.activation(sq2t, xres[:, b, :], ACT.Square, accum_out=ssq[:, 8 + b:9 + b]).then_inc(sq2, 1)
                if b >= 1:
                    h_column(b - 1)
            h_column(NB - 1)
            act.wait_ge(r_dve, 1)
            act.activation(rt[:, 0:16], rt[:, 0:16], ACT.Exp).then_inc(r_exp, 1)
            act.wait_ge(r_dve, 2)
            act.activation(rt[:, 32:36], rt[:, 32:36], ACT.Exp).then_inc(r_exp, 1)

            def turn(e, u):
                act.wait_ge(e_turned, e + 1)
                act.activation(heT[u % 2][:, 4:8, :], ps[1][:, 0:4 * CAP].rearrange("p (k t) -> p k t", k=4),
                               ACT.Copy).then_inc(e_ta, 1)

            def silu(e, u):
                act.wait_ge(e_gu, e + 1)
                act.activation(sg[u % 2], ps[2 + u % 2][:, 0:FC * CAP], ACT.Silu).then_inc(e_silu, 1)

            def give(e, u, j, first):
                act.wait_ge(e_down, e + 1)
                if not (first and u < 2):
                    act.wait_ge(scat[(u + 2) % 4], 16 * (j if u < 2 else j + 1))
                act.activation(eo[u % 2][:, 512:1024], ps[5 + 2 * (u % 2)][0:CAP, :], ACT.Copy).then_inc(e_oa, 1)

            def group(j, first=False, last=False):
                for u in range(SLOTS):
                    e = SLOTS * j + u
                    silu(e, u)
                    if not (last and u == SLOTS - 1):
                        turn(e + 1, u + 1)
                    if not (first and u == 0):
                        give(e - 1, (u + 3) % 4, j - 1 if u == 0 else j, first)
            turn(0, 0)
            group(0, first=True)
            with act.Fori(1, NE // SLOTS - 1) as j:
                group(j)
            group(NE // SLOTS - 1, last=True)
            give(NE - 1, 3, NE // SLOTS - 1, False)

            act.wait_ge(r_dve, 3)
            extra = act.value_load(extra_i[0:1, 0:1], min_val=0, max_val=EXTRA)
            with act.If(extra > 0):
                with act.Fori(0, extra) as m:
                    with act.Fori(0, NE) as e:
                        n = m * NE + e
                        act.wait_ge(ov_t, n + 1)
                        act.activation(heT[0][:, 4:8, :], ps[1][:, 0:4 * CAP].rearrange("p (k t) -> p k t", k=4),
                                       ACT.Copy).then_inc(ov_tc, 1)
                        act.wait_ge(ov_gu, n + 1)
                        act.activation(sg[0], ps[2][:, 0:FC * CAP], ACT.Silu).then_inc(ov_si, 1)
                        act.wait_ge(ov_dn, n + 1)
                        act.activation(eo[0][:, 512:1024], ps[5][0:CAP, :], ACT.Copy).then_inc(ov_oc, 1)
            act.wait_ge(h_dve2, 2 + NB)
            act.dma_start(fin_g[:, :], final_norm_g.unsqueeze(0).broadcast_to([P, D])).then_inc(fg_in, 16)
            yl = [y_in0, y_in1, y_in2, y_in3]
            for b in range(NB):
                act.wait_ge(yl[b], 32)
                y1 = ring[:, (2 * (b % 2)) * D:(2 * (b % 2) + 1) * D]
                act.activation(y1, y1, ACT.Identity, scale=topw[:, 0, b:b + 1]).then_inc(y1s, 1)
                act.wait_ge(yfin, b + 1)
                if b >= 1:
                    act.wait_ge(ysq, b)
                act.activation(ring[:, 4 * D:5 * D], xres[:, b, :], ACT.Square, accum_out=ssq[:, 12 + b:13 + b])\
                    .then_inc(ysq, 1)

        @block.vector
        def _(dve):
            links = [0]

            def link(ins):
                links[0] += 1
                ins.then_inc(chain, 1)
                dve.wait_ge(chain, links[0])

            dve.wait_ge(consts, CONSTS)
            dve.wait_ge(pos_in, 16)
            a3 = [ang[:, i, :].rearrange("p (b d) -> p b d", b=NB) for i in range(3)]
            link(dve.tensor_copy(trig[:, 0, 0:NB], posi[:, :]))
            link(dve.tensor_tensor(a3[0], trig[:, 0, 0:NB].unsqueeze(2).broadcast_to([P, NB, HALF]),
                                   freq[:, :].unsqueeze(1).broadcast_to([P, NB, HALF]), ALU.mult))
            magic = 1.5 * 2 ** 23
            link(dve.tensor_scalar(ang[:, 1, :], ang[:, 0, :], float(1 / (2 * np.pi)), magic, ALU.mult, ALU.add))
            link(dve.tensor_scalar(ang[:, 1, :], ang[:, 1, :], -magic, None, ALU.add))
            for part in (6.25, 0.03125, 0.001953125, float(2 * np.pi - 6.283203125)):
                link(dve.scalar_tensor_tensor(out=ang[:, 0, :], in0=ang[:, 1, :], scalar=-part, in1=ang[:, 0, :],
                                              op0=ALU.mult, op1=ALU.add))
            link(dve.tensor_scalar(ang[:, 0, :], ang[:, 0, :], 3.1415925, -3.1415925, ALU.min, ALU.max))
            link(dve.tensor_scalar(ang[:, 1, :], ang[:, 0, :], -1.0, None, ALU.mult))
            link(dve.tensor_tensor(ang[:, 1, :], ang[:, 1, :], ang[:, 0, :], ALU.min))
            dve.tensor_scalar(ang[:, 1, :], ang[:, 1, :], float(np.pi / 2), None, ALU.add).then_inc(ang_ready, 1)
            dve.wait_ge(silu_e, 1)
            link(dve.tensor_scalar(csil[:, :], csil[:, :], 1.0, None, ALU.add))
            link(dve.reciprocal(csil[:, :], csil[:, :]))
            link(dve.tensor_tensor(csil[:, :], csil[:, :], ccol[:, :], ALU.mult))
            dve.wait_ge(ssq_ready, NB)
            dve.tensor_scalar(ssq[:, 0:NB], ssq[:, 0:NB], 1.0 / D, EPS, ALU.mult, ALU.add).then_inc(mean_ready, 1)

            ada_sem = [ada_in0, ada_in1, ada_in2]

            def piece(i):
                a = acc[:, i % 2, :]
                if i >= 6:
                    dve.wait_ge(turn_ready, TURN[("mod", i - 2)] + 1)
                elif i >= 2:
                    dve.wait_ge(mod_col, i - 1)
                for k in range(KD):
                    q = 2 * i + k // KH
                    if k % KH == 0:
                        dve.wait_ge(ada_sem[q % 3], 16 * (q // 3 + 1))
                    w = ada_sb[q % 3][:, k % KH, :]
                    if k == 0:
                        link(dve.tensor_scalar(a, w, csil[:, k:k + 1], None, ALU.mult))
                    else:
                        link(dve.scalar_tensor_tensor(out=a, in0=w, scalar=csil[:, k:k + 1], in1=a,
                                                      op0=ALU.mult, op1=ALU.add))
                    if k % KH == KH - 1:
                        dve.sem_inc(ada_used, 1)
                dve.wait_ge(brow_in, 16 * (i + 1))
                dve.tensor_tensor(a[0:1, :], a[0:1, :], brow, ALU.add).then_inc(acc_ready, 1)

            for i in range(4):
                piece(i)
            dve.wait_ge(mod_col, 4)
            dve.wait_ge(small_in, 160)
            link(dve.tensor_copy(mcol[:, 0, :], ps[7][:, 0:KD]))
            dve.tensor_copy(mcol[:, 1, :], ps[7][:, KD:2 * KD]).then_inc(col_vec, 1)
            dve.scalar_tensor_tensor(out=mcol[:, 3, :], in0=mcol[:, 0, :], scalar=1.0, in1=mcol[:, 2, :],
                                     op0=ALU.add, op1=ALU.mult).then_inc(col_vec, 1)
            dve.wait_ge(col_vec, 2)
            for k in range(0, KD, 2):
                dve.wait_ge(x_turned, k + 1)
                dve.tensor_scalar(hT[:, k, :], ps[k % 6][:, :], mcol[:, 3, k:k + 1], mcol[:, 1, k:k + 1],
                                  ALU.mult, ALU.add).then_inc(h_dve, 1)
            piece(4)
            piece(5)

            next_piece = [6]
            for st in MIXER_ORDER:
                kind = st[0]
                if kind == "mod":
                    if next_piece[0] < NPC:
                        piece(next_piece[0])
                        next_piece[0] += 1
                    if st[1] in (6, 7):
                        cols = slice((st[1] % 2) * PC, (st[1] % 2 + 1) * PC)
                        dve.wait_ge(turn_free, TURN[st] + 1)
                        dve.scalar_tensor_tensor(out=amp_f[:, cols], in0=gt_f[:, cols], scalar=1.0,
                                                 in1=amp_f[:, cols], op0=ALU.add, op1=ALU.mult).then_inc(h_dve2, 1)
                elif kind == "rope":
                    dve.wait_ge(turn_free, TURN[("proj", 1, NB - 1)] + 1)
                    dve.wait_ge(trig_ready, 2)
                    qk = proj[:, :, CSQ:CSV].rearrange("p b (h d) -> p b h d", h=10)
                    x1, x2 = qk[:, :, :, 0:HALF], qk[:, :, :, HALF:ROPE]
                    t = [ropet[:, f] for f in range(4)]
                    dve.tensor_tensor(t[0], x1, trig_b(1), ALU.mult)
                    dve.tensor_tensor(t[1], x2, trig_b(0), ALU.mult)
                    dve.tensor_tensor(t[2], x2, trig_b(1), ALU.mult)
                    link(dve.tensor_tensor(t[3], x1, trig_b(0), ALU.mult))
                    link(dve.tensor_tensor(x1, t[0], t[1], ALU.subtract))
                    dve.tensor_tensor(x2, t[2], t[3], ALU.add).then_inc(rope_done, 1)
                elif kind == "ga":
                    dve.wait_ge(low_t, 1)
                    dve.tensor_copy(lowT[0:RANK, :], ps[7][0:RANK, :]).then_inc(low_ready, 1)
                    dve.wait_ge(z_ready, 2)
                    dve.scalar_tensor_tensor(out=lexp, in0=loga, scalar=-1.0, in1=loga, op0=ALU.mult, op1=ALU.min)\
                        .then_inc(nz_ready, 1)
                    dve.wait_ge(l_ready, 1)
                    dve.scalar_tensor_tensor(out=loga, in0=loga, scalar=0.0, in1=lexp, op0=ALU.min,
                                             op1=ALU.subtract).then_inc(loga_ready, 1)
                elif kind == "sB":
                    n = st[1]
                    lo = 0 if n else P
                    if n >= 1:
                        dve.wait_ge(s_pt, 4 * n)
                    else:
                        dve.wait_ge(rope_done, 1)
                    for h in range(SH):
                        bank, o = score_place(h)
                        dve.wait_ge(s_sc, 4 * n + bank - 2)
                        dve.tensor_tensor_reduce(out=probs[:, h, lo:], in0=ps[bank][:, o + lo:o + 256],
                                                 in1=band[:, lo:], scale=1.0, scalar=-BIG, op0=ALU.add, op1=ALU.max,
                                                 accum_out=sm[:, 0, h:h + 1]).then_inc(s_masked, 1)
                    dve.wait_ge(s_masked, SH * (n + 1))
                    link(dve.scalar_tensor_tensor(out=sm[:, 0, :], in0=sm[:, 0, :], scalar=HD ** -0.5, in1=sinks[:, :],
                                                  op0=ALU.mult, op1=ALU.max))
                    link(dve.tensor_scalar(sm[:, 1, :], sm[:, 0, :], -1.0, None, ALU.mult))
                    dve.tensor_tensor(sm[:, 3, :], sinks[:, :], sm[:, 0, :], ALU.subtract).then_inc(s_max, 1)
                elif kind == "sD":
                    n = st[1]
                    dve.wait_ge(s_exp, (SH + 1) * (n + 1))
                    link(dve.tensor_tensor(sm[:, 4, :], sm[:, 2, :], sm[:, 3, :], ALU.add))
                    dve.reciprocal(sm[:, 5, :], sm[:, 4, :]).then_inc(s_norm, 1)
                    for i in range(0, 4, 2):
                        dve.wait_ge(s_pt, 4 * n + i + 1)
                        src = ps[3 + i][:, :].rearrange("p (h c q) -> p h c q", h=2, c=2)
                        if n == 0:
                            dve.tensor_copy(probsT[:, 2 * i:2 * i + 2, 1, :], src[:, :, 1, :]).then_inc(s_pc, 1)
                        else:
                            dve.tensor_copy(probsT[:, 2 * i:2 * i + 2, :, :], src).then_inc(s_pc, 1)
                elif kind == "sE":
                    n = st[1]
                    dve.wait_ge(s_pv, n + 1)
                    dve.wait_ge(s_norm, n + 1)
                    dve.tensor_tensor(proj[:, n, CSQ:CSK].rearrange("p (h d) -> p h d", h=SH),
                                      ps[3][:, :].rearrange("p (h d) -> p h d", h=SH),
                                      sm[:, 5, :].unsqueeze(2).broadcast_to([P, SH, HD]), ALU.mult).then_inc(s_out, 1)
                elif kind == "gC":
                    if st[1] == 0:
                        dve.wait_ge(turn_ready, TURN[("proj", 2, 3)] + 1)
                        dve.memset(aT, 0.0)
                        link(dve.memset(state, 0.0))
                elif kind == "gD":
                    n = st[1]
                    dve.wait_ge(gexp, 6 * (n + 1))
                    if n >= 1:
                        dve.wait_ge(g_kv, n)
                        dve.wait_ge(gq_t, n)
                    q3 = proj[:, n, CQ:CK].rearrange("p (h d) -> p h d", h=GH).unsqueeze(2).broadcast_to([P, GH, 2, DK])
                    e3 = ebr[:, 0:256].rearrange("p (h d) -> p h d", h=GH).unsqueeze(2).broadcast_to([P, GH, 2, DK])
                    dve.tensor_tensor(qdup, q3, e3, ALU.mult)
                    dve.tensor_tensor(kdec, proj[:, n, CK:CV], enb, ALU.mult)
                    link(dve.tensor_tensor(krem, proj[:, n, CK:CV], ebr[:, 256:512], ALU.mult))
                    k3 = krem.rearrange("p (h d) -> p h d", h=GH).unsqueeze(2).broadcast_to([P, GH, 2, DK])
                    m3 = blockm[:, :].rearrange("p (c d) -> p c d", c=2).unsqueeze(1).broadcast_to([P, GH, 2, DK])
                    dve.tensor_tensor(krm, k3, m3, ALU.mult).then_inc(gops, 1)
                    dve.wait_ge(gq_t, n + 1)
                    if n >= 1:
                        dve.wait_ge(g_a, 2 * n)
                        dve.wait_ge(g_o, n)
                    dve.tensor_copy(gkT, ps[7][:, 256:512].rearrange("p (h t) -> p h t", h=2)).then_inc(gk_c, 1)
                    dve.wait_ge(gq_c, n + 1)
                    dve.tensor_tensor(gqTm, gqT, blockm[:, :].unsqueeze(1).broadcast_to([P, GH, P]), ALU.mult)\
                        .then_inc(gk_c, 1)
                elif kind == "gE":
                    n = st[1]
                    dve.wait_ge(g_a, 2 * (n + 1))
                    if n >= 1:
                        dve.wait_ge(g_o, n)
                    dve.copy_predicated(out=aT, mask=causal[:, :].bitcast(U32).unsqueeze(1).broadcast_to([P, GH, P]),
                                        data=ps[2][:, :].rearrange("p (h t) -> p h t", h=GH)).then_inc(g_am, 1)
                    dve.wait_ge(g_kv, n + 1)
                    kv = ps[7][:, :].rearrange("p (h v) -> p h v", h=GH)
                    for h in range(GH):
                        dve.scalar_tensor_tensor(out=state[CHUNK:P, h, :], in0=state[0:CHUNK, h, :],
                                                 scalar=dec[0:CHUNK, 2 * h:2 * h + 1], in1=kv[0:CHUNK, h, :],
                                                 op0=ALU.mult, op1=ALU.add).then_inc(g_st, 1)
                elif kind == "gF":
                    n = st[1]
                    dve.wait_ge(g_o, n + 1)
                    kv = ps[7][:, :].rearrange("p (h v) -> p h v", h=GH)
                    for h in range(GH):
                        dve.scalar_tensor_tensor(out=state[0:CHUNK, h, :], in0=state[CHUNK:P, h, :],
                                                 scalar=dec[CHUNK:P, 2 * h + 1:2 * h + 2], in1=kv[CHUNK:P, h, :],
                                                 op0=ALU.mult, op1=ALU.add).then_inc(g_st, 1)
                    dve.wait_ge(g_osq, GH * (n + 1))
                    dve.tensor_scalar(ssq[:, 4:8], ssq[:, 4:8], 1.0 / DV, EPS, ALU.mult, ALU.add).then_inc(g_mean, 1)
                    dve.wait_ge(g_pow, n + 1)
                    dve.tensor_tensor(proj[:, n, CV:CG].rearrange("p (h v) -> p h v", h=GH),
                                      ps[2][:, :].rearrange("p (h v) -> p h v", h=GH),
                                      rstd[:, 4:8].unsqueeze(2).broadcast_to([P, GH, DV]), ALU.mult).then_inc(g_out, 1)
            dve.wait_ge(gate_ready, 1)
            for b in range(NB):
                link(dve.tensor_tensor(proj[:, b, CG:CA], proj[:, b, CG:CA], gla_g[:, :], ALU.mult))
                dve.wait_ge(g_out, b + 1)
                dve.tensor_tensor(proj[:, b, CV:CG], proj[:, b, CV:CG], proj[:, b, CG:CA], ALU.mult)\
                    .then_inc(gate_scaled, 1)
            for b in range(NB):
                dve.wait_ge(mt, 2 * b + 1)
                if b >= 1:
                    dve.wait_ge(mo, b)
                dve.tensor_copy(mixT[:, 0:4, :], ps[3][:, :].rearrange("p (k t) -> p k t", k=4)).then_inc(mt_c, 1)
                dve.wait_ge(mo, b + 1)
                dve.wait_ge(turn_free, len(TURN))
                for i in range(2):
                    cols = slice(512 * i, 512 * (i + 1))
                    t = hreg[:, 3 * D + 512 * i:3 * D + 512 * (i + 1)]
                    link(dve.tensor_tensor(t, ps[5 + i][:, :], gt_a[:, cols], ALU.mult))
                    dve.tensor_tensor(xres[:, b, cols], xres[:, b, cols], t, ALU.add).then_inc(x1_done, 1)
                dve.wait_ge(sq2, b + 1)
                dve.tensor_scalar(ssq[:, 8 + b:9 + b], ssq[:, 8 + b:9 + b], 1.0 / D, EPS, ALU.mult, ALU.add)\
                    .then_inc(mean2, 1)
                dve.wait_ge(pow2, b + 1)
                if b >= 2:
                    dve.wait_ge(h_stored[b - 2], 16)
                    dve.wait_ge(h_turned, 2 * (b - 1))
                link(dve.scalar_tensor_tensor(out=hb[:, b % 2, :], in0=xres[:, b, :], scalar=rstd[:, 8 + b:9 + b],
                                              in1=amp_f[:, :], op0=ALU.mult, op1=ALU.mult))
                dve.tensor_tensor(hb[:, b % 2, :], hb[:, b % 2, :], sh_f[:, :], ALU.add).then_inc(h_ready, 1)
                dve.sem_inc(h_dve2, 1)

            r4 = lambda o, n: rt[:, o:o + NB * n].rearrange("p (b n) -> p b n", b=NB)
            col = lambda o: rt[:, o:o + NB]
            wide4 = lambda ap, n: ap.unsqueeze(2).broadcast_to([P, NB, n])
            key4 = lambda ap, n: ap.unsqueeze(1).broadcast_to([P, NB, n])
            L, eg = lg[:, :, 0:NG], r4(0, NG)
            gmax, gate, e12, t1, t2 = col(16), col(20), col(32), col(24), col(28)
            key, oh1, oh2, M = r4(64, NE), r4(192, NE), r4(320, NE), r4(448, NE)
            gk4, goh = r4(576, NG), r4(592, NG)
            kmax = col(608)
            dve.wait_ge(r_log, NB)
            for b in range(NB):
                link(dve.tensor_tensor(lg[:, b, :], ps[7][:, b * NR:(b + 1) * NR], br[:, :], ALU.add))
            link(dve.tensor_reduce(gmax, L, AX, ALU.max))
            dve.tensor_tensor(eg, L, wide4(gmax, NG), ALU.subtract).then_inc(r_dve, 1)

            def first_of(values, top, keys, n, key_t, one_hot):
                link(dve.tensor_tensor(key_t, values, wide4(top, n), ALU.is_equal))
                link(dve.tensor_tensor(key_t, key_t, key4(keys, n), ALU.mult))
                link(dve.tensor_reduce(kmax, key_t, AX, ALU.max))
                link(dve.tensor_tensor(one_hot, key_t, wide4(kmax, n), ALU.is_equal))

            first_of(L, gmax, gkey[:, :], NG, gk4, goh)
            link(dve.tensor_scalar(goh, goh, 1.0, BIG, ALU.subtract, ALU.mult))
            for b in range(NB):
                link(dve.tensor_tensor(M[:, b, :].rearrange("p (g e) -> p g e", g=NG),
                                       lg[:, b, NG:].rearrange("p (g e) -> p g e", g=NG),
                                       goh[:, b, :].unsqueeze(2).broadcast_to([P, NG, EPG]), ALU.add))
            link(dve.tensor_reduce(t1, M, AX, ALU.max))
            first_of(M, t1, ekey[:, :], NE, key, oh1)
            link(dve.scalar_tensor_tensor(out=M, in0=oh1, scalar=-3.0 * BIG, in1=M, op0=ALU.mult, op1=ALU.add))
            link(dve.tensor_reduce(t2, M, AX, ALU.max))
            first_of(M, t2, ekey[:, :], NE, key, oh2)
            link(dve.tensor_tensor(key, oh1, oh2, ALU.add))
            dve.sem_inc(r_cnt, 1)
            dve.tensor_tensor(e12, t2, t1, ALU.subtract).then_inc(r_dve, 1)
            dve.wait_ge(r_exp, 2)
            link(dve.tensor_reduce(gate, eg, AX, ALU.add))
            link(dve.tensor_scalar(col(36), e12, 1.0, None, ALU.add))
            link(dve.tensor_tensor(col(36), col(36), gate, ALU.mult))
            link(dve.reciprocal(topw[:, 0, :], col(36)))
            dve.tensor_tensor(topw[:, 1, :], topw[:, 0, :], e12, ALU.mult)
            dve.wait_ge(r_pos, 1)
            pos = ps[2][:, 0:NB * NE].rearrange("p (b n) -> p b n", b=NB)
            link(dve.tensor_scalar(M, pos, float(NE), None, ALU.mult))
            link(dve.tensor_tensor(M, M, key4(eidx[:, :], NE), ALU.add))
            for r, oh in enumerate((oh1, oh2)):
                link(dve.tensor_tensor(key, oh, M, ALU.mult))
                link(dve.tensor_reduce(col(40 + 4 * r), key, AX, ALU.add))
            link(dve.tensor_copy(slot_i[:, :], rt[:, 40:48]))
            dve.sem_inc(slot_ready, 1)
            link(dve.tensor_reduce(col(48)[:, 0:1], ps[2][:, 128:160], AX, ALU.max))
            link(dve.tensor_scalar(rt[:, 52:52 + EXTRA], steps[:, :], col(48)[:, 0:1], None, ALU.is_lt))
            link(dve.tensor_reduce(col(60)[:, 0:1], rt[:, 52:52 + EXTRA], AX, ALU.add))
            link(dve.tensor_copy(extra_i[:, :], col(60)[:, 0:1]))
            dve.sem_inc(r_dve, 1)

            def tokens(tok, pair, f):
                link(dve.tensor_scalar(f, pair, float(SEQ), float(SEQ), ALU.is_ge, ALU.mult))
                return dve.tensor_tensor(tok, pair, f, ALU.subtract)
            dve.wait_ge(tab_in, 16)
            tokens(tabs[:, 0, :], tabs[:, 1, :], tabf[:, :]).then_inc(tok_ready, 1)

            def turn(e, u):
                dve.wait_ge(e_turned, e + 1)
                dve.tensor_copy(heT[u % 2][:, 0:4, :], ps[0][:, 0:4 * CAP].rearrange("p (k t) -> p k t", k=4))\
                    .then_inc(e_td, 1)

            def product(e, u):
                dve.wait_ge(e_silu, e + 1)
                dve.tensor_tensor(eact[u % 2], sg[u % 2].rearrange("p (c t) -> p c t", c=FC),
                                  ps[2 + u % 2][:, FC * CAP:2 * FC * CAP].rearrange("p (c t) -> p c t", c=FC),
                                  ALU.mult).then_inc(e_act, 1)

            def give(e, u, j, first):
                dve.wait_ge(e_down, e + 1)
                if not (first and u < 2):
                    dve.wait_ge(scat[(u + 2) % 4], 16 * (j if u < 2 else j + 1))
                dve.tensor_copy(eo[u % 2][:, 0:512], ps[4 + 2 * (u % 2)][0:CAP, :]).then_inc(e_od, 1)

            def group(j, first=False, last=False):
                for u in range(SLOTS):
                    e = SLOTS * j + u
                    product(e, u)
                    if not (last and u == SLOTS - 1):
                        turn(e + 1, u + 1)
                    if not (first and u == 0):
                        give(e - 1, (u + 3) % 4, j - 1 if u == 0 else j, first)
            turn(0, 0)
            group(0, first=True)
            with dve.Fori(1, NE // SLOTS - 1) as j:
                group(j)
            group(NE // SLOTS - 1, last=True)
            give(NE - 1, 3, NE // SLOTS - 1, False)

            dve.wait_ge(r_dve, 3)
            extra = dve.value_load(extra_i[0:1, 0:1], min_val=0, max_val=EXTRA)
            with dve.If(extra > 0):
                with dve.Fori(0, extra) as m:
                    with dve.Fori(0, NE) as e:
                        n = m * NE + e
                        dve.wait_ge(ov_idx, (n + 1) * 16)
                        dve.tensor_scalar(tabf[:, 0:1], now[:, 0, 1:2], float(SEQ), float(SEQ), ALU.is_ge, ALU.mult)\
                            .then_inc(ov_ac, 1)
                        dve.wait_ge(ov_ac, n * 2 + 1)
                        dve.tensor_tensor(now[:, 0, 0:1], now[:, 0, 1:2], tabf[:, 0:1], ALU.subtract).then_inc(ov_tok, 1)
                        dve.wait_ge(ov_t, n + 1)
                        dve.tensor_copy(heT[0][:, 0:4, :], ps[0][:, 0:4 * CAP].rearrange("p (k t) -> p k t", k=4))\
                            .then_inc(ov_tc, 1)
                        dve.wait_ge(ov_si, n + 1)
                        dve.tensor_tensor(eact[0], sg[0].rearrange("p (c t) -> p c t", c=FC),
                                          ps[2][:, FC * CAP:2 * FC * CAP].rearrange("p (c t) -> p c t", c=FC),
                                          ALU.mult).then_inc(ov_ac, 1)
                        dve.wait_ge(ov_dn, n + 1)
                        dve.tensor_copy(eo[0][:, 0:512], ps[4][0:CAP, :]).then_inc(ov_oc, 1)

            for b in range(NB):
                y1 = ring[:, (2 * (b % 2)) * D:(2 * (b % 2) + 1) * D]
                y2 = ring[:, (2 * (b % 2) + 1) * D:(2 * (b % 2) + 2) * D]
                dve.wait_ge(y1s, b + 1)
                link(dve.scalar_tensor_tensor(out=y1, in0=y2, scalar=topw[:, 1, b:b + 1], in1=y1, op0=ALU.mult,
                                              op1=ALU.add))
                link(dve.tensor_tensor(y1, y1, gt_f[:, :], ALU.mult))
                dve.tensor_tensor(xres[:, b, :], xres[:, b, :], y1, ALU.add).then_inc(yfin, 1)
                dve.wait_ge(ysq, b + 1)
                link(dve.tensor_scalar(ssq[:, 12 + b:13 + b], ssq[:, 12 + b:13 + b], 1.0 / D, EPS, ALU.mult, ALU.add))
                dve.sem_inc(ymean, 1)
                dve.wait_ge(ypow, b + 1)
                if b == 0:
                    dve.wait_ge(fg_in, 16)
                dve.scalar_tensor_tensor(out=xres[:, b, :], in0=xres[:, b, :], scalar=rstd[:, 12 + b:13 + b],
                                         in1=fin_g[:, :], op0=ALU.mult, op1=ALU.mult).then_inc(ynorm, 1)

        @block.tensor
        def _(pe):
            pe.wait_ge(consts, CONSTS)
            for i in range(4):
                pe.wait_ge(acc_ready, i + 1)
                for j in range(4):
                    o = (i // 2) * KD + (i % 2) * 4 + j
                    mm = pe.matmul(ps[7][:, o:o + 1], acc[:, i % 2, j * P:(j + 1) * P], ones[:, 0:1], start=True, stop=True)
                mm.then_inc(mod_col, 1)
            pe.wait_ge(xs_ready, NB)
            for k in range(KD):
                if k >= 6:
                    pe.wait_ge(h_dve if k % 2 == 0 else h_act, 1)
                for b in range(NB):
                    mm = pe.transpose(ps[k % 6][:, b * P:(b + 1) * P], scm[:, b, k * P:(k + 1) * P], ident[:, :])
                mm.then_inc(x_turned, 1)
            pe.wait_ge(h_dve, KD // 2)
            pe.wait_ge(h_act, KD // 2)

            for st in MIXER_ORDER:
                kind = st[0]
                if kind == "proj":
                    ch, b = st[1:]
                    r = TURN[st]
                    if b == 0:
                        pe.wait_ge([wi0, wi1, wi2, wi3, wi4][ch], 16)
                    if r >= 2:
                        pe.wait_ge(turn_free, r - 1)
                    for k in range(KD):
                        mm = pe.matmul(ps[r % 2][:, 0:CW[ch]], hT[:, k, b * P:(b + 1) * P], win_sb[ch][:, k, :],
                                       start=k == 0, stop=k == KD - 1)
                    mm.then_inc(turn_ready, 1)
                elif kind == "mod":
                    r = TURN[st]
                    pe.wait_ge(acc_ready, st[1] + 1)
                    pe.wait_ge(turn_free, r - 1)
                    pe.matmul(ps[r % 2][:, :], ones[:, :], acc[:, st[1] % 2, :], start=True, stop=True)\
                        .then_inc(turn_ready, 1)
                elif kind == "ga":
                    pe.wait_ge(turn_free, TURN[("proj", 0, NB - 1)] + 1)
                    for b in range(NB):
                        mm = pe.transpose(ps[7][0:RANK, b * P:(b + 1) * P], proj[:, b, CA:CA + RANK], ident[:, :])
                    mm.then_inc(low_t, 1)
                    pe.wait_ge(low_ready, 1)
                    for b in range(NB):
                        mm = pe.matmul(ps[2 if b < 2 else 7][:, (b % 2) * 256:(b % 2) * 256 + 256],
                                       lowT[0:RANK + 1, b * P:(b + 1) * P], wa2[:, :], start=True, stop=True)
                    mm.then_inc(low_z, 1)
                elif kind == "sA":
                    n = st[1]
                    pe.wait_ge(rope_done, 1)
                    if n >= 1:
                        pe.wait_ge(s_pc, 4 * n)
                        if n >= 2:
                            pe.wait_ge(s_out, n - 1)
                    for i in range(4):
                        pe.transpose(ps[3][:, i * P:(i + 1) * P], proj[:, n, CSQ + i * P:CSQ + (i + 1) * P],
                                     ident[:, :])
                    pe.transpose(ps[4][:, 0:P], proj[:, n, CSK:CSV], ident[:, :]).then_inc(sq_t, 1)
                elif kind == "sB":
                    n = st[1]
                    pe.wait_ge(sq_c, 5 * (n + 1))
                    if n >= 1:
                        pe.wait_ge(s_pc, 4 * n)
                        pe.wait_ge(s_out, n)
                    for h in range(SH):
                        kv, i = h // 4, h // 2
                        rows = slice((h % 2) * HD, (h % 2 + 1) * HD)
                        bank, o = score_place(h)
                        if n >= 1:
                            mm = pe.matmul(ps[bank][:, o:o + 256], sqT[rows, i, :],
                                           skT[rows, kv, n - 1:n + 1, :].rearrange("p b s -> p (b s)"), start=True, stop=True)
                        else:
                            mm = pe.matmul(ps[bank][:, o + P:o + 256], sqT[rows, i, :], skT[rows, kv, n, :],
                                           start=True, stop=True)
                        if h % 4 >= 2:
                            mm.then_inc(s_sc, 1)
                elif kind == "sD":
                    n = st[1]
                    pe.wait_ge(s_exp, (SH + 1) * (n + 1))
                    if n >= 1:
                        pe.wait_ge(s_out, n)
                    for h in range(SH):
                        for cc in range(0 if n else 1, 2):
                            mm = pe.transpose(ps[3 + h // 2][:, (h % 2) * 256 + cc * P:(h % 2) * 256 + (cc + 1) * P],
                                              probs[:, h, cc * P:(cc + 1) * P], ident[:, :])
                        if h % 2:
                            mm.then_inc(s_pt, 1)
                elif kind == "sE":
                    n = st[1]
                    pe.wait_ge(s_pc, 4 * (n + 1))
                    if n + 1 < NB:
                        pe.wait_ge(sq_c, 5 * (n + 2))
                    for h in range(SH):
                        kv = h // 4
                        for cc in range(0 if n else 1, 2):
                            mm = pe.matmul(ps[3][:, h * HD:(h + 1) * HD], probsT[:, h, cc, :],
                                           proj[:, n - 1 + cc, CSV + kv * HD:CSV + (kv + 1) * HD],
                                           start=cc == (0 if n else 1), stop=cc == 1)
                    mm.then_inc(s_pv, 1)
                elif kind == "gC":
                    n = st[1]
                    if n == 0:
                        pe.wait_ge(loga_ready, 1)
                    else:
                        pe.wait_ge(g_out, n)
                        pe.wait_ge(g_st, 2 * GH * n)
                    pe.matmul(ps[2][:, 0:256], u16[:, :], loga[:, n, :], start=True, stop=True)
                    pe.matmul(ps[2][:, 256:512], r16[:, :], loga[:, n, :], start=True, stop=True)
                    for i in range(2):
                        mm = pe.matmul(ps[7][:, 2 * i:2 * i + 2], loga[:, n, i * P:(i + 1) * P], ind16[:, :],
                                       start=True, stop=True)
                    mm.then_inc(gb, 1)
                elif kind == "gD":
                    n = st[1]
                    pe.wait_ge(gops, n + 1)
                    pe.wait_ge(gexp, 6 * (n + 1))
                    for h in range(GH):
                        pe.transpose(ps[2][:, h * P:(h + 1) * P], qdup[:, h].rearrange("p c d -> p (c d)"), ident[:, :])
                    for i in range(2):
                        mm = pe.transpose(ps[7][:, 256 + i * P:256 + (i + 1) * P], kdec[:, i * P:(i + 1) * P], ident[:, :])
                    mm.then_inc(gq_t, 1)
                elif kind == "gE":
                    n = st[1]
                    pe.wait_ge(gk_c, 2 * (n + 1))
                    pe.wait_ge(gq_c, n + 1)
                    for odd in range(2):
                        for h in range(odd, GH, 2):
                            rows = slice(odd * DK, (odd + 1) * DK)
                            mm = pe.matmul(ps[2][:, h * P:(h + 1) * P], gkT[rows, h // 2, :], gqT[rows, h, :],
                                           start=True, stop=True)
                        mm.then_inc(g_a, 1)
                        if odd == 0:
                            pe.wait_ge(g_a, 2 * n + 1)
                    pe.wait_ge(turn_free, TURN[("proj", 3, n)] + 1)
                    for h in range(GH):
                        mm = pe.matmul(ps[7][:, h * DV:(h + 1) * DV], krm[:, h].rearrange("p c d -> p (c d)"),
                                       proj[:, n, CV + h * DV:CV + (h + 1) * DV], start=True, stop=True)
                    mm.then_inc(g_kv, 1)
                elif kind == "gF":
                    n = st[1]
                    pe.wait_ge(g_am, n + 1)
                    pe.wait_ge(g_st, 2 * GH * n + GH)
                    for h in range(GH):
                        o = ps[2][:, h * DV:(h + 1) * DV]
                        pe.matmul(o, aT[:, h, :], proj[:, n, CV + h * DV:CV + (h + 1) * DV], start=True, stop=False)
                        mm = pe.matmul(o, gqTm[:, h, :], state[:, h, :], start=False, stop=True)
                    mm.then_inc(g_o, 1)

            pe.wait_ge(wo_in, 16)

            def logits(b):
                pe.wait_ge(h_ready, b + 1)
                for i in range(2):
                    for k in range(4 * i, 4 * i + 4):
                        mm = pe.transpose(ps[i][:, (k % 4) * P:(k % 4 + 1) * P], hb[:, b % 2, k * P:(k + 1) * P], ident[:, :])
                    mm.then_inc(h_turned, 1)
                pe.wait_ge(h_col, 2 * b + 2)
                for k in range(KD):
                    mm = pe.matmul(ps[7][:, b * NR:(b + 1) * NR], hcT[:, k, :], wr[:, k, :], start=k == 0, stop=k == KD - 1)
                mm.then_inc(r_log, 1)

            for b in range(NB):
                if b == 0:
                    pe.wait_ge(s_out, NB)
                    pe.wait_ge(turn_free, len(TURN))
                else:
                    pe.wait_ge(mt_c, 2 * b)
                pe.wait_ge(gate_scaled, b + 1)
                for i in range(2):
                    for k in range(4 * i, 4 * i + 4):
                        lo = (CV if i == 0 else CSQ) + (k % 4) * P
                        mm = pe.transpose(ps[3 + i][:, (k % 4) * P:(k % 4 + 1) * P], proj[:, b, lo:lo + P], ident[:, :])
                    mm.then_inc(mt, 1)
                if b >= 1:
                    pe.wait_ge(x1_done, 2 * b)
                pe.wait_ge(mt_c, 2 * b + 2)
                for i in range(2):
                    for k in range(KD):
                        mm = pe.matmul(ps[5 + i][:, :], mixT[:, k, :], wout_sb[:, k, 512 * i:512 * (i + 1)],
                                       start=k == 0, stop=k == KD - 1)
                mm.then_inc(mo, 1)
                if b >= 1:
                    logits(b - 1)
            logits(NB - 1)

            pe.wait_ge(r_cnt, 1)
            cnt = rt[:, 64:64 + NB * NE].rearrange("p (b n) -> p b n", b=NB)
            for b in range(NB):
                for a in range(b):
                    pe.matmul(ps[2][:, b * NE:(b + 1) * NE], ones[:, :], cnt[:, a, :], start=a == 0, stop=False)
                pe.matmul(ps[2][:, b * NE:(b + 1) * NE], ustrict[:, :], cnt[:, b, :], start=b == 0, stop=True)
            for a in range(NB):
                mm = pe.matmul(ps[2][:, 128:160], ones[:, :], cnt[:, a, :], start=a == 0, stop=a == NB - 1)
            mm.then_inc(r_pos, 1)

            def turn_tile(src, done):
                for i in range(2):
                    for k in range(4 * i, 4 * i + 4):
                        rows = src.rearrange("t (p k) -> t k p", k=KD)[:, k, :]
                        mm = pe.transpose(ps[i][:, (k % 4) * CAP:(k % 4 + 1) * CAP], rows, ident[0:CAP, 0:CAP])
                mm.then_inc(done, 1)

            def gate_up(bank, w, u, hx, done):
                for m, wt in enumerate((wg_sb[w], wu_sb[w])):
                    for f in range(FC):
                        o = (m * FC + f) * CAP
                        for k in range(KD):
                            mm = pe.matmul(ps[bank][:, o:o + CAP], wt[:, k, f * P:(f + 1) * P], hx[:, k, :],
                                           start=k == 0, stop=k == KD - 1)
                mm.then_inc(done, 1)

            def down_tile(bank, w, a, done):
                for i in range(2):
                    for f in range(FC):
                        mm = pe.matmul(ps[bank + i][0:CAP, :], a[:, f, :], wd_sb[w][:, f, 512 * i:512 * (i + 1)],
                                       start=f == 0, stop=f == FC - 1)
                mm.then_inc(done, 1)

            def turn(e, u, j):
                pe.wait_ge(gath[u], 16 * (j + 1))
                turn_tile(hg[u], e_turned)

            def down(e, u, j, first):
                pe.wait_ge(e_act, e + 1)
                pe.wait_ge(wd_sem[u], 16 * (j + 1))
                if not (first and u < 2):
                    pe.wait_ge(e_oa, e - 1)
                    pe.wait_ge(e_od, e - 1)
                down_tile(4 + 2 * (u % 2), u, eact[u % 2], e_down)

            def group(j, first=False, last=False):
                for u in range(SLOTS):
                    e = SLOTS * j + u
                    pe.wait_ge(e_ta, e + 1)
                    pe.wait_ge(e_td, e + 1)
                    pe.wait_ge(w_sem[u], 32 * (j + 1))
                    if not (first and u < 2):
                        pe.wait_ge(e_act, e - 1)
                    gate_up(2 + u % 2, u, u, heT[u % 2], e_gu)
                    if not (last and u == SLOTS - 1):
                        turn(e + 1, (u + 1) % 4, j + 1 if u == SLOTS - 1 else j)
                    if not (first and u == 0):
                        down(e - 1, (u + 3) % 4, j - 1 if u == 0 else j, first)
            pe.wait_ge(slot_ready, 1)
            pe.wait_ge(r_dve, 3)
            turn(0, 0, 0)
            group(0, first=True)
            with pe.Fori(1, NE // SLOTS - 1) as j:
                group(j)
            group(NE // SLOTS - 1, last=True)
            down(NE - 1, 3, NE // SLOTS - 1, False)

            extra = pe.value_load(extra_i[0:1, 0:1], min_val=0, max_val=EXTRA)
            with pe.If(extra > 0):
                pe.wait_ge(e_oa, NE)
                pe.wait_ge(e_od, NE)
                with pe.Fori(0, extra) as m:
                    with pe.Fori(0, NE) as e:
                        n = m * NE + e
                        pe.wait_ge(ov_hg, (n + 1) * 16)
                        turn_tile(hg[0], ov_t)
                        pe.wait_ge(ov_tc, (n + 1) * 2)
                        pe.wait_ge(ov_w, (n + 1) * 48)
                        gate_up(2, 0, 0, heT[0], ov_gu)
                        pe.wait_ge(ov_ac, (n + 1) * 2)
                        down_tile(4, 0, eact[0], ov_dn)


_INS = ["x", "c", "positions", "ada_w", "ada_b", "norm_mix_g", "w_in", "gla_w_a2", "gla_b_a2", "gla_norm_g",
        "swa_sinks", "w_out", "norm_ffn_g", "w_grp", "b_grp", "w_exp", "b_exp", "w_gate", "w_up", "w_down",
        "final_norm_g"]


def kernel(**inputs):
    import concourse.bacc as bacc
    from concourse.bass_utils import run_bass_kernel_spmd

    nc = bacc.Bacc("TRN2", target_bir_lowering=False, num_devices=1)
    arrays, args = {}, []
    for name in _INS:
        a = np.ascontiguousarray(inputs[name])
        arrays[f"in_{name}"] = a
        args.append(nc.dram_tensor(f"in_{name}", a.shape, mybir.dt.from_np(a.dtype), kind="ExternalInput").ap())
    out = nc.dram_tensor("out_x", [1, SEQ, D], F32, kind="ExternalOutput").ap()
    layer_kernel(nc, *args, out)
    r = run_bass_kernel_spmd(nc, [arrays], core_ids=[0])
    return r.results[0]["out_x"]
```

```python
from contextlib import ExitStack

import numpy as np
import concourse.bass as bass
from concourse import mybir

P = 128
SEQ, D = 512, 1024
NB = SEQ // P
KD = D // P
GH, DK, DV, RANK = 4, 64, 128, 16
CHUNK = 64
SH, SKV, HD = 8, 2, 64
ROPE = HD // 4
HALF = ROPE // 2
THETA = 500000.0
NG, EPG = 4, 8
NE = NG * EPG
F = 256
FC = F // P
EPS = 1e-6
CQ, CK, CV, CG = 0, GH * DK, 2 * GH * DK, 2 * GH * DK + GH * DV
CA = CG + GH * DV
CSQ = CA + RANK
CSK = CSQ + SH * HD
CSV = CSK + SKV * HD
WIN = CSV + SKV * HD
CHUNKS = [(CA, CA + 512), (CA + 512, WIN), (CQ, CV), (CV, CG), (CG, CA)]
NCH = len(CHUNKS)
PARTS = [1, 0, 2, 4, 3, 5]
PC = 512
NPC = 2 * len(PARTS)
KH = KD // 2
CAP = 96
EXTRA = -(-SEQ // CAP) - 1
ROWS = (EXTRA + 1) * CAP
PAD = 8192
BIG = 1.0e30
SLOTS = 4

F32, I32, U32 = mybir.dt.float32, mybir.dt.int32, mybir.dt.uint32
ALU = mybir.AluOpType
ACT = mybir.ActivationFunctionType
AX = mybir.AxisListType.X

def _cycle(n, first, second):
    nxt = [("sA", n + 1)] if n + 1 < NB else []
    more = [("sB", n + 1)] if n + 1 < NB else [("gs", 0), ("oT", 0)]
    return ([first, ("gC", n), ("sD", n), second, ("gD", n)] + nxt + [("sE", n), ("gE", n)] + more +
            [("gF", n)] + ([("sX", n + 1)] if n + 1 < NB else []))


MIXER_ORDER = (
    [("piece", 4), ("piece", 5), ("proj", 0, 0), ("piece", 6), ("proj", 0, 1), ("mod", 4), ("piece", 7),
     ("proj", 0, 2), ("mod", 5), ("piece", 8), ("proj", 0, 3), ("mod", 6), ("piece", 9), ("proj", 1, 0), ("gaT",),
     ("proj", 1, 1), ("mod", 7), ("proj", 1, 2), ("proj", 1, 3), ("rope",), ("mod", 8), ("gaZ",),
     ("proj", 2, 0), ("mod", 9), ("amp",), ("gaL",), ("piece", 10), ("proj", 2, 1), ("gaF",), ("piece", 11),
     ("sA", 0), ("proj", 2, 2), ("mod", 10), ("sB", 0), ("sX", 0), ("proj", 2, 3), ("mod", 11)] +
    _cycle(0, ("proj", 3, 0), ("proj", 3, 1)) + _cycle(1, ("proj", 3, 2), ("proj", 3, 3)) +
    _cycle(2, ("proj", 4, 0), ("proj", 4, 1)) + [("gate", 0), ("gate", 1)] +
    _cycle(3, ("proj", 4, 2), ("proj", 4, 3)) +
    [("gate", 2), ("gate", 3), ("gs", 1), ("oM", 0, 0), ("oT", 1), ("oM", 0, 1), ("gs", 2), ("oN", 0), ("oM", 1, 0),
     ("oT", 2), ("oM", 1, 1), ("gs", 3), ("oN", 1), ("oL", 0), ("oM", 2, 0), ("oT", 3), ("oM", 2, 1), ("oN", 2),
     ("oL", 1), ("oM", 3, 0), ("oL", 2), ("oM", 3, 1), ("oN", 3), ("oL", 3)]
)
CONSTS = 38

TURN = {s: n for n, s in enumerate(s for s in MIXER_ORDER if s[0] in ("proj", "mod"))}


def layer_kernel(nc, x, c, positions, ada_w, ada_b, norm_mix_g, w_in, gla_w_a2, gla_b_a2, gla_norm_g,
                 swa_sinks, w_out, norm_ffn_g, w_grp, b_grp, w_exp, b_exp, w_gate, w_up, w_down,
                 final_norm_g, out):
    h_rows = nc.dram_tensor("h_rows", [SEQ, D], F32, kind="Internal").ap()
    y_rows = nc.dram_tensor("y_rows", [2 * SEQ, D], F32, kind="Internal").ap()
    table = nc.dram_tensor("pair_table", [ROWS * NE, 1], I32, kind="Internal").ap()

    with ExitStack() as ctx:
        def sb(name, shape, dt=F32):
            return ctx.enter_context(nc.sbuf_tensor(name, shape, dt))

        def sem(name):
            return ctx.enter_context(nc.semaphore(name))

        CW = [hi - lo for lo, hi in CHUNKS]
        ring = sb("ring", [P, KD * WIN])
        at_c = {}
        off = 0
        for ch in (3, 4, 2, 0, 1):
            at_c[ch] = off
            off += KD * CW[ch]
        win_sb = [ring[:, at_c[ch]:at_c[ch] + KD * CW[ch]].rearrange("p (k n) -> p k n", k=KD)
                  for ch in range(NCH)]
        wide = sb("wide", [P, KD * D])
        ada_sb = [wide[:, i * KH * PC:(i + 1) * KH * PC].rearrange("p (k n) -> p k n", k=KH) for i in range(3)]
        o_ = 3 * KH * PC
        acc = wide[:, o_:o_ + 2 * PC].rearrange("p (a n) -> p a n", a=2)
        acc2 = wide[:, o_ + 2 * PC:o_ + 3 * PC]
        brow = wide[0:1, o_ + 3 * PC:o_ + 4 * PC]
        wout_sb = wide[:, :].rearrange("p (k n) -> p k n", k=KD)
        xres = sb("xres", [P, NB, D])
        hreg = sb("hreg", [P, KD * SEQ])
        hT = hreg[:, :].rearrange("p (k t) -> p k t", k=KD)
        proj = sb("proj", [P, NB, WIN])
        pflat = proj[:, :, :].rearrange("p b n -> p (b n)")
        scm = proj[:, :, 0:D]

        def shared(ch, start, size):
            return ring[:, at_c[ch] + start:at_c[ch] + start + size]

        probs = shared(0, 0, SH * 2 * P).rearrange("p (h s) -> p h s", h=SH)
        probsT = shared(0, SH * 2 * P, SH * 2 * P).rearrange("p (h c q) -> p h c q", h=SH, c=2)
        ropet = shared(0, 0, 4 * NB * 10 * HALF).rearrange("p (f b h d) -> p f b h d", f=4, b=NB, h=10)
        loga = shared(1, 0, NB * GH * DK).rearrange("p (b n) -> p b n", b=NB)
        lexp = shared(1, NB * GH * DK, NB * GH * DK).rearrange("p (b n) -> p b n", b=NB)
        gqT = shared(1, 1024, 512).rearrange("p (h t) -> p h t", h=GH)
        gqTm = shared(1, 1536, 512).rearrange("p (h t) -> p h t", h=GH)
        ebr = shared(2, 0, 512)
        enb = shared(2, 512, 256)
        krem = shared(2, 768, 256)
        qdup = shared(2, 1024, 512).rearrange("p (h c d) -> p h c d", h=GH, c=2)
        krm = shared(2, 1536, 512).rearrange("p (h c d) -> p h c d", h=GH, c=2)
        gkT = shared(2, 2048, 256).rearrange("p (h t) -> p h t", h=2)
        aT = shared(2, 2304, 512).rearrange("p (h t) -> p h t", h=GH)
        state = shared(2, 2816, 512).rearrange("p (h v) -> p h v", h=GH)
        kdec = shared(2, 3328, 256)
        osq = shared(2, 3584, 512)

        gt_a = sb("gt_a", [P, D])
        amp_f = sb("amp_f", [P, D])
        sh_f = sb("sh_f", [P, D])
        gt_f = sb("gt_f", [P, D])
        gla_g = sb("gla_g", [P, GH * DV])
        sqT = sb("sqT", [P, 4, P])
        skT = sb("skT", [P, SKV, NB, P])
        lowT = sb("lowT", [32, SEQ])
        wa2 = sb("wa2", [RANK + 1, GH * DK])
        fin_g = amp_f

        ident = sb("ident", [P, P])
        causal = sb("causal", [P, P])
        u16 = sb("u16", [P, P])
        r16 = sb("r16", [P, P])
        ind16 = sb("ind16", [P, 2])
        blockm = sb("blockm", [P, P])
        band = sb("band", [P, 2 * P])
        ones = sb("ones", [P, P])

        ccol = sb("ccol", [P, KD])
        csil = sb("csil", [P, KD])
        mcol = sb("mcol", [P, 4, KD])
        ssq = sb("ssq", [P, 16])
        rstd = sb("rstd", [P, 16])
        halfm = sb("halfm", [P, 4])
        posi = sb("posi", [P, NB], I32)
        freq = sb("freq", [P, HALF])
        ang = sb("ang", [P, 3, NB * HALF])
        trig = sb("trig", [P, 2, NB * HALF])
        sinks = sb("sinks", [P, SH])
        sm = sb("sm", [P, 6, SH])
        dec = sb("dec", [P, 8])

        ps = [ctx.enter_context(nc.psum_tensor(f"ps{i}", [P, 512], F32)) for i in range(8)]

        consts, low_ready, c_in, x_in0, x_in1, x_in2 = (
            sem(n) for n in ('consts', 'low_ready', 'c_in', 'x_in0', 'x_in1', 'x_in2'))
        x_in3, small_in, ada_in0, ada_in1, ada_in2, brow_in = (
            sem(n) for n in ('x_in3', 'small_in', 'ada_in0', 'ada_in1', 'ada_in2', 'brow_in'))
        wi0, wi1, wi2, wi3, wi4, wo_in = (
            sem(n) for n in ('wi0', 'wi1', 'wi2', 'wi3', 'wi4', 'wo_in'))
        fg_in, pos_in, silu_e, ssq_ready, mean_ready, pow_ready = (
            sem(n) for n in ('fg_in', 'pos_in', 'silu_e', 'ssq_ready', 'mean_ready', 'pow_ready'))
        xs_ready, ada_rows, bias_added, acc_ready, mod_col, col_vec, x_turned = (
            sem(n) for n in ('xs_ready', 'ada_rows', 'bias_added', 'acc_ready', 'mod_col', 'col_vec', 'x_turned'))
        h_dve, h_act, turn_ready, turn_free, rope_done, ang_ready = (
            sem(n) for n in ('h_dve', 'h_act', 'turn_ready', 'turn_free', 'rope_done', 'ang_ready'))
        trig_ready, low_t, low_z, z_ready, nz_ready, e_ready = (
            sem(n) for n in ('trig_ready', 'low_t', 'low_z', 'z_ready', 'nz_ready', 'e_ready'))
        l_ready, loga_ready, sq_t, sq_c, s_sc, s_masked = (
            sem(n) for n in ('l_ready', 'loga_ready', 'sq_t', 'sq_c', 's_sc', 's_masked'))
        s_max, s_exp, s_norm, s_pt, s_pc, s_pv = (
            sem(n) for n in ('s_max', 's_exp', 's_norm', 's_pt', 's_pc', 's_pv'))
        s_out, gb, gexp, gops, gq_t, gq_c = (
            sem(n) for n in ('s_out', 'gb', 'gexp', 'gops', 'gq_t', 'gq_c'))
        gk_c, g_a, g_kv, g_am, g_st, g_o = (
            sem(n) for n in ('gk_c', 'g_a', 'g_kv', 'g_am', 'g_st', 'g_o'))
        g_osq, g_mean, g_pow, g_out, gate_ready, gate_scaled = (
            sem(n) for n in ('g_osq', 'g_mean', 'g_pow', 'g_out', 'gate_ready', 'gate_scaled'))
        mt, mt_c, mo, x1_done, sq2, mean2 = (
            sem(n) for n in ('mt', 'mt_c', 'mo', 'x1_done', 'sq2', 'mean2'))
        pow2, amp_ready, h_ready, h_st0, h_st1, h_st2 = (
            sem(n) for n in ('pow2', 'amp_ready', 'h_ready', 'h_st0', 'h_st1', 'h_st2'))
        h_st3, h_turned, h_col, r_log, lg_read, chain, r_dve = (
            sem(n) for n in ('h_st3', 'h_turned', 'h_col', 'r_log', 'lg_read', 'chain', 'r_dve'))
        r_exp, r_cnt, r_pos, table_set, table_out, slot_ready = (
            sem(n) for n in ('r_exp', 'r_cnt', 'r_pos', 'table_set', 'table_out', 'slot_ready'))
        ids_out, tab_in, tok_ready, w_in0, w_in1, w_in2 = (
            sem(n) for n in ('ids_out', 'tab_in', 'tok_ready', 'w_in0', 'w_in1', 'w_in2'))
        w_in3, wd_in0, wd_in1, wd_in2, wd_in3, gath0 = (
            sem(n) for n in ('w_in3', 'wd_in0', 'wd_in1', 'wd_in2', 'wd_in3', 'gath0'))
        gath1, gath2, gath3, scat0, scat1, scat2 = (
            sem(n) for n in ('gath1', 'gath2', 'gath3', 'scat0', 'scat1', 'scat2'))
        scat3, idx_ready, pair_ready, e_turned, e_ta, e_td, e_gu = (
            sem(n) for n in ('scat3', 'idx_ready', 'pair_ready', 'e_turned', 'e_ta', 'e_td', 'e_gu'))
        e_silu, e_act, e_down, e_od, hg_init = (
            sem(n) for n in ('e_silu', 'e_act', 'e_down', 'e_od', 'hg_init'))
        ov_w, ov_idx, ov_tok, ov_hg, ov_t, ov_tc = (
            sem(n) for n in ('ov_w', 'ov_idx', 'ov_tok', 'ov_hg', 'ov_t', 'ov_tc'))
        ov_gu, ov_si, ov_ac, ov_dn, ov_oc, ov_sc = (
            sem(n) for n in ('ov_gu', 'ov_si', 'ov_ac', 'ov_dn', 'ov_oc', 'ov_sc'))
        ov_done, ov_free, dma_let, y_in0, y_in1, y_in2 = (
            sem(n) for n in ('ov_done', 'ov_free', 'dma_let', 'y_in0', 'y_in1', 'y_in2'))
        y_in3, y1s, yfin, ysq, ymean, ypow = (
            sem(n) for n in ('y_in3', 'y1s', 'yfin', 'ysq', 'ymean', 'ypow'))
        ynorm, out_done = (
            sem(n) for n in ('ynorm', 'out_done'))

        w_in_v = w_in.rearrange("l (k p) n -> p (l k) n", p=P)
        w_out_v = w_out.rearrange("l (k p) n -> p (l k) n", p=P)
        ada_v = ada_w.rearrange("l (p k) n -> p (l k) n", k=KD)
        x_v = x.rearrange("a (b p) d -> (a b) p d", p=P)
        out_v = out.rearrange("a (b p) d -> (a b) p d", p=P)
        gate_v = w_gate.rearrange("l g e (p k) f -> (l g e) p (k f)", k=KD)
        up_v = w_up.rearrange("l g e (p k) f -> (l g e) p (k f)", k=KD)
        down_v = w_down.rearrange("l g e (k p) d -> (l g e) p k d", p=P)
        SLOT = 2 * KD * F + FC * D
        slot = [ring[:, i * SLOT:(i + 1) * SLOT] for i in range(3)] + [wide[:, 0:SLOT]]
        wg_sb = [t[:, 0:KD * F].rearrange("p (k f) -> p k f", k=KD) for t in slot]
        wu_sb = [t[:, KD * F:2 * KD * F].rearrange("p (k f) -> p k f", k=KD) for t in slot]
        wd_sb = [t[:, 2 * KD * F:SLOT].rearrange("p (k d) -> p k d", k=FC) for t in slot]
        w_sem = [w_in0, w_in1, w_in2, w_in3]
        wd_sem = [wd_in0, wd_in1, wd_in2, wd_in3]
        h_stored = [h_st0, h_st1, h_st2, h_st3]
        gath = [gath0, gath1, gath2, gath3]
        scat = [scat0, scat1, scat2, scat3]

        hb = hreg[:, 0:2 * D].rearrange("p (a d) -> p a d", a=2)
        hcT = hreg[:, 2 * D:3 * D].rearrange("p (k t) -> p k t", k=KD)
        rt = hreg[:, 3 * D:4 * D]
        mixT = [ring[:, at_c[0] + i * D:at_c[0] + (i + 1) * D].rearrange("p (k t) -> p k t", k=KD) for i in range(2)]
        sq2t = ring[:, at_c[0] + 2 * D:at_c[0] + 3 * D]
        NR = NG + NE
        wr = sb("wr", [P, KD, NR])
        br = sb("br", [P, NR])
        lg = sb("lg", [P, NB, NR])
        topw = sb("topw", [P, 2, NB])
        ustrict = sb("ustrict", [P, P])
        eidx = sb("eidx", [P, NE])
        gkey = sb("gkey", [P, NG])
        ekey = sb("ekey", [P, NE])
        slot_i = sb("slot_i", [P, 2 * NB], I32)
        pair_i = sb("pair_i", [P, 2 * NB], I32)
        steps = sb("steps", [P, EXTRA])
        extra_i = sb("extra_i", [P, 1], I32)
        tabs = rt[0:CAP, 704:704 + 2 * NE].bitcast(I32).rearrange("p (a e) -> p a e", a=2)
        tabf = rt[0:CAP, 768:768 + NE]
        now = rt[0:CAP, 800:808].bitcast(I32).rearrange("p (u a) -> p u a", u=4)

        EOFF = [0]

        def take(n):
            EOFF[0] += n
            return pflat[:, EOFF[0] - n:EOFF[0]]
        hg = [take(D)[0:CAP, :] for i in range(4)]
        heT = [take(KD * CAP).rearrange("p (k t) -> p k t", k=KD) for i in range(2)]
        eo = [take(D)[0:CAP, :] for i in range(2)]
        sg = [take(FC * CAP) for i in range(2)]
        eact = [take(FC * CAP).rearrange("p (c t) -> p c t", c=FC) for i in range(2)]
        assert EOFF[0] <= NB * WIN
        padt = pflat[:, 0:ROWS * NE // P].bitcast(I32)

        block = ctx.enter_context(nc.Block())

        def bc(ap, shape):
            return ap.broadcast_to(shape)

        def score_place(h):
            return 3 + h % 2 + 2 * (h // 4), (h // 2 % 2) * 256

        def trig_b(i):
            return trig[:, i, :].rearrange("p (b d) -> p b d", b=NB).unsqueeze(2).broadcast_to([P, NB, 10, HALF])

        @block.sync
        def _(sp):
            sp.dma_start(ccol[:, :], c.rearrange("a (p k) -> (a p) k", k=KD)).then_inc(c_in, 16)
            for b in range(NB):
                sp.dma_start(xres[:, b, :], x_v[b]).then_inc([x_in0, x_in1, x_in2, x_in3][b], 16)
            ada_sem = [ada_in0, ada_in1, ada_in2]

            def piece(i):
                col = PARTS[i // 2] * D + (i % 2) * PC
                for kh in range(2):
                    q = 2 * i + kh
                    if q >= 3:
                        sp.wait_ge(ada_rows, KH * (q - 2))
                    sp.dma_start(ada_sb[q % 3], ada_v[:, kh * KH:(kh + 1) * KH, col:col + PC])\
                        .then_inc(ada_sem[q % 3], 16)
                if i >= 1:
                    sp.wait_ge(bias_added, i)
                sp.dma_start(brow, ada_b[0:1, col:col + PC]).then_inc(brow_in, 16)

            def win(ch):
                lo, hi = CHUNKS[ch]
                sp.dma_start(win_sb[ch], w_in_v[:, :, lo:hi]).then_inc([wi0, wi1, wi2, wi3, wi4][ch], 16)

            for i in range(4):
                piece(i)
            win(0)
            win(1)
            for i in range(4, 8):
                piece(i)
            win(2)
            piece(8)
            piece(9)
            win(3)
            piece(10)
            win(4)
            piece(11)
            sp.wait_ge(turn_ready, TURN[("mod", NPC - 1)] + 1)
            sp.dma_start(wout_sb, w_out_v).then_inc(wo_in, 16)

            def gates(e, u):
                sp.dma_start(slot[u][:, 0:KD * F], gate_v[e]).then_inc(w_sem[u], 16)
                sp.dma_start(slot[u][:, KD * F:2 * KD * F], up_v[e]).then_inc(w_sem[u], 16)

            def expert(e, u):
                gates(e, u)
                sp.dma_start(wd_sb[u], down_v[e]).then_inc(wd_sem[u], 16)

            def store_h(b):
                sp.wait_ge(h_ready, b + 1)
                sp.dma_start(h_rows[b * P:(b + 1) * P, :], hb[:, b % 2, :]).then_inc(h_stored[b], 16)

            sp.wait_ge(turn_ready, len(TURN))
            expert(0, 0)
            store_h(0)
            sp.wait_ge(gate_scaled, NB)
            expert(1, 1)
            for b in range(1, NB):
                store_h(b)
            sp.wait_ge(mo, 2 * NB)
            sp.wait_ge(sq2, NB)
            expert(2, 2)
            expert(3, 3)
            sp.wait_ge(ids_out, 16 * 2 * NB)
            sp.dma_start(tabs[:, 1, :], table[0:CAP * NE, :].rearrange("(q e) o -> q (e o)", e=NE))\
                .then_inc(tab_in, 16)

            def refill(j):
                for u in range(SLOTS):
                    e = SLOTS * j + u
                    sp.wait_ge(e_gu, SLOTS * (j - 1) + u + 1)
                    gates(e, u)
                    sp.wait_ge(e_down, SLOTS * (j - 1) + u + 1)
                    sp.dma_start(wd_sb[u], down_v[e]).then_inc(wd_sem[u], 16)
            with sp.Fori(1, NE // SLOTS) as j:
                refill(j)

            sp.wait_ge(r_dve, 3)
            extra = sp.value_load(extra_i[0:1, 0:1], min_val=0, max_val=EXTRA)
            with sp.If(extra > 0):
                sp.wait_ge(e_down, NE)
                with sp.Fori(0, extra) as m:
                    with sp.Fori(0, NE) as e:
                        sp.wait_ge(ov_free, m * NE + e + 1)
                        sp.dma_start(slot[0][:, 0:KD * F], gate_v[e]).then_inc(ov_w, 16)
                        sp.dma_start(slot[0][:, KD * F:2 * KD * F], up_v[e]).then_inc(ov_w, 16)
                        sp.dma_start(wd_sb[0], down_v[e]).then_inc(ov_w, 16)
                        with nc.allow_non_contiguous_dma("one id a place"):
                            sp.dma_start(now[:, 0, 1:2], table[bass.ds((m + 1) * CAP * NE, CAP * NE), :]
                                         .rearrange("(q e) o -> q (e o)", e=NE)[:, bass.ds(e, 1)]).then_inc(ov_idx, 16)
                sp.wait_ge(ov_free, extra * NE + 1)
                sp.sem_inc(ov_done, 1)
            for i in range(4):
                sp.wait_ge(scat[i], 16 * (NE // 4))
            yl = [y_in0, y_in1, y_in2, y_in3]
            for b in range(NB):
                if b >= 2:
                    sp.wait_ge(yfin, 2 * (b - 1))
                sp.dma_start(ring[:, (2 * (b % 2)) * D:(2 * (b % 2) + 1) * D], y_rows[b * P:(b + 1) * P, :])\
                    .then_inc(yl[b], 16)
                sp.dma_start(ring[:, (2 * (b % 2) + 1) * D:(2 * (b % 2) + 2) * D],
                             y_rows[SEQ + b * P:SEQ + (b + 1) * P, :]).then_inc(yl[b], 16)
            for b in range(NB):
                sp.wait_ge(ynorm, b + 1)
                sp.dma_start(out_v[b], xres[:, b, :]).then_inc(out_done, 16)
            sp.wait_ge(out_done, 16 * NB)

        @block.gpsimd
        def _(pool):
            n_const = [0]

            def made(ins, wait=True):
                n_const[0] += 1
                ins.then_inc(consts, 1)
                if wait:
                    pool.wait_ge(consts, n_const[0])
            made(pool.memset(halfm[:, :], -0.5))
            made(pool.memset(ones[:, :], 1.0))
            made(pool.memset(ident[:, :], 0.0))
            made(pool.affine_select(out=ident[:, :], in_=ident[:, :], compare_op=ALU.not_equal, fill=1.0, base=0,
                                    pattern=[[-1, P]], channel_multiplier=1))
            for i in range(HALF):
                made(pool.memset(freq[:, i:i + 1], float(np.float32(THETA) ** np.float32(-2.0 * i / ROPE))), False)
            made(pool.memset(lowT[:, :], 1.0), False)
            for t, v in ((causal, 1.0), (u16, 1.0 / 16), (r16, 1.0 / 16), (blockm, 0.0), (ind16, 0.0),
                         (band, 0.0), (ustrict, 1.0)):
                made(pool.memset(t[:, :], v))
            for t in (causal, u16):
                made(pool.affine_select(out=t[:, :], in_=t[:, :], compare_op=ALU.is_ge, fill=0.0, base=0,
                                        pattern=[[1, P]], channel_multiplier=-1))
                made(pool.memset(t[0:CHUNK, CHUNK:P], 0.0))
            made(pool.affine_select(out=r16[:, :], in_=r16[:, :], compare_op=ALU.is_ge, fill=0.0, base=-1,
                                    pattern=[[-1, P]], channel_multiplier=1))
            made(pool.memset(r16[CHUNK:P, 0:CHUNK], 0.0))
            made(pool.affine_select(out=ustrict[:, :], in_=ustrict[:, :], compare_op=ALU.is_ge, fill=0.0, base=-1,
                                    pattern=[[1, P]], channel_multiplier=-1))
            made(pool.memset(blockm[0:CHUNK, 0:CHUNK], 1.0))
            made(pool.memset(blockm[CHUNK:P, CHUNK:P], 1.0))
            made(pool.memset(ind16[0:CHUNK, 0:1], 1.0 / 16))
            made(pool.memset(ind16[CHUNK:P, 1:2], 1.0 / 16))
            made(pool.affine_select(out=band[:, 0:P], in_=band[:, 0:P], compare_op=ALU.is_ge, fill=-BIG, base=-1,
                                    pattern=[[1, P]], channel_multiplier=-1))
            made(pool.affine_select(out=band[:, P:2 * P], in_=band[:, P:2 * P], compare_op=ALU.is_ge, fill=-BIG,
                                    base=0, pattern=[[-1, P]], channel_multiplier=1))
            imp = dict(allow_small_or_imprecise_dtypes=True)
            made(pool.iota(eidx[:, :], pattern=[[1, NE]], base=0, channel_multiplier=0, **imp))
            made(pool.iota(ekey[:, :], pattern=[[-1, NE]], base=NE, channel_multiplier=0, **imp))
            made(pool.iota(gkey[:, :], pattern=[[-1, NG]], base=NG, channel_multiplier=0, **imp))
            made(pool.iota(steps[:, :], pattern=[[CAP, EXTRA]], base=CAP, channel_multiplier=0, **imp))
            made(pool.iota(pair_i[:, :], pattern=[[P, 2 * NB]], base=0, channel_multiplier=1))
            assert n_const[0] == CONSTS, n_const[0]

            def power(o, i, ready, n, done):
                pool.wait_ge(ready, n)
                pool.tensor_tensor(rstd[:, o:o + i], ssq[:, o:o + i], halfm[:, 0:i], ALU.pow).then_inc(done, 1)
            power(0, 4, mean_ready, 1, pow_ready)
            for st in MIXER_ORDER:
                if st[0] == "gF":
                    power(4, 4, g_mean, st[1] + 1, g_pow)
                elif st[0] == "oN":
                    power(8 + st[1], 1, mean2, st[1] + 1, pow2)

            pool.wait_ge(mt_c, 2 * NB)
            pool.memset(padt, PAD).then_inc(table_set, 1)
            pool.wait_ge(table_set, 1)
            pool.dma_start(table.rearrange("(p n) o -> p (n o)", p=P), padt).then_inc(table_out, 16)
            pool.wait_ge(table_out, 16)
            for i in range(4):
                pool.memset(hg[i], 0.0).then_inc(hg_init, 1)
            pool.wait_ge(slot_ready, 1)
            for i in range(2 * NB):
                pool.indirect_dma_start(out=table, out_offset=bass.IndirectOffsetOnAxis(ap=slot_i[:, i:i + 1], axis=0),
                                        in_=pair_i[:, i:i + 1], in_offset=None).then_inc(ids_out, 16)
            for b in range(NB):
                pool.wait_ge(h_stored[b], 16)
            pool.wait_ge(hg_init, 4)
            pool.wait_ge(tok_ready, 1)

            last_token = pool.to_reg(SEQ - 1)
            last_pair = pool.to_reg(2 * SEQ - 1)

            def hold():
                pool.sem_inc(dma_let, 1)

            def pick(e, u):
                pool.tensor_copy(now[:, u, 0:1], tabs[:, 0, bass.ds(e, 1)]).then_inc(idx_ready, 1)

            def gather(e, u):
                pool.wait_ge(idx_ready, e + 1)
                hold()
                pool.indirect_dma_start(out=hg[u], out_offset=None, in_=h_rows,
                                        in_offset=bass.IndirectOffsetOnAxis(ap=now[:, u, 0:1], axis=0),
                                        bounds_check=last_token, oob_is_err=False).then_inc(gath[u], 16)

            def scatter(e, u, src, done):
                pool.indirect_dma_start(out=y_rows, out_offset=bass.IndirectOffsetOnAxis(ap=now[:, u, 1:2], axis=0),
                                        in_=src, in_offset=None, bounds_check=last_pair, oob_is_err=False)\
                    .then_inc(done, 16)

            for e in range(3):
                pick(e, e)
                gather(e, e)

            def step(e, u, j, first=False, last=False):
                here = e if isinstance(e, int) else pool.snap(e + 0)
                if not (last and u >= 1):
                    ahead = e + 3 if isinstance(e, int) else pool.snap(e + 3)
                    if not (first and u == 0):
                        pool.wait_ge(e_turned, e)
                    pick(ahead, (u + 3) % 4)
                    gather(e + 3, (u + 3) % 4)
                if not first:
                    pool.wait_ge(scat[u], 16 * j)
                pool.tensor_copy(now[:, u, 1:2], tabs[:, 1, bass.ds(here, 1)]).then_inc(pair_ready, 1)
                pool.wait_ge(pair_ready, e + 1)
                pool.wait_ge(e_od, 2 * (e + 1))
                hold()
                scatter(e, u, eo[u % 2], scat[u])

            for u in range(SLOTS):
                step(u, u, 0, first=True)
            with pool.Fori(1, NE // SLOTS - 1) as j:
                for u in range(SLOTS):
                    step(SLOTS * j + u, u, j)
            for u in range(SLOTS):
                step(NE - SLOTS + u, u, NE // SLOTS - 1, last=True)

            pool.wait_ge(r_dve, 3)
            extra = pool.value_load(extra_i[0:1, 0:1], min_val=0, max_val=EXTRA)
            with pool.If(extra > 0):
                for i in range(4):
                    pool.wait_ge(scat[i], 16 * (NE // 4))
                pool.sem_inc(ov_free, 1)
                with pool.Fori(0, extra) as m:
                    with pool.Fori(0, NE) as e:
                        n = m * NE + e
                        pool.wait_ge(ov_tok, n + 1)
                        hold()
                        pool.indirect_dma_start(out=hg[0], out_offset=None, in_=h_rows,
                                                in_offset=bass.IndirectOffsetOnAxis(ap=now[:, 0, 0:1], axis=0),
                                                bounds_check=last_token, oob_is_err=False).then_inc(ov_hg, 16)
                        pool.wait_ge(ov_oc, (n + 1) * 2)
                        hold()
                        scatter(e, 0, eo[0], ov_sc)
                        pool.wait_ge(ov_sc, (n + 1) * 16)
                        pool.sem_inc(ov_free, 1)
            for b in range(NB):
                power(12 + b, 1, ymean, b + 1, ypow)

        @block.scalar
        def _(act):
            act.wait_ge(c_in, 16)
            act.activation(csil[:, :], ccol[:, :], ACT.Exp, scale=-1.0).then_inc(silu_e, 1)

            def few(o, i):
                act.dma_start(o, i).then_inc(small_in, 16)
            with nc.allow_non_contiguous_dma("column and broadcast loads of small vectors"):
                act.dma_start(posi[:, :], positions.rearrange("a (b p) -> p (a b)", p=P)).then_inc(pos_in, 16)
                few(mcol[:, 2, :], norm_mix_g.rearrange("l (k p) -> p (l k)", p=P))
                few(sinks[:, :], swa_sinks[0:1, :].broadcast_to([P, SH]))
                few(gla_g[:, :], gla_norm_g.rearrange("l h v -> l (h v)").broadcast_to([P, GH * DV]))
                few(wa2[0:RANK, :], gla_w_a2[0])
                few(wa2[RANK:RANK + 1, :], gla_b_a2)
                few(amp_f[:, :], norm_ffn_g[0:1, :].broadcast_to([P, D]))
                few(wr[:, :, 0:NG], w_grp.rearrange("l (k p) n -> p (l k) n", p=P))
                few(wr[:, :, NG:], w_exp.rearrange("l (k p) n -> p (l k) n", p=P))
                few(br[:, 0:NG], b_grp[0:1, :].broadcast_to([P, NG]))
                few(br[:, NG:], b_exp[0:1, :].broadcast_to([P, NE]))
            for b in range(NB):
                act.wait_ge([x_in0, x_in1, x_in2, x_in3][b], 16)
                act.activation(scm[:, b, :], xres[:, b, :], ACT.Square, accum_out=ssq[:, b:b + 1]).then_inc(ssq_ready, 1)
            act.wait_ge(pow_ready, 1)
            act.wait_ge(ssq_ready, NB)
            for b in range(NB):
                act.activation(scm[:, b, :], xres[:, b, :], ACT.Identity, scale=rstd[:, b:b + 1]).then_inc(xs_ready, 1)
            act.wait_ge(col_vec, 2)
            for k in range(1, KD, 2):
                act.wait_ge(x_turned, k + 1)
                act.activation(hT[:, k, :], ps[k % 6][:, :], ACT.Identity, scale=mcol[:, 3, k:k + 1],
                               bias=mcol[:, 1, k:k + 1]).then_inc(h_act, 1)

            mod_dst = {2: gt_a, 4: None, 3: sh_f, 5: gt_f}
            act.wait_ge(ang_ready, 1)
            act.activation(trig[:, 0, :], ang[:, 0, :], ACT.Sin).then_inc(trig_ready, 1)
            act.activation(trig[:, 1, :], ang[:, 1, :], ACT.Sin).then_inc(trig_ready, 1)
            for st in MIXER_ORDER:
                kind = st[0]
                if kind in ("proj", "mod"):
                    r = TURN[st]
                    act.wait_ge(turn_ready, r + 1)
                    if kind == "proj":
                        lo, hi = CHUNKS[st[1]]
                        if r == 0:
                            act.wait_ge(x_turned, KD)
                        act.activation(proj[:, st[2], lo:hi], ps[r % 2][:, 0:hi - lo], ACT.Copy).then_inc(turn_free, 1)
                    else:
                        i = st[1]
                        part, cols = PARTS[i // 2], slice((i % 2) * PC, (i % 2 + 1) * PC)
                        dst = {2: gt_a, 4: sh_f, 3: sh_f, 5: gt_f}[part]
                        if part == 4:
                            act.activation(gt_f[:, cols], ps[r % 2][:, :], ACT.Copy).then_inc(turn_free, 1)
                        else:
                            if part == 5:
                                act.wait_ge(amp_ready, 1)
                            act.activation(dst[:, cols], ps[r % 2][:, :], ACT.Copy).then_inc(turn_free, 1)
                elif kind == "gaT":
                    act.wait_ge(low_t, 1)
                    act.activation(lowT[0:RANK, :], ps[7][0:RANK, :], ACT.Copy).then_inc(low_ready, 1)
                elif kind == "gaZ":
                    act.wait_ge(low_z, 1)
                    act.activation(loga[:, 0:2, :], ps[2][:, :].rearrange("p (b n) -> p b n", b=2), ACT.Copy).then_inc(z_ready, 1)
                    act.activation(loga[:, 2:4, :], ps[7][:, :].rearrange("p (b n) -> p b n", b=2), ACT.Copy).then_inc(z_ready, 1)
                elif kind == "gaL":
                    act.wait_ge(nz_ready, 1)
                    act.activation(lexp[:, :, :], lexp[:, :, :], ACT.Exp).then_inc(e_ready, 1)
                    act.wait_ge(e_ready, 1)
                    act.activation(lexp[:, :, :], lexp[:, :, :], ACT.Ln, bias=1.0).then_inc(l_ready, 1)
                elif kind == "sA":
                    n = st[1]
                    act.wait_ge(sq_t, n + 1)
                    act.activation(sqT[:, :, :], ps[3][:, :].rearrange("p (h t) -> p h t", h=4), ACT.Copy).then_inc(sq_c, 1)
                    for kv in range(SKV):
                        for half in range(2):
                            act.activation(skT[half * HD:(half + 1) * HD, kv, n, :], ps[4][kv * HD:(kv + 1) * HD, 0:P],
                                           ACT.Copy).then_inc(sq_c, 1)
                elif kind == "sX":
                    n = st[1]
                    act.wait_ge(s_max, n + 1)
                    lo = 0 if n else P
                    for h in range(SH):
                        act.activation(probs[:, h, lo:], probs[:, h, lo:], ACT.Exp, bias=sm[:, 1, h:h + 1],
                                       scale=HD ** -0.5, accum_out=sm[:, 2, h:h + 1]).then_inc(s_exp, 1)
                    act.activation(sm[:, 3, :], sm[:, 3, :], ACT.Exp).then_inc(s_exp, 1)
                elif kind == "sD":
                    n = st[1]
                    for i in range(1, 4, 2):
                        act.wait_ge(s_pt, 4 * n + i + 1)
                        if n == 0:
                            act.activation(probsT[:, 2 * i:2 * i + 2, 1, :],
                                           ps[3 + i][:, :].rearrange("p (h c q) -> p h c q", h=2, c=2)[:, :, 1, :],
                                           ACT.Copy).then_inc(s_pc, 1)
                        else:
                            act.activation(probsT[:, 2 * i:2 * i + 2, :, :],
                                           ps[3 + i][:, :].rearrange("p (h c q) -> p h c q", h=2, c=2),
                                           ACT.Copy).then_inc(s_pc, 1)
                elif kind == "gC":
                    n = st[1]
                    act.wait_ge(gb, n + 1)
                    if n >= 1:
                        act.wait_ge(gops, n)
                        act.wait_ge(g_st, 2 * n * GH)
                    else:
                        act.wait_ge(turn_ready, TURN[("proj", 2, 3)] + 1)
                    act.activation(ebr, ps[2][:, :], ACT.Exp).then_inc(gexp, 1)
                    act.activation(enb, ps[2][:, 0:256], ACT.Exp, scale=-1.0).then_inc(gexp, 1)
                    src = ps[7][:, 0:4].rearrange("p (i c) -> p i c", c=2)
                    for odd in range(2):
                        for ch in range(2):
                            act.activation(dec[ch * DK:(ch + 1) * DK, :].rearrange("p (i o c) -> p i o c", i=2, o=2)
                                           [:, :, odd, ch], src[odd * DK:(odd + 1) * DK, :, ch], ACT.Exp)\
                                .then_inc(gexp, 1)
                elif kind == "gD":
                    n = st[1]
                    act.wait_ge(gq_t, n + 1)
                    if n >= 1:
                        act.wait_ge(g_o, n)
                    act.activation(gqT[:, :, :], ps[2][:, :].rearrange("p (h t) -> p h t", h=GH), ACT.Copy,
                                   scale=DK ** -0.5).then_inc(gq_c, 1)
                elif kind == "gate":
                    b = st[1]
                    act.wait_ge(turn_free, TURN[("proj", 4, b)] + 1)
                    act.activation(proj[:, b, CG:CA], proj[:, b, CG:CA], ACT.Silu).then_inc(gate_ready, 1)
                elif kind == "oT":
                    b = st[1]
                    act.wait_ge(mt, 2 * b + 2)
                    act.activation(mixT[b % 2][:, 4:8, :], ps[4][:, :].rearrange("p (k t) -> p k t", k=4), ACT.Copy)\
                        .then_inc(mt_c, 1)
                elif kind == "oM" and st[2] == 1:
                    b = st[1]
                    act.wait_ge(x1_done, 2 * b + 2)
                    act.activation(sq2t, xres[:, b, :], ACT.Square, accum_out=ssq[:, 8 + b:9 + b]).then_inc(sq2, 1)
                elif kind == "oL":
                    b = st[1]
                    for i in range(2):
                        act.wait_ge(h_turned, 2 * b + i + 1)
                        act.activation(hcT[:, 4 * i:4 * i + 4, :], ps[i][:, :].rearrange("p (k t) -> p k t", k=4),
                                       ACT.Copy).then_inc(h_col, 1)
                elif kind == "gF":
                    n = st[1]
                    act.wait_ge(g_o, n + 1)
                    if n >= 1:
                        act.wait_ge(g_mean, n)
                    act.activation(osq, ps[2][:, :], ACT.Square).then_inc(g_osq, 1)
            act.wait_ge(r_dve, 1)
            act.activation(rt[:, 0:16], rt[:, 0:16], ACT.Exp).then_inc(r_exp, 1)
            act.wait_ge(r_dve, 2)
            act.activation(rt[:, 32:36], rt[:, 32:36], ACT.Exp).then_inc(r_exp, 1)

            def turn(e, u):
                act.wait_ge(e_turned, e + 1)
                act.activation(heT[u % 2][:, 4:8, :], ps[1][:, 0:4 * CAP].rearrange("p (k t) -> p k t", k=4),
                               ACT.Copy).then_inc(e_ta, 1)

            def silu(e, u):
                act.wait_ge(e_gu, e + 1)
                act.activation(sg[u % 2], ps[2 + u % 2][:, 0:FC * CAP], ACT.Silu).then_inc(e_silu, 1)

            def group(j, first=False, last=False):
                for u in range(SLOTS):
                    e = SLOTS * j + u
                    silu(e, u)
                    if not (last and u == SLOTS - 1):
                        turn(e + 1, u + 1)
            turn(0, 0)
            group(0, first=True)
            with act.Fori(1, NE // SLOTS - 1) as j:
                group(j)
            group(NE // SLOTS - 1, last=True)

            act.wait_ge(r_dve, 3)
            extra = act.value_load(extra_i[0:1, 0:1], min_val=0, max_val=EXTRA)
            with act.If(extra > 0):
                with act.Fori(0, extra) as m:
                    with act.Fori(0, NE) as e:
                        n = m * NE + e
                        act.wait_ge(ov_t, n + 1)
                        act.activation(heT[0][:, 4:8, :], ps[1][:, 0:4 * CAP].rearrange("p (k t) -> p k t", k=4),
                                       ACT.Copy).then_inc(ov_tc, 1)
                        act.wait_ge(ov_gu, n + 1)
                        act.activation(sg[0], ps[2][:, 0:FC * CAP], ACT.Silu).then_inc(ov_si, 1)
            act.wait_ge(h_ready, NB)
            act.dma_start(fin_g[:, :], final_norm_g.unsqueeze(0).broadcast_to([P, D])).then_inc(fg_in, 16)
            for b in range(NB):
                act.wait_ge(yfin, 2 * (b + 1))
                if b >= 1:
                    act.wait_ge(ysq, b)
                act.activation(ring[:, 4 * D:5 * D], xres[:, b, :], ACT.Square, accum_out=ssq[:, 12 + b:13 + b])\
                    .then_inc(ysq, 1)

        @block.vector
        def _(dve):
            links = [0]

            def link(ins):
                links[0] += 1
                ins.then_inc(chain, 1)
                dve.wait_ge(chain, links[0])

            dve.wait_ge(silu_e, 1)
            link(dve.tensor_scalar(csil[:, :], csil[:, :], 1.0, None, ALU.add))
            link(dve.reciprocal(csil[:, :], csil[:, :]))
            link(dve.tensor_tensor(csil[:, :], csil[:, :], ccol[:, :], ALU.mult))
            ada_sem = [ada_in0, ada_in1, ada_in2]

            def piece(i):
                a = acc[:, i % 2, :]
                if i >= 6:
                    dve.wait_ge(turn_ready, TURN[("mod", i - 2)] + 1)
                elif i >= 2:
                    dve.wait_ge(mod_col, i - 1)
                for k in range(KD):
                    q = 2 * i + k // KH
                    if k % KH == 0:
                        dve.wait_ge(ada_sem[q % 3], 16 * (q // 3 + 1))
                    w = ada_sb[q % 3][:, k % KH, :]
                    to = a if k % 2 == 0 else acc2
                    if k == 1 and i >= 1:
                        dve.wait_ge(acc_ready, i)
                    if k < 2:
                        dve.tensor_scalar(to, w, csil[:, k:k + 1], None, ALU.mult).then_inc(ada_rows, 1)
                    else:
                        dve.wait_ge(ada_rows, KD * i + k - 1)
                        dve.scalar_tensor_tensor(out=to, in0=w, scalar=csil[:, k:k + 1], in1=to,
                                                 op0=ALU.mult, op1=ALU.add).then_inc(ada_rows, 1)
                dve.wait_ge(brow_in, 16 * (i + 1))
                dve.wait_ge(ada_rows, KD * i + KD - 1)
                dve.tensor_tensor(a[0:1, :], a[0:1, :], brow, ALU.add).then_inc(bias_added, 1)
                dve.wait_ge(ada_rows, KD * (i + 1))
                dve.wait_ge(bias_added, i + 1)
                dve.tensor_tensor(a, a, acc2, ALU.add).then_inc(acc_ready, 1)

            piece(0)
            dve.wait_ge(ssq_ready, NB)
            dve.tensor_scalar(ssq[:, 0:NB], ssq[:, 0:NB], 1.0 / D, EPS, ALU.mult, ALU.add).then_inc(mean_ready, 1)
            for i in range(1, 4):
                piece(i)
            dve.wait_ge(mod_col, 4)
            dve.wait_ge(small_in, 160)
            link(dve.tensor_copy(mcol[:, 0, :], ps[7][:, 0:KD]))
            dve.tensor_copy(mcol[:, 1, :], ps[7][:, KD:2 * KD]).then_inc(col_vec, 1)
            dve.scalar_tensor_tensor(out=mcol[:, 3, :], in0=mcol[:, 0, :], scalar=1.0, in1=mcol[:, 2, :],
                                     op0=ALU.add, op1=ALU.mult).then_inc(col_vec, 1)
            dve.wait_ge(col_vec, 2)
            for k in range(0, KD, 2):
                dve.wait_ge(x_turned, k + 1)
                dve.tensor_scalar(hT[:, k, :], ps[k % 6][:, :], mcol[:, 3, k:k + 1], mcol[:, 1, k:k + 1],
                                  ALU.mult, ALU.add).then_inc(h_dve, 1)
            dve.wait_ge(consts, CONSTS)
            dve.wait_ge(pos_in, 16)
            a3 = [ang[:, i, :].rearrange("p (b d) -> p b d", b=NB) for i in range(3)]
            link(dve.tensor_copy(trig[:, 0, 0:NB], posi[:, :]))
            link(dve.tensor_tensor(a3[0], trig[:, 0, 0:NB].unsqueeze(2).broadcast_to([P, NB, HALF]),
                                   freq[:, :].unsqueeze(1).broadcast_to([P, NB, HALF]), ALU.mult))
            magic = 1.5 * 2 ** 23
            link(dve.tensor_scalar(ang[:, 1, :], ang[:, 0, :], float(1 / (2 * np.pi)), magic, ALU.mult, ALU.add))
            link(dve.tensor_scalar(ang[:, 1, :], ang[:, 1, :], -magic, None, ALU.add))
            for part in (6.25, 0.03125, 0.001953125, float(2 * np.pi - 6.283203125)):
                link(dve.scalar_tensor_tensor(out=ang[:, 0, :], in0=ang[:, 1, :], scalar=-part, in1=ang[:, 0, :],
                                              op0=ALU.mult, op1=ALU.add))
            link(dve.tensor_scalar(ang[:, 0, :], ang[:, 0, :], 3.1415925, -3.1415925, ALU.min, ALU.max))
            link(dve.tensor_scalar(ang[:, 1, :], ang[:, 0, :], -1.0, None, ALU.mult))
            link(dve.tensor_tensor(ang[:, 1, :], ang[:, 1, :], ang[:, 0, :], ALU.min))
            dve.tensor_scalar(ang[:, 1, :], ang[:, 1, :], float(np.pi / 2), None, ALU.add).then_inc(ang_ready, 1)
            for st in MIXER_ORDER:
                kind = st[0]
                if kind == "piece":
                    piece(st[1])
                elif kind == "amp":
                    dve.wait_ge(turn_free, TURN[("mod", 7)] + 1)
                    dve.scalar_tensor_tensor(out=amp_f[:, :], in0=gt_f[:, :], scalar=1.0,
                                             in1=amp_f[:, :], op0=ALU.add, op1=ALU.mult).then_inc(amp_ready, 1)
                elif kind == "rope":
                    dve.wait_ge(turn_free, TURN[("proj", 1, NB - 1)] + 1)
                    dve.wait_ge(trig_ready, 2)
                    qk = proj[:, :, CSQ:CSV].rearrange("p b (h d) -> p b h d", h=10)
                    x1, x2 = qk[:, :, :, 0:HALF], qk[:, :, :, HALF:ROPE]
                    t = [ropet[:, f] for f in range(4)]
                    dve.tensor_tensor(t[0], x1, trig_b(1), ALU.mult)
                    dve.tensor_tensor(t[1], x2, trig_b(0), ALU.mult)
                    dve.tensor_tensor(t[2], x2, trig_b(1), ALU.mult)
                    link(dve.tensor_tensor(t[3], x1, trig_b(0), ALU.mult))
                    link(dve.tensor_tensor(x1, t[0], t[1], ALU.subtract))
                    dve.tensor_tensor(x2, t[2], t[3], ALU.add).then_inc(rope_done, 1)
                elif kind == "gaL":
                    dve.wait_ge(z_ready, 2)
                    dve.scalar_tensor_tensor(out=lexp, in0=loga, scalar=-1.0, in1=loga, op0=ALU.mult, op1=ALU.min)\
                        .then_inc(nz_ready, 1)
                elif kind == "gaF":
                    dve.wait_ge(l_ready, 1)
                    dve.scalar_tensor_tensor(out=loga, in0=loga, scalar=0.0, in1=lexp, op0=ALU.min,
                                             op1=ALU.subtract).then_inc(loga_ready, 1)
                elif kind == "sB":
                    n = st[1]
                    lo = 0 if n else P
                    if n >= 1:
                        dve.wait_ge(s_pt, 4 * n)
                    else:
                        dve.wait_ge(rope_done, 1)
                    for h in range(SH):
                        bank, o = score_place(h)
                        dve.wait_ge(s_sc, 4 * n + bank - 2)
                        dve.tensor_tensor_reduce(out=probs[:, h, lo:], in0=ps[bank][:, o + lo:o + 256],
                                                 in1=band[:, lo:], scale=1.0, scalar=-BIG, op0=ALU.add, op1=ALU.max,
                                                 accum_out=sm[:, 0, h:h + 1]).then_inc(s_masked, 1)
                    dve.wait_ge(s_masked, SH * (n + 1))
                    link(dve.scalar_tensor_tensor(out=sm[:, 0, :], in0=sm[:, 0, :], scalar=HD ** -0.5, in1=sinks[:, :],
                                                  op0=ALU.mult, op1=ALU.max))
                    link(dve.tensor_scalar(sm[:, 1, :], sm[:, 0, :], -1.0, None, ALU.mult))
                    dve.tensor_tensor(sm[:, 3, :], sinks[:, :], sm[:, 0, :], ALU.subtract).then_inc(s_max, 1)
                elif kind == "sD":
                    n = st[1]
                    dve.wait_ge(s_exp, (SH + 1) * (n + 1))
                    link(dve.tensor_tensor(sm[:, 4, :], sm[:, 2, :], sm[:, 3, :], ALU.add))
                    dve.reciprocal(sm[:, 5, :], sm[:, 4, :]).then_inc(s_norm, 1)
                    for i in range(0, 4, 2):
                        dve.wait_ge(s_pt, 4 * n + i + 1)
                        src = ps[3 + i][:, :].rearrange("p (h c q) -> p h c q", h=2, c=2)
                        if n == 0:
                            dve.tensor_copy(probsT[:, 2 * i:2 * i + 2, 1, :], src[:, :, 1, :]).then_inc(s_pc, 1)
                        else:
                            dve.tensor_copy(probsT[:, 2 * i:2 * i + 2, :, :], src).then_inc(s_pc, 1)
                elif kind == "sE":
                    n = st[1]
                    dve.wait_ge(s_pv, n + 1)
                    dve.wait_ge(s_norm, n + 1)
                    dve.tensor_tensor(proj[:, n, CSQ:CSK].rearrange("p (h d) -> p h d", h=SH),
                                      ps[3][:, :].rearrange("p (h d) -> p h d", h=SH),
                                      sm[:, 5, :].unsqueeze(2).broadcast_to([P, SH, HD]), ALU.mult).then_inc(s_out, 1)
                elif kind == "gC":
                    if st[1] == 0:
                        dve.wait_ge(turn_ready, TURN[("proj", 2, 3)] + 1)
                        dve.memset(aT, 0.0)
                        link(dve.memset(state, 0.0))
                elif kind == "gD":
                    n = st[1]
                    dve.wait_ge(gexp, 6 * (n + 1))
                    if n >= 1:
                        dve.wait_ge(g_kv, n)
                        dve.wait_ge(gq_t, n)
                    q3 = proj[:, n, CQ:CK].rearrange("p (h d) -> p h d", h=GH).unsqueeze(2).broadcast_to([P, GH, 2, DK])
                    e3 = ebr[:, 0:256].rearrange("p (h d) -> p h d", h=GH).unsqueeze(2).broadcast_to([P, GH, 2, DK])
                    dve.tensor_tensor(qdup, q3, e3, ALU.mult)
                    dve.tensor_tensor(kdec, proj[:, n, CK:CV], enb, ALU.mult)
                    link(dve.tensor_tensor(krem, proj[:, n, CK:CV], ebr[:, 256:512], ALU.mult))
                    k3 = krem.rearrange("p (h d) -> p h d", h=GH).unsqueeze(2).broadcast_to([P, GH, 2, DK])
                    m3 = blockm[:, :].rearrange("p (c d) -> p c d", c=2).unsqueeze(1).broadcast_to([P, GH, 2, DK])
                    dve.tensor_tensor(krm, k3, m3, ALU.mult).then_inc(gops, 1)
                    dve.wait_ge(gq_t, n + 1)
                    if n >= 1:
                        dve.wait_ge(g_a, 2 * n)
                        dve.wait_ge(g_o, n)
                    dve.tensor_copy(gkT, ps[7][:, 256:512].rearrange("p (h t) -> p h t", h=2)).then_inc(gk_c, 1)
                    dve.wait_ge(gq_c, n + 1)
                    dve.tensor_tensor(gqTm, gqT, blockm[:, :].unsqueeze(1).broadcast_to([P, GH, P]), ALU.mult)\
                        .then_inc(gk_c, 1)
                elif kind == "gE":
                    n = st[1]
                    dve.wait_ge(g_a, 2 * (n + 1))
                    if n >= 1:
                        dve.wait_ge(g_o, n)
                    dve.copy_predicated(out=aT, mask=causal[:, :].bitcast(U32).unsqueeze(1).broadcast_to([P, GH, P]),
                                        data=ps[2][:, :].rearrange("p (h t) -> p h t", h=GH)).then_inc(g_am, 1)
                    dve.wait_ge(g_kv, n + 1)
                    kv = ps[7][:, :].rearrange("p (h v) -> p h v", h=GH)
                    for h in range(GH):
                        dve.scalar_tensor_tensor(out=state[CHUNK:P, h, :], in0=state[0:CHUNK, h, :],
                                                 scalar=dec[0:CHUNK, 2 * h:2 * h + 1], in1=kv[0:CHUNK, h, :],
                                                 op0=ALU.mult, op1=ALU.add).then_inc(g_st, 1)
                elif kind == "gs":
                    b = st[1]
                    dve.wait_ge(gate_ready, b + 1)
                    link(dve.tensor_tensor(proj[:, b, CG:CA], proj[:, b, CG:CA], gla_g[:, :], ALU.mult))
                    dve.wait_ge(g_out, b + 1)
                    dve.tensor_tensor(proj[:, b, CV:CG], proj[:, b, CV:CG], proj[:, b, CG:CA], ALU.mult)\
                        .then_inc(gate_scaled, 1)
                elif kind == "oT":
                    b = st[1]
                    dve.wait_ge(mt, 2 * b + 1)
                    dve.tensor_copy(mixT[b % 2][:, 0:4, :], ps[3][:, :].rearrange("p (k t) -> p k t", k=4))\
                        .then_inc(mt_c, 1)
                elif kind == "oM":
                    b, i = st[1:]
                    dve.wait_ge(mo, 2 * b + i + 1)
                    dve.wait_ge(turn_free, len(TURN))
                    cols = slice(512 * i, 512 * (i + 1))
                    t = hreg[:, 3 * D + 512 * i:3 * D + 512 * (i + 1)]
                    link(dve.tensor_tensor(t, ps[5 + i][:, :], gt_a[:, cols], ALU.mult))
                    dve.tensor_tensor(xres[:, b, cols], xres[:, b, cols], t, ALU.add).then_inc(x1_done, 1)
                elif kind == "oN":
                    b = st[1]
                    dve.wait_ge(sq2, b + 1)
                    dve.tensor_scalar(ssq[:, 8 + b:9 + b], ssq[:, 8 + b:9 + b], 1.0 / D, EPS, ALU.mult, ALU.add)\
                        .then_inc(mean2, 1)
                    dve.wait_ge(pow2, b + 1)
                    if b >= 2:
                        dve.wait_ge(h_stored[b - 2], 16)
                        dve.wait_ge(h_turned, 2 * (b - 1))
                    link(dve.scalar_tensor_tensor(out=hb[:, b % 2, :], in0=xres[:, b, :], scalar=rstd[:, 8 + b:9 + b],
                                                  in1=amp_f[:, :], op0=ALU.mult, op1=ALU.mult))
                    dve.tensor_tensor(hb[:, b % 2, :], hb[:, b % 2, :], sh_f[:, :], ALU.add).then_inc(h_ready, 1)
                elif kind == "oL":
                    b = st[1]
                    dve.wait_ge(r_log, b + 1)
                    dve.tensor_tensor(lg[:, b, :], ps[0][:, 0:NR], br[:, :], ALU.add).then_inc(lg_read, 1)
                elif kind == "gF":
                    n = st[1]
                    dve.wait_ge(g_o, n + 1)
                    kv = ps[7][:, :].rearrange("p (h v) -> p h v", h=GH)
                    for h in range(GH):
                        dve.scalar_tensor_tensor(out=state[0:CHUNK, h, :], in0=state[CHUNK:P, h, :],
                                                 scalar=dec[CHUNK:P, 2 * h + 1:2 * h + 2], in1=kv[CHUNK:P, h, :],
                                                 op0=ALU.mult, op1=ALU.add).then_inc(g_st, 1)
                    dve.wait_ge(g_osq, n + 1)
                    link(dve.tensor_reduce(ssq[:, 4:8], osq.rearrange("p (h v) -> p h v", h=GH), AX, ALU.add))
                    dve.tensor_scalar(ssq[:, 4:8], ssq[:, 4:8], 1.0 / DV, EPS, ALU.mult, ALU.add).then_inc(g_mean, 1)
                    dve.wait_ge(g_pow, n + 1)
                    dve.tensor_tensor(proj[:, n, CV:CG].rearrange("p (h v) -> p h v", h=GH),
                                      ps[2][:, :].rearrange("p (h v) -> p h v", h=GH),
                                      rstd[:, 4:8].unsqueeze(2).broadcast_to([P, GH, DV]), ALU.mult).then_inc(g_out, 1)
            r4 = lambda o, n: rt[:, o:o + NB * n].rearrange("p (b n) -> p b n", b=NB)
            col = lambda o: rt[:, o:o + NB]
            wide4 = lambda ap, n: ap.unsqueeze(2).broadcast_to([P, NB, n])
            key4 = lambda ap, n: ap.unsqueeze(1).broadcast_to([P, NB, n])
            L, eg = lg[:, :, 0:NG], r4(0, NG)
            gmax, gate, e12, t1, t2 = col(16), col(20), col(32), col(24), col(28)
            key, oh1, oh2, M = r4(64, NE), r4(192, NE), r4(320, NE), r4(448, NE)
            gk4, goh = r4(576, NG), r4(592, NG)
            kmax = col(608)
            dve.wait_ge(lg_read, NB)
            link(dve.tensor_reduce(gmax, L, AX, ALU.max))
            dve.tensor_tensor(eg, L, wide4(gmax, NG), ALU.subtract).then_inc(r_dve, 1)

            def first_of(values, top, keys, n, key_t, one_hot):
                link(dve.tensor_tensor(key_t, values, wide4(top, n), ALU.is_equal))
                link(dve.tensor_tensor(key_t, key_t, key4(keys, n), ALU.mult))
                link(dve.tensor_reduce(kmax, key_t, AX, ALU.max))
                link(dve.tensor_tensor(one_hot, key_t, wide4(kmax, n), ALU.is_equal))

            first_of(L, gmax, gkey[:, :], NG, gk4, goh)
            link(dve.tensor_scalar(goh, goh, 1.0, BIG, ALU.subtract, ALU.mult))
            for b in range(NB):
                link(dve.tensor_tensor(M[:, b, :].rearrange("p (g e) -> p g e", g=NG),
                                       lg[:, b, NG:].rearrange("p (g e) -> p g e", g=NG),
                                       goh[:, b, :].unsqueeze(2).broadcast_to([P, NG, EPG]), ALU.add))
            link(dve.tensor_reduce(t1, M, AX, ALU.max))
            first_of(M, t1, ekey[:, :], NE, key, oh1)
            link(dve.scalar_tensor_tensor(out=M, in0=oh1, scalar=-3.0 * BIG, in1=M, op0=ALU.mult, op1=ALU.add))
            link(dve.tensor_reduce(t2, M, AX, ALU.max))
            first_of(M, t2, ekey[:, :], NE, key, oh2)
            link(dve.tensor_tensor(key, oh1, oh2, ALU.add))
            dve.sem_inc(r_cnt, 1)
            dve.tensor_tensor(e12, t2, t1, ALU.subtract).then_inc(r_dve, 1)
            dve.wait_ge(r_exp, 2)
            link(dve.tensor_reduce(gate, eg, AX, ALU.add))
            link(dve.tensor_scalar(col(36), e12, 1.0, None, ALU.add))
            link(dve.tensor_tensor(col(36), col(36), gate, ALU.mult))
            link(dve.reciprocal(topw[:, 0, :], col(36)))
            dve.tensor_tensor(topw[:, 1, :], topw[:, 0, :], e12, ALU.mult)
            dve.wait_ge(r_pos, 1)
            pos = ps[2][:, 0:NB * NE].rearrange("p (b n) -> p b n", b=NB)
            link(dve.tensor_scalar(M, pos, float(NE), None, ALU.mult))
            link(dve.tensor_tensor(M, M, key4(eidx[:, :], NE), ALU.add))
            for r, oh in enumerate((oh1, oh2)):
                link(dve.tensor_tensor(key, oh, M, ALU.mult))
                link(dve.tensor_reduce(col(40 + 4 * r), key, AX, ALU.add))
            link(dve.tensor_copy(slot_i[:, :], rt[:, 40:48]))
            dve.sem_inc(slot_ready, 1)
            link(dve.tensor_reduce(col(48)[:, 0:1], ps[2][:, 128:160], AX, ALU.max))
            link(dve.tensor_scalar(rt[:, 52:52 + EXTRA], steps[:, :], col(48)[:, 0:1], None, ALU.is_lt))
            link(dve.tensor_reduce(col(60)[:, 0:1], rt[:, 52:52 + EXTRA], AX, ALU.add))
            link(dve.tensor_copy(extra_i[:, :], col(60)[:, 0:1]))
            dve.sem_inc(r_dve, 1)

            def tokens(tok, pair, f):
                link(dve.tensor_scalar(f, pair, float(SEQ), float(SEQ), ALU.is_ge, ALU.mult))
                return dve.tensor_tensor(tok, pair, f, ALU.subtract)
            dve.wait_ge(tab_in, 16)
            tokens(tabs[:, 0, :], tabs[:, 1, :], tabf[:, :]).then_inc(tok_ready, 1)

            def turn(e, u):
                dve.wait_ge(e_turned, e + 1)
                dve.tensor_copy(heT[u % 2][:, 0:4, :], ps[0][:, 0:4 * CAP].rearrange("p (k t) -> p k t", k=4))\
                    .then_inc(e_td, 1)

            def product(e, u):
                dve.wait_ge(e_silu, e + 1)
                dve.tensor_tensor(eact[u % 2], sg[u % 2].rearrange("p (c t) -> p c t", c=FC),
                                  ps[2 + u % 2][:, FC * CAP:2 * FC * CAP].rearrange("p (c t) -> p c t", c=FC),
                                  ALU.mult).then_inc(e_act, 1)

            def give(e, u, j, first):
                dve.wait_ge(e_down, e + 1)
                if not (first and u < 2):
                    dve.wait_ge(scat[(u + 2) % 4], 16 * (j if u < 2 else j + 1))
                for i in range(2):
                    cols = slice(512 * i, 512 * (i + 1))
                    dve.tensor_tensor(eo[u % 2][:, cols], ps[4 + 2 * (u % 2) + i][0:CAP, :], gt_f[0:CAP, cols],
                                      ALU.mult).then_inc(e_od, 1)

            def group(j, first=False, last=False):
                for u in range(SLOTS):
                    e = SLOTS * j + u
                    product(e, u)
                    if not (last and u == SLOTS - 1):
                        turn(e + 1, u + 1)
                    if not (first and u == 0):
                        give(e - 1, (u + 3) % 4, j - 1 if u == 0 else j, first)
            turn(0, 0)
            group(0, first=True)
            with dve.Fori(1, NE // SLOTS - 1) as j:
                group(j)
            group(NE // SLOTS - 1, last=True)
            give(NE - 1, 3, NE // SLOTS - 1, False)

            dve.wait_ge(r_dve, 3)
            extra = dve.value_load(extra_i[0:1, 0:1], min_val=0, max_val=EXTRA)
            with dve.If(extra > 0):
                with dve.Fori(0, extra) as m:
                    with dve.Fori(0, NE) as e:
                        n = m * NE + e
                        dve.wait_ge(ov_idx, (n + 1) * 16)
                        dve.tensor_scalar(tabf[:, 0:1], now[:, 0, 1:2], float(SEQ), float(SEQ), ALU.is_ge, ALU.mult)\
                            .then_inc(ov_ac, 1)
                        dve.wait_ge(ov_ac, n * 2 + 1)
                        dve.tensor_tensor(now[:, 0, 0:1], now[:, 0, 1:2], tabf[:, 0:1], ALU.subtract).then_inc(ov_tok, 1)
                        dve.wait_ge(ov_t, n + 1)
                        dve.tensor_copy(heT[0][:, 0:4, :], ps[0][:, 0:4 * CAP].rearrange("p (k t) -> p k t", k=4))\
                            .then_inc(ov_tc, 1)
                        dve.wait_ge(ov_si, n + 1)
                        dve.tensor_tensor(eact[0], sg[0].rearrange("p (c t) -> p c t", c=FC),
                                          ps[2][:, FC * CAP:2 * FC * CAP].rearrange("p (c t) -> p c t", c=FC),
                                          ALU.mult).then_inc(ov_ac, 1)
                        dve.wait_ge(ov_dn, n + 1)
                        for i in range(2):
                            cols = slice(512 * i, 512 * (i + 1))
                            dve.tensor_tensor(eo[0][:, cols], ps[4 + i][0:CAP, :], gt_f[0:CAP, cols], ALU.mult)\
                                .then_inc(ov_oc, 1)

            def add_experts(b):
                y1 = ring[:, (2 * (b % 2)) * D:(2 * (b % 2) + 1) * D]
                y2 = ring[:, (2 * (b % 2) + 1) * D:(2 * (b % 2) + 2) * D]
                dve.wait_ge([y_in0, y_in1, y_in2, y_in3][b], 32)
                for i in range(2):
                    cols = slice(512 * i, 512 * (i + 1))
                    dve.scalar_tensor_tensor(out=y1[:, cols], in0=y1[:, cols], scalar=topw[:, 0, b:b + 1],
                                             in1=xres[:, b, cols], op0=ALU.mult, op1=ALU.add).then_inc(y1s, 1)
                for i in range(2):
                    cols = slice(512 * i, 512 * (i + 1))
                    dve.wait_ge(y1s, 2 * b + i + 1)
                    dve.scalar_tensor_tensor(out=xres[:, b, cols], in0=y2[:, cols], scalar=topw[:, 1, b:b + 1],
                                             in1=y1[:, cols], op0=ALU.mult, op1=ALU.add).then_inc(yfin, 1)

            def finish(b):
                dve.wait_ge(ysq, b + 1)
                link(dve.tensor_scalar(ssq[:, 12 + b:13 + b], ssq[:, 12 + b:13 + b], 1.0 / D, EPS, ALU.mult, ALU.add))
                dve.sem_inc(ymean, 1)
                dve.wait_ge(ypow, b + 1)
                if b == 0:
                    dve.wait_ge(fg_in, 16)
                dve.scalar_tensor_tensor(out=xres[:, b, :], in0=xres[:, b, :], scalar=rstd[:, 12 + b:13 + b],
                                         in1=fin_g[:, :], op0=ALU.mult, op1=ALU.mult).then_inc(ynorm, 1)

            for b in range(NB):
                add_experts(b)
                if b >= 1:
                    finish(b - 1)
            finish(NB - 1)

        @block.tensor
        def _(pe):
            pe.wait_ge(consts, CONSTS)
            def turn_x(k):
                if k >= 6:
                    pe.wait_ge(h_dve if k % 2 == 0 else h_act, 1)
                for b in range(NB):
                    mm = pe.transpose(ps[k % 6][:, b * P:(b + 1) * P], scm[:, b, k * P:(k + 1) * P], ident[:, :])
                mm.then_inc(x_turned, 1)

            def sum_columns(i):
                pe.wait_ge(acc_ready, i + 1)
                for j in range(4):
                    o = (i // 2) * KD + (i % 2) * 4 + j
                    mm = pe.matmul(ps[7][:, o:o + 1], acc[:, i % 2, j * P:(j + 1) * P], ones[:, 0:1], start=True, stop=True)
                mm.then_inc(mod_col, 1)

            sum_columns(0)
            sum_columns(1)
            pe.wait_ge(xs_ready, NB)
            for k in range(6):
                turn_x(k)
            sum_columns(2)
            sum_columns(3)
            turn_x(6)
            turn_x(7)
            pe.wait_ge(h_dve, KD // 2)
            pe.wait_ge(h_act, KD // 2)

            for st in MIXER_ORDER:
                kind = st[0]
                if kind == "proj":
                    ch, b = st[1:]
                    r = TURN[st]
                    if b == 0:
                        pe.wait_ge([wi0, wi1, wi2, wi3, wi4][ch], 16)
                    if r >= 2:
                        pe.wait_ge(turn_free, r - 1)
                    for k in range(KD):
                        mm = pe.matmul(ps[r % 2][:, 0:CW[ch]], hT[:, k, b * P:(b + 1) * P], win_sb[ch][:, k, :],
                                       start=k == 0, stop=k == KD - 1)
                    mm.then_inc(turn_ready, 1)
                elif kind == "mod":
                    r = TURN[st]
                    pe.wait_ge(acc_ready, st[1] + 1)
                    pe.wait_ge(turn_free, r - 1)
                    pe.matmul(ps[r % 2][:, :], ones[:, :], acc[:, st[1] % 2, :], start=True, stop=True)\
                        .then_inc(turn_ready, 1)
                elif kind == "gaT":
                    pe.wait_ge(turn_free, TURN[("proj", 0, NB - 1)] + 1)
                    for b in range(NB):
                        mm = pe.transpose(ps[7][0:RANK, b * P:(b + 1) * P], proj[:, b, CA:CA + RANK], ident[:, :])
                    mm.then_inc(low_t, 1)
                elif kind == "gaZ":
                    pe.wait_ge(low_ready, 1)
                    for b in range(NB):
                        mm = pe.matmul(ps[2 if b < 2 else 7][:, (b % 2) * 256:(b % 2) * 256 + 256],
                                       lowT[0:RANK + 1, b * P:(b + 1) * P], wa2[:, :], start=True, stop=True)
                    mm.then_inc(low_z, 1)
                elif kind == "sA":
                    n = st[1]
                    pe.wait_ge(rope_done, 1)
                    if n >= 1:
                        pe.wait_ge(s_pc, 4 * n)
                        if n >= 2:
                            pe.wait_ge(s_out, n - 1)
                    for i in range(4):
                        pe.transpose(ps[3][:, i * P:(i + 1) * P], proj[:, n, CSQ + i * P:CSQ + (i + 1) * P],
                                     ident[:, :])
                    pe.transpose(ps[4][:, 0:P], proj[:, n, CSK:CSV], ident[:, :]).then_inc(sq_t, 1)
                elif kind == "sB":
                    n = st[1]
                    pe.wait_ge(sq_c, 5 * (n + 1))
                    if n >= 1:
                        pe.wait_ge(s_pc, 4 * n)
                        pe.wait_ge(s_out, n)
                    for h in range(SH):
                        kv, i = h // 4, h // 2
                        rows = slice((h % 2) * HD, (h % 2 + 1) * HD)
                        bank, o = score_place(h)
                        if n >= 1:
                            mm = pe.matmul(ps[bank][:, o:o + 256], sqT[rows, i, :],
                                           skT[rows, kv, n - 1:n + 1, :].rearrange("p b s -> p (b s)"), start=True, stop=True)
                        else:
                            mm = pe.matmul(ps[bank][:, o + P:o + 256], sqT[rows, i, :], skT[rows, kv, n, :],
                                           start=True, stop=True)
                        if h % 4 >= 2:
                            mm.then_inc(s_sc, 1)
                elif kind == "sD":
                    n = st[1]
                    pe.wait_ge(s_exp, (SH + 1) * (n + 1))
                    if n >= 1:
                        pe.wait_ge(s_out, n)
                    for h in range(SH):
                        for cc in range(0 if n else 1, 2):
                            mm = pe.transpose(ps[3 + h // 2][:, (h % 2) * 256 + cc * P:(h % 2) * 256 + (cc + 1) * P],
                                              probs[:, h, cc * P:(cc + 1) * P], ident[:, :])
                        if h % 2:
                            mm.then_inc(s_pt, 1)
                elif kind == "sE":
                    n = st[1]
                    pe.wait_ge(s_pc, 4 * (n + 1))
                    if n + 1 < NB:
                        pe.wait_ge(sq_c, 5 * (n + 2))
                    for h in range(SH):
                        kv = h // 4
                        for cc in range(0 if n else 1, 2):
                            mm = pe.matmul(ps[3][:, h * HD:(h + 1) * HD], probsT[:, h, cc, :],
                                           proj[:, n - 1 + cc, CSV + kv * HD:CSV + (kv + 1) * HD],
                                           start=cc == (0 if n else 1), stop=cc == 1)
                    mm.then_inc(s_pv, 1)
                elif kind == "gC":
                    n = st[1]
                    if n == 0:
                        pe.wait_ge(loga_ready, 1)
                    else:
                        pe.wait_ge(g_out, n)
                        pe.wait_ge(g_st, 2 * GH * n)
                    pe.matmul(ps[2][:, 0:256], u16[:, :], loga[:, n, :], start=True, stop=True)
                    pe.matmul(ps[2][:, 256:512], r16[:, :], loga[:, n, :], start=True, stop=True)
                    for i in range(2):
                        mm = pe.matmul(ps[7][:, 2 * i:2 * i + 2], loga[:, n, i * P:(i + 1) * P], ind16[:, :],
                                       start=True, stop=True)
                    mm.then_inc(gb, 1)
                elif kind == "gD":
                    n = st[1]
                    pe.wait_ge(gops, n + 1)
                    pe.wait_ge(gexp, 6 * (n + 1))
                    for h in range(GH):
                        pe.transpose(ps[2][:, h * P:(h + 1) * P], qdup[:, h].rearrange("p c d -> p (c d)"), ident[:, :])
                    for i in range(2):
                        mm = pe.transpose(ps[7][:, 256 + i * P:256 + (i + 1) * P], kdec[:, i * P:(i + 1) * P], ident[:, :])
                    mm.then_inc(gq_t, 1)
                elif kind == "gE":
                    n = st[1]
                    pe.wait_ge(gk_c, 2 * (n + 1))
                    pe.wait_ge(gq_c, n + 1)
                    for odd in range(2):
                        for h in range(odd, GH, 2):
                            rows = slice(odd * DK, (odd + 1) * DK)
                            mm = pe.matmul(ps[2][:, h * P:(h + 1) * P], gkT[rows, h // 2, :], gqT[rows, h, :],
                                           start=True, stop=True)
                        mm.then_inc(g_a, 1)
                        if odd == 0:
                            pe.wait_ge(g_a, 2 * n + 1)
                    pe.wait_ge(turn_free, TURN[("proj", 3, n)] + 1)
                    for h in range(GH):
                        mm = pe.matmul(ps[7][:, h * DV:(h + 1) * DV], krm[:, h].rearrange("p c d -> p (c d)"),
                                       proj[:, n, CV + h * DV:CV + (h + 1) * DV], start=True, stop=True)
                    mm.then_inc(g_kv, 1)
                elif kind == "oT":
                    b = st[1]
                    if b == 0:
                        pe.wait_ge(s_out, NB)
                    else:
                        pe.wait_ge(mt_c, 2 * b)
                    pe.wait_ge(gate_scaled, b + 1)
                    for i in range(2):
                        for k in range(4 * i, 4 * i + 4):
                            lo = (CV if i == 0 else CSQ) + (k % 4) * P
                            mm = pe.transpose(ps[3 + i][:, (k % 4) * P:(k % 4 + 1) * P], proj[:, b, lo:lo + P],
                                              ident[:, :])
                        mm.then_inc(mt, 1)
                elif kind == "oM":
                    b, i = st[1:]
                    if b == 0:
                        pe.wait_ge(wo_in, 16)
                    else:
                        pe.wait_ge(x1_done, 2 * b - 1 + i)
                    pe.wait_ge(mt_c, 2 * b + 2)
                    for k in range(KD):
                        mm = pe.matmul(ps[5 + i][:, :], mixT[b % 2][:, k, :], wout_sb[:, k, 512 * i:512 * (i + 1)],
                                       start=k == 0, stop=k == KD - 1)
                    mm.then_inc(mo, 1)
                elif kind == "oL":
                    b = st[1]
                    pe.wait_ge(h_ready, b + 1)
                    pe.wait_ge(turn_free, len(TURN))
                    if b >= 1:
                        pe.wait_ge(lg_read, b)
                    for i in range(2):
                        for k in range(4 * i, 4 * i + 4):
                            mm = pe.transpose(ps[i][:, (k % 4) * P:(k % 4 + 1) * P], hb[:, b % 2, k * P:(k + 1) * P],
                                              ident[:, :])
                        mm.then_inc(h_turned, 1)
                    pe.wait_ge(h_col, 2 * b + 2)
                    for k in range(KD):
                        mm = pe.matmul(ps[0][:, 0:NR], hcT[:, k, :], wr[:, k, :], start=k == 0, stop=k == KD - 1)
                    mm.then_inc(r_log, 1)
                elif kind == "gF":
                    n = st[1]
                    pe.wait_ge(g_am, n + 1)
                    pe.wait_ge(g_st, 2 * GH * n + GH)
                    for h in range(GH):
                        o = ps[2][:, h * DV:(h + 1) * DV]
                        pe.matmul(o, aT[:, h, :], proj[:, n, CV + h * DV:CV + (h + 1) * DV], start=True, stop=False)
                        mm = pe.matmul(o, gqTm[:, h, :], state[:, h, :], start=False, stop=True)
                    mm.then_inc(g_o, 1)

            pe.wait_ge(r_cnt, 1)
            cnt = rt[:, 64:64 + NB * NE].rearrange("p (b n) -> p b n", b=NB)
            for b in range(NB):
                for a in range(b):
                    pe.matmul(ps[2][:, b * NE:(b + 1) * NE], ones[:, :], cnt[:, a, :], start=a == 0, stop=False)
                pe.matmul(ps[2][:, b * NE:(b + 1) * NE], ustrict[:, :], cnt[:, b, :], start=b == 0, stop=True)
            for a in range(NB):
                mm = pe.matmul(ps[2][:, 128:160], ones[:, :], cnt[:, a, :], start=a == 0, stop=a == NB - 1)
            mm.then_inc(r_pos, 1)

            def turn_tile(src, done):
                for i in range(2):
                    for k in range(4 * i, 4 * i + 4):
                        rows = src.rearrange("t (p k) -> t k p", k=KD)[:, k, :]
                        mm = pe.transpose(ps[i][:, (k % 4) * CAP:(k % 4 + 1) * CAP], rows, ident[0:CAP, 0:CAP])
                mm.then_inc(done, 1)

            def gate_up(bank, w, u, hx, done):
                for m, wt in enumerate((wg_sb[w], wu_sb[w])):
                    for f in range(FC):
                        o = (m * FC + f) * CAP
                        for k in range(KD):
                            mm = pe.matmul(ps[bank][:, o:o + CAP], wt[:, k, f * P:(f + 1) * P], hx[:, k, :],
                                           start=k == 0, stop=k == KD - 1)
                mm.then_inc(done, 1)

            def down_tile(bank, w, a, done):
                for i in range(2):
                    for f in range(FC):
                        mm = pe.matmul(ps[bank + i][0:CAP, :], a[:, f, :], wd_sb[w][:, f, 512 * i:512 * (i + 1)],
                                       start=f == 0, stop=f == FC - 1)
                mm.then_inc(done, 1)

            def turn(e, u, j):
                pe.wait_ge(gath[u], 16 * (j + 1))
                turn_tile(hg[u], e_turned)

            def down(e, u, j, first):
                pe.wait_ge(e_act, e + 1)
                pe.wait_ge(wd_sem[u], 16 * (j + 1))
                if not (first and u < 2):
                    pe.wait_ge(e_od, 2 * (e - 1))
                down_tile(4 + 2 * (u % 2), u, eact[u % 2], e_down)

            def group(j, first=False, last=False):
                for u in range(SLOTS):
                    e = SLOTS * j + u
                    pe.wait_ge(e_ta, e + 1)
                    pe.wait_ge(e_td, e + 1)
                    pe.wait_ge(w_sem[u], 32 * (j + 1))
                    if not (first and u < 2):
                        pe.wait_ge(e_act, e - 1)
                    gate_up(2 + u % 2, u, u, heT[u % 2], e_gu)
                    if not (last and u == SLOTS - 1):
                        turn(e + 1, (u + 1) % 4, j + 1 if u == SLOTS - 1 else j)
                    if not (first and u == 0):
                        down(e - 1, (u + 3) % 4, j - 1 if u == 0 else j, first)
            pe.wait_ge(slot_ready, 1)
            pe.wait_ge(r_dve, 3)
            turn(0, 0, 0)
            group(0, first=True)
            with pe.Fori(1, NE // SLOTS - 1) as j:
                group(j)
            group(NE // SLOTS - 1, last=True)
            down(NE - 1, 3, NE // SLOTS - 1, False)

            extra = pe.value_load(extra_i[0:1, 0:1], min_val=0, max_val=EXTRA)
            with pe.If(extra > 0):
                pe.wait_ge(e_od, 2 * NE)
                with pe.Fori(0, extra) as m:
                    with pe.Fori(0, NE) as e:
                        n = m * NE + e
                        pe.wait_ge(ov_hg, (n + 1) * 16)
                        turn_tile(hg[0], ov_t)
                        pe.wait_ge(ov_tc, (n + 1) * 2)
                        pe.wait_ge(ov_w, (n + 1) * 48)
                        gate_up(2, 0, 0, heT[0], ov_gu)
                        pe.wait_ge(ov_ac, (n + 1) * 2)
                        down_tile(4, 0, eact[0], ov_dn)


_INS = ["x", "c", "positions", "ada_w", "ada_b", "norm_mix_g", "w_in", "gla_w_a2", "gla_b_a2", "gla_norm_g",
        "swa_sinks", "w_out", "norm_ffn_g", "w_grp", "b_grp", "w_exp", "b_exp", "w_gate", "w_up", "w_down",
        "final_norm_g"]


def kernel(**inputs):
    import concourse.bacc as bacc
    from concourse.bass_utils import run_bass_kernel_spmd

    nc = bacc.Bacc("TRN2", target_bir_lowering=False, num_devices=1)
    arrays, args = {}, []
    for name in _INS:
        a = np.ascontiguousarray(inputs[name])
        arrays[f"in_{name}"] = a
        args.append(nc.dram_tensor(f"in_{name}", a.shape, mybir.dt.from_np(a.dtype), kind="ExternalInput").ap())
    out = nc.dram_tensor("out_x", [1, SEQ, D], F32, kind="ExternalOutput").ap()
    layer_kernel(nc, *args, out)
    r = run_bass_kernel_spmd(nc, [arrays], core_ids=[0])
    return r.results[0]["out_x"]
```

```python
from contextlib import ExitStack

import numpy as np
import concourse.bass as bass
from concourse import mybir

P = 128
SEQ, D = 512, 1024
NB = SEQ // P
KD = D // P
GH, DK, DV, RANK = 4, 64, 128, 16
CHUNK = 64
SH, SKV, HD = 8, 2, 64
ROPE = HD // 4
HALF = ROPE // 2
THETA = 500000.0
NG, EPG = 4, 8
NE = NG * EPG
F = 256
FC = F // P
EPS = 1e-6
CQ, CK, CV, CG = 0, GH * DK, 2 * GH * DK, 2 * GH * DK + GH * DV
CA = CG + GH * DV
CSQ = CA + RANK
CSK = CSQ + SH * HD
CSV = CSK + SKV * HD
WIN = CSV + SKV * HD
CHUNKS = [(CA, CA + 512), (CA + 512, WIN), (CQ, CV), (CV, CG), (CG, CA)]
NCH = len(CHUNKS)
PARTS = [1, 0, 2, 4, 3, 5]
PC = 512
NPC = 2 * len(PARTS)
KH = KD // 2
CAP = 96
EXTRA = -(-SEQ // CAP) - 1
ROWS = (EXTRA + 1) * CAP
PAD = 8192
BIG = 1.0e30
SLOTS = 4
AHEAD = 3

F32, I32, U32 = mybir.dt.float32, mybir.dt.int32, mybir.dt.uint32
ALU = mybir.AluOpType
ACT = mybir.ActivationFunctionType
AX = mybir.AxisListType.X

def _projected(n, first, second, mods=()):
    last = n + 1 == NB
    return ([first, ("gla_decay", n), ("probs_turn", n), second, *mods, ("gla_operands", n)] +
            ([] if last else [("attn_turn", n + 1)]) + [("attn_value", n), ("gla_scores", n)] +
            ([("gate_scale", 0), ("mix_turn", 0)] if last else [("attn_score", n + 1)]) + [("gla_output", n)] +
            ([] if last else [("attn_exp", n + 1)]))


MIXER_ORDER = (
    [("ada_sum", 4), ("ada_sum", 5), ("proj", 0, 0), ("proj", 0, 1), ("mod", 4), ("ada_sum", 6), ("proj", 0, 2),
     ("proj", 0, 3), ("mod", 5), ("ada_sum", 7), ("proj", 1, 0), ("low_turn",), ("mod", 6), ("proj", 1, 1),
     ("proj", 1, 2), ("mod", 7), ("proj", 1, 3), ("rope",), ("decay_logit",), ("amp",), ("log_sigmoid",)] +
    [("proj", 2, 0), ("ada_sum", 8), ("proj", 2, 1), ("mod", 8), ("decay",), ("attn_turn", 0), ("ada_sum", 9),
     ("proj", 2, 2), ("mod", 9), ("attn_score", 0), ("attn_exp", 0), ("ada_sum", 10), ("ada_sum", 11),
     ("proj", 2, 3), ("mod", 10)] +
    _projected(0, ("proj", 3, 0), ("proj", 3, 1), [("mod", 11)]) + _projected(1, ("proj", 3, 2), ("proj", 3, 3)) +
    _projected(2, ("proj", 4, 0), ("proj", 4, 1)) + [("gate", 0), ("gate", 1)] +
    _projected(3, ("proj", 4, 2), ("proj", 4, 3)) + [("gate", 2), ("gate", 3), ("gate_scale", 1)] +
    [("out_proj", 0, 0), ("mix_turn", 1), ("out_proj", 0, 1), ("gate_scale", 2), ("norm2", 0),
     ("out_proj", 1, 0), ("mix_turn", 2), ("out_proj", 1, 1), ("gate_scale", 3), ("norm2", 1), ("h_turn", 0),
     ("out_proj", 2, 0), ("router", 0), ("h_turn", 1), ("mix_turn", 3), ("out_proj", 2, 1), ("norm2", 2),
     ("router", 1), ("places", 0), ("out_proj", 3, 0), ("h_turn", 2), ("out_proj", 3, 1),
     ("norm2", 3), ("router", 2), ("places", 1), ("h_turn", 3), ("router", 3), ("places", 2), ("places", 3)]
)
FIRST = [0, 2, 1, 3] + list(range(4, NPC))
X_BANK = [4, 5, 6, 3, 4, 5, 6, 4]
SMALL = 16 * 9
CONSTS = 38

TURN = {s: n for n, s in enumerate(s for s in MIXER_ORDER if s[0] in ("proj", "mod"))}


def layer_kernel(nc, x, c, positions, ada_w, ada_b, norm_mix_g, w_in, gla_w_a2, gla_b_a2, gla_norm_g,
                 swa_sinks, w_out, norm_ffn_g, w_grp, b_grp, w_exp, b_exp, w_gate, w_up, w_down,
                 final_norm_g, out):
    h_rows = nc.dram_tensor("h_rows", [2 * SEQ, D], F32, kind="Internal").ap()
    y_rows = nc.dram_tensor("y_rows", [2 * SEQ, D], F32, kind="Internal").ap()
    table = nc.dram_tensor("pair_table", [ROWS * NE, 1], I32, kind="Internal").ap()

    with ExitStack() as ctx:
        def sb(name, shape, dt=F32):
            return ctx.enter_context(nc.sbuf_tensor(name, shape, dt))

        def sem(name):
            return ctx.enter_context(nc.semaphore(name))

        CW = [hi - lo for lo, hi in CHUNKS]
        ring = sb("ring", [P, KD * WIN])
        at_c = {}
        off = 0
        for ch in (3, 4, 2, 0, 1):
            at_c[ch] = off
            off += KD * CW[ch]
        win_sb = [ring[:, at_c[ch]:at_c[ch] + KD * CW[ch]].rearrange("p (k n) -> p k n", k=KD)
                  for ch in range(NCH)]
        wide = sb("wide", [P, KD * D])
        ada_sb = [wide[:, i * KH * PC:(i + 1) * KH * PC].rearrange("p (k n) -> p k n", k=KH) for i in range(3)]
        o_ = 3 * KH * PC
        acc = wide[:, o_:o_ + 2 * PC].rearrange("p (a n) -> p a n", a=2)
        acc2 = wide[:, o_ + 2 * PC:o_ + 3 * PC]
        brow = wide[0:1, o_ + 3 * PC:o_ + 4 * PC]
        wout_sb = wide[:, :].rearrange("p (k n) -> p k n", k=KD)
        xres = sb("xres", [P, NB, D])
        hreg = sb("hreg", [P, KD * SEQ])
        hT = hreg[:, :].rearrange("p (k t) -> p k t", k=KD)
        proj = sb("proj", [P, NB, WIN])
        pflat = proj[:, :, :].rearrange("p b n -> p (b n)")
        scm = proj[:, :, 0:D]

        def shared(ch, start, size):
            return ring[:, at_c[ch] + start:at_c[ch] + start + size]

        probs = shared(0, 0, SH * 2 * P).rearrange("p (h s) -> p h s", h=SH)
        probsT = shared(0, SH * 2 * P, SH * 2 * P).rearrange("p (h c q) -> p h c q", h=SH, c=2)
        ropet = shared(0, 0, 4 * NB * 10 * HALF).rearrange("p (f b h d) -> p f b h d", f=4, b=NB, h=10)
        loga = shared(1, 0, NB * GH * DK).rearrange("p (b n) -> p b n", b=NB)
        lexp = shared(1, NB * GH * DK, NB * GH * DK).rearrange("p (b n) -> p b n", b=NB)
        gqT = shared(1, 1024, 512).rearrange("p (h t) -> p h t", h=GH)
        gqTm = shared(1, 1536, 512).rearrange("p (h t) -> p h t", h=GH)
        ebr = shared(2, 0, 512)
        enb = shared(2, 512, 256)
        krem = shared(2, 768, 256)
        qdup = shared(2, 1024, 512).rearrange("p (h c d) -> p h c d", h=GH, c=2)
        krm = shared(2, 1536, 512).rearrange("p (h c d) -> p h c d", h=GH, c=2)
        gkT = shared(2, 2048, 256).rearrange("p (h t) -> p h t", h=2)
        aT = shared(2, 2304, 512).rearrange("p (h t) -> p h t", h=GH)
        state = shared(2, 2816, 512).rearrange("p (h v) -> p h v", h=GH)
        kdec = shared(2, 3328, 256)
        osq = shared(2, 3584, 512)

        gt_a = sb("gt_a", [P, D])
        amp_f = sb("amp_f", [P, D])
        sh_f = sb("sh_f", [P, D])
        gt_f = sb("gt_f", [P, D])
        gla_g = sb("gla_g", [P, GH * DV])
        sqT = sb("sqT", [P, 4, P])
        skT = sb("skT", [P, SKV, NB, P])
        lowT = sb("lowT", [32, SEQ])
        wa2 = sb("wa2", [RANK + 1, GH * DK])
        fin_g = amp_f

        ident = sb("ident", [P, P])
        causal = sb("causal", [P, P])
        u16 = sb("u16", [P, P])
        r16 = sb("r16", [P, P])
        ind16 = sb("ind16", [P, 2])
        blockm = sb("blockm", [P, P])
        band = sb("band", [P, 2 * P])
        ones = sb("ones", [P, P])

        ccol = sb("ccol", [P, KD])
        csil = sb("csil", [P, KD])
        mcol = sb("mcol", [P, 4, KD])
        ssq = sb("ssq", [P, 16])
        rstd = sb("rstd", [P, 16])
        halfm = sb("halfm", [P, 4])
        posi = sb("posi", [P, NB], I32)
        freq = sb("freq", [P, HALF])
        ang = sb("ang", [P, 3, NB * HALF])
        trig = sb("trig", [P, 2, NB * HALF])
        sinks = sb("sinks", [P, SH])
        sm = sb("sm", [P, 6, SH])
        dec = sb("dec", [P, 8])

        ps = [ctx.enter_context(nc.psum_tensor(f"ps{i}", [P, 512], F32)) for i in range(8)]

        consts, chain, c_in, x_in0 = (
            sem(n) for n in ('consts', 'chain', 'c_in', 'x_in0'))
        x_in1, x_in2, x_in3, pos_in = (
            sem(n) for n in ('x_in1', 'x_in2', 'x_in3', 'pos_in'))
        gain_in, small_in, ada_in0, ada_in1 = (
            sem(n) for n in ('gain_in', 'small_in', 'ada_in0', 'ada_in1'))
        ada_in2, brow_in, win_in0, win_in1 = (
            sem(n) for n in ('ada_in2', 'brow_in', 'win_in0', 'win_in1'))
        win_in2, win_in3, win_in4, wout_in = (
            sem(n) for n in ('win_in2', 'win_in3', 'win_in4', 'wout_in'))
        silu_e, ssq_ready, mean1_ready, rstd1_ready = (
            sem(n) for n in ('silu_e', 'ssq_ready', 'mean1_ready', 'rstd1_ready'))
        xs_ready, ada_rows, bias_added, acc_ready = (
            sem(n) for n in ('xs_ready', 'ada_rows', 'bias_added', 'acc_ready'))
        mod_col, col_vec, x_turned, h_dve = (
            sem(n) for n in ('mod_col', 'col_vec', 'x_turned', 'h_dve'))
        h_act, amp_ready = (
            sem(n) for n in ('h_act', 'amp_ready'))
        turn_ready, turn_free, ang_ready, trig_ready = (
            sem(n) for n in ('turn_ready', 'turn_free', 'ang_ready', 'trig_ready'))
        rope_done, low_turned, low_ready, logit_ready = (
            sem(n) for n in ('rope_done', 'low_turned', 'low_ready', 'logit_ready'))
        logit_copied, negabs_ready, negabs_exp, ln_ready = (
            sem(n) for n in ('logit_copied', 'negabs_ready', 'negabs_exp', 'ln_ready'))
        loga_ready = sem('loga_ready')
        attn_turned, attn_copied, scores_ready, scores_masked = (
            sem(n) for n in ('attn_turned', 'attn_copied', 'scores_ready', 'scores_masked'))
        rowmax_ready, probs_ready, sums_ready, probs_turned = (
            sem(n) for n in ('rowmax_ready', 'probs_ready', 'sums_ready', 'probs_turned'))
        probs_copied, values_ready, attn_out = (
            sem(n) for n in ('probs_copied', 'values_ready', 'attn_out'))
        gla_logs, gla_exps, gla_ops, gla_turned = (
            sem(n) for n in ('gla_logs', 'gla_exps', 'gla_ops', 'gla_turned'))
        gla_q_copied, gla_k_copied, gla_scored, gla_masked = (
            sem(n) for n in ('gla_q_copied', 'gla_k_copied', 'gla_scored', 'gla_masked'))
        gla_kv, gla_state, gla_out, gla_squared = (
            sem(n) for n in ('gla_kv', 'gla_state', 'gla_out', 'gla_squared'))
        gla_mean, gla_rstd, gla_normed, gate_ready = (
            sem(n) for n in ('gla_mean', 'gla_rstd', 'gla_normed', 'gate_ready'))
        gate_scaled = sem('gate_scaled')
        mix_turned, mix_copied, out_proj_done, x1_done = (
            sem(n) for n in ('mix_turned', 'mix_copied', 'out_proj_done', 'x1_done'))
        squares2, mean2, rstd2, h_ready = (
            sem(n) for n in ('squares2', 'mean2', 'rstd2', 'h_ready'))
        h_st0, h_st1, h_st2, h_st3 = (
            sem(n) for n in ('h_st0', 'h_st1', 'h_st2', 'h_st3'))
        h_turned, h_col = (
            sem(n) for n in ('h_turned', 'h_col'))
        logits_ready, logits_read, pairs_marked, places_ready = (
            sem(n) for n in ('logits_ready', 'logits_read', 'pairs_marked', 'places_ready'))
        slot_ready, router_step, router_exps, table_set = (
            sem(n) for n in ('slot_ready', 'router_step', 'router_exps', 'table_set'))
        table_out, ids_out, tab_in = (
            sem(n) for n in ('table_out', 'ids_out', 'tab_in'))
        w_in0, w_in1, w_in2, w_in3 = (
            sem(n) for n in ('w_in0', 'w_in1', 'w_in2', 'w_in3'))
        wd_in0, wd_in1, wd_in2, wd_in3 = (
            sem(n) for n in ('wd_in0', 'wd_in1', 'wd_in2', 'wd_in3'))
        hg_init, idx_ready, pair_ready, dma_let = (
            sem(n) for n in ('hg_init', 'idx_ready', 'pair_ready', 'dma_let'))
        gath0, gath1, gath2, gath3 = (
            sem(n) for n in ('gath0', 'gath1', 'gath2', 'gath3'))
        scat0, scat1, scat2, scat3 = (
            sem(n) for n in ('scat0', 'scat1', 'scat2', 'scat3'))
        e_turned, e_tokens_dve, e_tokens_act, e_gate_up = (
            sem(n) for n in ('e_turned', 'e_tokens_dve', 'e_tokens_act', 'e_gate_up'))
        e_silu, e_act, e_down, e_out = (
            sem(n) for n in ('e_silu', 'e_act', 'e_down', 'e_out'))
        ov_w, ov_idx, ov_gath = (
            sem(n) for n in ('ov_w', 'ov_idx', 'ov_gath'))
        ov_turned, ov_copied, ov_gate_up, ov_silu = (
            sem(n) for n in ('ov_turned', 'ov_copied', 'ov_gate_up', 'ov_silu'))
        ov_act, ov_down, ov_out, ov_scat = (
            sem(n) for n in ('ov_act', 'ov_down', 'ov_out', 'ov_scat'))
        ov_free, ov_done = (
            sem(n) for n in ('ov_free', 'ov_done'))
        fg_in, y_in0, y_in1, y_in2 = (
            sem(n) for n in ('fg_in', 'y_in0', 'y_in1', 'y_in2'))
        y_in3, y1_added, y2_added, y_squared = (
            sem(n) for n in ('y_in3', 'y1_added', 'y2_added', 'y_squared'))
        y_mean, y_rstd, ynorm, out_done = (
            sem(n) for n in ('y_mean', 'y_rstd', 'ynorm', 'out_done'))
        w_in_v = w_in.rearrange("l (k p) n -> p (l k) n", p=P)
        w_out_v = w_out.rearrange("l (k p) n -> p (l k) n", p=P)
        ada_v = ada_w.rearrange("l (p k) n -> p (l k) n", k=KD)
        x_v = x.rearrange("a (b p) d -> (a b) p d", p=P)
        out_v = out.rearrange("a (b p) d -> (a b) p d", p=P)
        gate_v = w_gate.rearrange("l g e (p k) f -> (l g e) p (k f)", k=KD)
        up_v = w_up.rearrange("l g e (p k) f -> (l g e) p (k f)", k=KD)
        down_v = w_down.rearrange("l g e (k p) d -> (l g e) p k d", p=P)
        SLOT = 2 * KD * F + FC * D
        slot = [ring[:, i * SLOT:(i + 1) * SLOT] for i in range(3)] + [wide[:, 0:SLOT]]
        wg_sb = [t[:, 0:KD * F].rearrange("p (k f) -> p k f", k=KD) for t in slot]
        wu_sb = [t[:, KD * F:2 * KD * F].rearrange("p (k f) -> p k f", k=KD) for t in slot]
        wd_sb = [t[:, 2 * KD * F:SLOT].rearrange("p (k d) -> p k d", k=FC) for t in slot]
        w_sem = [w_in0, w_in1, w_in2, w_in3]
        wd_sem = [wd_in0, wd_in1, wd_in2, wd_in3]
        h_stored = [h_st0, h_st1, h_st2, h_st3]
        gath = [gath0, gath1, gath2, gath3]
        scat = [scat0, scat1, scat2, scat3]

        hb = hreg[:, 0:2 * D].rearrange("p (a d) -> p a d", a=2)
        hcT = hreg[:, 2 * D:3 * D].rearrange("p (k t) -> p k t", k=KD)
        rt = hreg[:, 3 * D:4 * D]
        mixT = [ring[:, at_c[0] + i * D:at_c[0] + (i + 1) * D].rearrange("p (k t) -> p k t", k=KD) for i in range(2)]
        sq2t = ring[:, at_c[0] + 2 * D:at_c[0] + 3 * D]
        NR = NG + NE
        wr = sb("wr", [P, KD, NR])
        br = sb("br", [P, NR])
        lg = sb("lg", [P, NB, NR])
        topw = sb("topw", [P, 2, NB])
        ustrict = sb("ustrict", [P, P])
        eidx = sb("eidx", [P, NE])
        gkey = sb("gkey", [P, NG])
        ekey = sb("ekey", [P, NE])
        slot_i = sb("slot_i", [P, 2 * NB], I32)
        pair_i = sb("pair_i", [P, 2 * NB], I32)
        steps = sb("steps", [P, EXTRA])
        extra_i = sb("extra_i", [P, 1], I32)
        ids = rt[0:CAP, 704:704 + NE].bitcast(I32)
        now = rt[0:CAP, 800:808].bitcast(I32).rearrange("p (u a) -> p u a", u=4)

        EOFF = [0]

        def take(n):
            EOFF[0] += n
            return pflat[:, EOFF[0] - n:EOFF[0]]
        hg = [take(D)[0:CAP, :] for i in range(4)]
        heT = [take(KD * CAP).rearrange("p (k t) -> p k t", k=KD) for i in range(2)]
        eo = [take(D)[0:CAP, :] for i in range(2)]
        sg = [take(FC * CAP) for i in range(2)]
        eact = [take(FC * CAP).rearrange("p (c t) -> p c t", c=FC) for i in range(2)]
        assert EOFF[0] <= NB * WIN
        padt = shared(1, 2048, ROWS * NE // P // 2).bitcast(I32)
        mo_t = shared(0, 3 * D, D)

        y_sb = [[ring[:, (2 * b + r) * D:(2 * b + r + 1) * D] for r in range(2)] for b in range(NB)]
        x_in = [x_in0, x_in1, x_in2, x_in3]
        y_in = [[y_in0, y_in1, y_in2, y_in3], x_in]

        block = ctx.enter_context(nc.Block())

        def bc(ap, shape):
            return ap.broadcast_to(shape)

        def score_place(h):
            return 3 + h % 2 + 2 * (h // 4), (h // 2 % 2) * 256

        def bank_of(stage):
            return stage[2] if stage[0:2] == ("proj", 0) else TURN[stage] % 2

        def place_bank(b):
            return 2 if b % 2 == 0 else 7

        def trig_b(i):
            return trig[:, i, :].rearrange("p (b d) -> p b d", b=NB).unsqueeze(2).broadcast_to([P, NB, 10, HALF])

        @block.sync
        def _(sp):
            sp.dma_start(ccol[:, :], c.rearrange("a (p k) -> (a p) k", k=KD)).then_inc(c_in, 16)
            ada_sem = [ada_in0, ada_in1, ada_in2]

            def piece(i):
                col = PARTS[i // 2] * D + (i % 2) * PC
                n = FIRST.index(i)
                for kh in range(2):
                    q = 2 * n + kh
                    if q >= 3:
                        sp.wait_ge(ada_rows, KH * (q - 2))
                    sp.dma_start(ada_sb[q % 3], ada_v[:, kh * KH:(kh + 1) * KH, col:col + PC])\
                        .then_inc(ada_sem[q % 3], 16)
                if n >= 1:
                    sp.wait_ge(bias_added, n)
                sp.dma_start(brow, ada_b[0:1, col:col + PC]).then_inc(brow_in, 16)

            def win(ch):
                lo, hi = CHUNKS[ch]
                sp.dma_start(win_sb[ch], w_in_v[:, :, lo:hi])\
                    .then_inc([win_in0, win_in1, win_in2, win_in3, win_in4][ch], 16)

            piece(0)
            for b in range(NB):
                sp.dma_start(xres[:, b, :], x_v[b]).then_inc(x_in[b], 16)
            piece(2)
            win(0)
            piece(1)
            piece(3)
            win(1)
            for i in range(4, 8):
                piece(i)
            win(2)
            piece(8)
            piece(9)
            win(3)
            piece(10)
            win(4)
            piece(11)
            sp.wait_ge(turn_ready, TURN[("mod", NPC - 1)] + 1)
            sp.dma_start(wout_sb, w_out_v).then_inc(wout_in, 16)

            def gates(e, u):
                sp.dma_start(slot[u][:, 0:KD * F], gate_v[e]).then_inc(w_sem[u], 16)
                sp.dma_start(slot[u][:, KD * F:2 * KD * F], up_v[e]).then_inc(w_sem[u], 16)

            def expert(e, u):
                gates(e, u)
                sp.dma_start(wd_sb[u], down_v[e]).then_inc(wd_sem[u], 16)

            def store_h(b):
                sp.wait_ge(h_ready, 2 * (b + 1))
                for r in range(2):
                    sp.dma_start(h_rows[r * SEQ + b * P:r * SEQ + (b + 1) * P, :], hb[:, b % 2, :])\
                        .then_inc(h_stored[b], 16)

            sp.wait_ge(turn_ready, len(TURN))
            expert(0, 0)
            store_h(0)
            sp.wait_ge(gate_scaled, NB)
            expert(1, 1)
            for b in range(1, NB):
                store_h(b)
            sp.wait_ge(out_proj_done, 2 * NB)
            sp.wait_ge(squares2, 2 * NB)
            sp.wait_ge(x1_done, 2 * NB)
            expert(2, 2)
            sp.wait_ge(ids_out, 16 * 2 * NB)
            sp.dma_start(ids, table[0:CAP * NE, :].rearrange("(q e) o -> q (e o)", e=NE))\
                .then_inc(tab_in, 16)
            sp.wait_ge(gath[2], 16)
            expert(3, 3)

            def refill(j):
                for u in range(SLOTS):
                    e = SLOTS * j + u
                    sp.wait_ge(e_gate_up, SLOTS * (j - 1) + u + 1)
                    gates(e, u)
                    sp.wait_ge(e_down, SLOTS * (j - 1) + u + 1)
                    sp.dma_start(wd_sb[u], down_v[e]).then_inc(wd_sem[u], 16)
            with sp.Fori(1, NE // SLOTS) as j:
                refill(j)

            sp.wait_ge(router_step, 3)
            extra = sp.value_load(extra_i[0:1, 0:1], min_val=0, max_val=EXTRA)
            with sp.If(extra > 0):
                sp.wait_ge(e_down, NE)
                with sp.Fori(0, extra) as m:
                    with sp.Fori(0, NE) as e:
                        sp.wait_ge(ov_free, m * NE + e + 1)
                        sp.dma_start(slot[0][:, 0:KD * F], gate_v[e]).then_inc(ov_w, 16)
                        sp.dma_start(slot[0][:, KD * F:2 * KD * F], up_v[e]).then_inc(ov_w, 16)
                        sp.dma_start(wd_sb[0], down_v[e]).then_inc(ov_w, 16)
                        with nc.allow_non_contiguous_dma("one id a place"):
                            sp.dma_start(now[:, 0, 1:2], table[bass.ds((m + 1) * CAP * NE, CAP * NE), :]
                                         .rearrange("(q e) o -> q (e o)", e=NE)[:, bass.ds(e, 1)])\
                                             .then_inc(ov_idx, 16)
                sp.wait_ge(ov_free, extra * NE + 1)
                sp.sem_inc(ov_done, 1)
            for i in range(4):
                sp.wait_ge(scat[i], 16 * (NE // 4))
            for b in range(NB):
                for r in range(2):
                    sp.dma_start(y_sb[b][r], y_rows[r * SEQ + b * P:r * SEQ + (b + 1) * P, :])\
                        .then_inc(y_in[r][b], 16)
            for b in range(NB):
                for i in range(2):
                    cols = slice(512 * i, 512 * (i + 1))
                    sp.wait_ge(ynorm, 2 * b + i + 1)
                    sp.dma_start(out_v[b][:, cols], xres[:, b, cols]).then_inc(out_done, 16)
            sp.wait_ge(out_done, 16 * 2 * NB)

        @block.gpsimd
        def _(pool):
            n_const = [0]

            def made(ins, wait=True):
                n_const[0] += 1
                ins.then_inc(consts, 1)
                if wait:
                    pool.wait_ge(consts, n_const[0])
            made(pool.memset(halfm[:, :], -0.5))
            made(pool.memset(ones[:, :], 1.0))
            made(pool.memset(ident[:, :], 0.0))
            made(pool.affine_select(out=ident[:, :], in_=ident[:, :], compare_op=ALU.not_equal, fill=1.0, base=0,
                                    pattern=[[-1, P]], channel_multiplier=1))
            for i in range(HALF):
                made(pool.memset(freq[:, i:i + 1], float(np.float32(THETA) ** np.float32(-2.0 * i / ROPE))), False)
            made(pool.memset(lowT[:, :], 1.0), False)
            for t, v in ((causal, 1.0), (u16, 1.0 / 16), (r16, 1.0 / 16), (blockm, 0.0), (ind16, 0.0),
                         (band, 0.0), (ustrict, 1.0)):
                made(pool.memset(t[:, :], v))
            for t in (causal, u16):
                made(pool.affine_select(out=t[:, :], in_=t[:, :], compare_op=ALU.is_ge, fill=0.0, base=0,
                                        pattern=[[1, P]], channel_multiplier=-1))
                made(pool.memset(t[0:CHUNK, CHUNK:P], 0.0))
            made(pool.affine_select(out=r16[:, :], in_=r16[:, :], compare_op=ALU.is_ge, fill=0.0, base=-1,
                                    pattern=[[-1, P]], channel_multiplier=1))
            made(pool.memset(r16[CHUNK:P, 0:CHUNK], 0.0))
            made(pool.affine_select(out=ustrict[:, :], in_=ustrict[:, :], compare_op=ALU.is_ge, fill=0.0, base=-1,
                                    pattern=[[1, P]], channel_multiplier=-1))
            made(pool.memset(blockm[0:CHUNK, 0:CHUNK], 1.0))
            made(pool.memset(blockm[CHUNK:P, CHUNK:P], 1.0))
            made(pool.memset(ind16[0:CHUNK, 0:1], 1.0 / 16))
            made(pool.memset(ind16[CHUNK:P, 1:2], 1.0 / 16))
            made(pool.affine_select(out=band[:, 0:P], in_=band[:, 0:P], compare_op=ALU.is_ge, fill=-BIG, base=-1,
                                    pattern=[[1, P]], channel_multiplier=-1))
            made(pool.affine_select(out=band[:, P:2 * P], in_=band[:, P:2 * P], compare_op=ALU.is_ge, fill=-BIG,
                                    base=0, pattern=[[-1, P]], channel_multiplier=1))
            imp = dict(allow_small_or_imprecise_dtypes=True)
            made(pool.iota(eidx[:, :], pattern=[[1, NE]], base=0, channel_multiplier=0, **imp))
            made(pool.iota(ekey[:, :], pattern=[[-1, NE]], base=NE, channel_multiplier=0, **imp))
            made(pool.iota(gkey[:, :], pattern=[[-1, NG]], base=NG, channel_multiplier=0, **imp))
            made(pool.iota(steps[:, :], pattern=[[CAP, EXTRA]], base=CAP, channel_multiplier=0, **imp))
            made(pool.iota(pair_i[:, :], pattern=[[P, 2 * NB]], base=0, channel_multiplier=1))
            assert n_const[0] == CONSTS, n_const[0]

            def power(o, i, ready, n, done):
                pool.wait_ge(ready, n)
                pool.tensor_tensor(rstd[:, o:o + i], ssq[:, o:o + i], halfm[:, 0:i], ALU.pow).then_inc(done, 1)
            power(0, 4, mean1_ready, 1, rstd1_ready)
            pool.wait_ge(turn_ready, TURN[("proj", 1, NB - 1)] + 1)
            pool.memset(padt, PAD).then_inc(table_set, 1)
            pool.wait_ge(table_set, 1)
            pool.dma_start(table.rearrange("(p a n) o -> p a (n o)", p=P, a=2),
                           padt.unsqueeze(1).broadcast_to([P, 2, ROWS * NE // P // 2])).then_inc(table_out, 16)
            for st in MIXER_ORDER:
                if st[0] == "gla_output":
                    power(4, 4, gla_mean, st[1] + 1, gla_rstd)
                elif st[0] == "norm2":
                    power(8 + st[1], 1, mean2, st[1] + 1, rstd2)
                elif st[0] == "places":
                    b = st[1]
                    pool.wait_ge(slot_ready, b + 1)
                    if b == 0:
                        pool.wait_ge(table_out, 16)
                    for i in (b, NB + b):
                        pool.indirect_dma_start(
                            out=table, out_offset=bass.IndirectOffsetOnAxis(ap=slot_i[:, i:i + 1], axis=0),
                            in_=pair_i[:, i:i + 1], in_offset=None).then_inc(ids_out, 16)
                elif st == ("out_proj", 3, 0):
                    pool.wait_ge(mix_copied, 2 * NB)
                    for i in range(4):
                        pool.memset(hg[i], 0.0).then_inc(hg_init, 1)

            for b in range(NB):
                pool.wait_ge(h_stored[b], 2 * 16)
            pool.wait_ge(hg_init, 4)
            pool.wait_ge(tab_in, 16)

            last_pair = pool.to_reg(2 * SEQ - 1)

            def hold():
                pool.sem_inc(dma_let, 1)

            def pick(e, u):
                pool.tensor_copy(now[:, u, 0:1], ids[:, bass.ds(e, 1)]).then_inc(idx_ready, 1)

            def gather(from_ids, u):
                pool.indirect_dma_start(out=hg[u], out_offset=None, in_=h_rows,
                                        in_offset=bass.IndirectOffsetOnAxis(ap=from_ids, axis=0),
                                        bounds_check=last_pair, oob_is_err=False).then_inc(gath[u], 16)

            def scatter(e, u, src, done):
                pool.indirect_dma_start(out=y_rows, out_offset=bass.IndirectOffsetOnAxis(ap=now[:, u, 1:2], axis=0),
                                        in_=src, in_offset=None, bounds_check=last_pair, oob_is_err=False)\
                    .then_inc(done, 16)

            for e in range(AHEAD):
                gather(ids[:, e:e + 1], e)

            def step(e, u, j, first=False, last=False):
                here = e if isinstance(e, int) else pool.snap(e + 0)
                if not (last and u >= 1):
                    ahead = e + AHEAD if isinstance(e, int) else pool.snap(e + AHEAD)
                    into = (u + AHEAD) % 4
                    if not (first and u == 0):
                        pool.wait_ge(e_turned, e)
                        hold()
                    pick(ahead, into)
                    pool.wait_ge(idx_ready, e + 1)
                    hold()
                    gather(now[:, into, 0:1], into)
                if not first:
                    pool.wait_ge(scat[u], 16 * j)
                    hold()
                pool.tensor_copy(now[:, u, 1:2], ids[:, bass.ds(here, 1)]).then_inc(pair_ready, 1)
                pool.wait_ge(pair_ready, e + 1)
                pool.wait_ge(e_out, 2 * (e + 1))
                hold()
                scatter(e, u, eo[u % 2], scat[u])

            for u in range(SLOTS):
                step(u, u, 0, first=True)
            with pool.Fori(1, NE // SLOTS - 1) as j:
                for u in range(SLOTS):
                    step(SLOTS * j + u, u, j)
            for u in range(SLOTS):
                step(NE - SLOTS + u, u, NE // SLOTS - 1, last=True)

            pool.wait_ge(router_step, 3)
            extra = pool.value_load(extra_i[0:1, 0:1], min_val=0, max_val=EXTRA)
            with pool.If(extra > 0):
                for i in range(4):
                    pool.wait_ge(scat[i], 16 * (NE // 4))
                pool.sem_inc(ov_free, 1)
                with pool.Fori(0, extra) as m:
                    with pool.Fori(0, NE) as e:
                        n = m * NE + e
                        pool.wait_ge(ov_idx, (n + 1) * 16)
                        hold()
                        pool.indirect_dma_start(out=hg[0], out_offset=None, in_=h_rows,
                                                in_offset=bass.IndirectOffsetOnAxis(ap=now[:, 0, 1:2], axis=0),
                                                bounds_check=last_pair, oob_is_err=False).then_inc(ov_gath, 16)
                        pool.wait_ge(ov_out, (n + 1) * 2)
                        hold()
                        scatter(e, 0, eo[0], ov_scat)
                        pool.wait_ge(ov_scat, (n + 1) * 16)
                        pool.sem_inc(ov_free, 1)
            for b in range(NB):
                power(8 + b, 1, y_mean, b + 1, y_rstd)

        @block.scalar
        def _(act):
            act.wait_ge(c_in, 16)
            act.activation(csil[:, :], ccol[:, :], ACT.Exp, scale=-1.0).then_inc(silu_e, 1)

            def few(o, i):
                act.dma_start(o, i).then_inc(small_in, 16)
            with nc.allow_non_contiguous_dma("column and broadcast loads of small vectors"):
                act.dma_start(posi[:, :], positions.rearrange("a (b p) -> p (a b)", p=P)).then_inc(pos_in, 16)
                act.dma_start(mcol[:, 2, :], norm_mix_g.rearrange("l (k p) -> p (l k)", p=P)).then_inc(gain_in, 16)
            for b in range(NB):
                act.wait_ge(x_in[b], 16)
                act.activation(scm[:, b, :], xres[:, b, :], ACT.Square, accum_out=ssq[:, b:b + 1])\
                    .then_inc(ssq_ready, 1)
            act.wait_ge(rstd1_ready, 1)
            act.wait_ge(ssq_ready, NB)
            for b in range(NB):
                act.activation(scm[:, b, :], xres[:, b, :], ACT.Identity, scale=rstd[:, b:b + 1])\
                    .then_inc(xs_ready, 1)
            for k in range(1, KD, 2):
                act.wait_ge(col_vec, k // 4 + 1)
                act.wait_ge(x_turned, k + 1)
                act.activation(hT[:, k, :], ps[X_BANK[k]][:, :], ACT.Identity, scale=mcol[:, 3, k:k + 1],
                               bias=mcol[:, 1, k:k + 1]).then_inc(h_act, 1)

            with nc.allow_non_contiguous_dma("broadcast loads of small vectors"):
                few(sinks[:, :], swa_sinks[0:1, :].broadcast_to([P, SH]))
                few(gla_g[:, :], gla_norm_g.rearrange("l h v -> l (h v)").broadcast_to([P, GH * DV]))
                few(wa2[0:RANK, :], gla_w_a2[0])
                few(wa2[RANK:RANK + 1, :], gla_b_a2)
                few(amp_f[:, :], norm_ffn_g[0:1, :].broadcast_to([P, D]))
                few(wr[:, :, 0:NG], w_grp.rearrange("l (k p) n -> p (l k) n", p=P))
                few(wr[:, :, NG:], w_exp.rearrange("l (k p) n -> p (l k) n", p=P))
                few(br[:, 0:NG], b_grp[0:1, :].broadcast_to([P, NG]))
                few(br[:, NG:], b_exp[0:1, :].broadcast_to([P, NE]))

            act.wait_ge(ang_ready, 1)
            act.activation(trig[:, 0, :], ang[:, 0, :], ACT.Sin).then_inc(trig_ready, 1)
            act.activation(trig[:, 1, :], ang[:, 1, :], ACT.Sin).then_inc(trig_ready, 1)
            for st in MIXER_ORDER:
                kind = st[0]
                if kind in ("proj", "mod"):
                    r = TURN[st]
                    act.wait_ge(turn_ready, r + 1)
                    if kind == "proj":
                        lo, hi = CHUNKS[st[1]]
                        if r == 0:
                            act.wait_ge(x_turned, KD)
                        act.activation(proj[:, st[2], lo:hi], ps[bank_of(st)][:, 0:hi - lo], ACT.Copy)\
                            .then_inc(turn_free, 1)
                    else:
                        i = st[1]
                        part, cols = PARTS[i // 2], slice((i % 2) * PC, (i % 2 + 1) * PC)
                        dst = {2: gt_a, 4: gt_f, 3: sh_f, 5: gt_f}[part]
                        if part == 5:
                            act.wait_ge(amp_ready, 1)
                        act.activation(dst[:, cols], ps[bank_of(st)][:, :], ACT.Copy).then_inc(turn_free, 1)
                elif kind == "low_turn":
                    act.wait_ge(low_turned, 1)
                    act.activation(lowT[0:RANK, :], ps[7][0:RANK, :], ACT.Copy).then_inc(low_ready, 1)
                elif kind == "decay_logit":
                    act.wait_ge(logit_ready, 1)
                    act.activation(loga[:, 0:2, :], ps[2][:, :].rearrange("p (b n) -> p b n", b=2), ACT.Copy)\
                        .then_inc(logit_copied, 1)
                    act.activation(loga[:, 2:4, :], ps[7][:, :].rearrange("p (b n) -> p b n", b=2), ACT.Copy)\
                        .then_inc(logit_copied, 1)
                elif kind == "log_sigmoid":
                    act.wait_ge(negabs_ready, 1)
                    act.activation(lexp[:, :, :], lexp[:, :, :], ACT.Exp).then_inc(negabs_exp, 1)
                    act.wait_ge(negabs_exp, 1)
                    act.activation(lexp[:, :, :], lexp[:, :, :], ACT.Ln, bias=1.0).then_inc(ln_ready, 1)
                elif kind == "attn_turn":
                    n = st[1]
                    act.wait_ge(attn_turned, n + 1)
                    act.activation(sqT[:, :, :], ps[3][:, :].rearrange("p (h t) -> p h t", h=4), ACT.Copy)\
                        .then_inc(attn_copied, 1)
                    for kv in range(SKV):
                        for half in range(2):
                            act.activation(skT[half * HD:(half + 1) * HD, kv, n, :], ps[4][kv * HD:(kv + 1) * HD, 0:P],
                                           ACT.Copy).then_inc(attn_copied, 1)
                elif kind == "attn_exp":
                    n = st[1]
                    act.wait_ge(rowmax_ready, n + 1)
                    lo = 0 if n else P
                    for h in range(SH):
                        act.activation(probs[:, h, lo:], probs[:, h, lo:], ACT.Exp, bias=sm[:, 1, h:h + 1],
                                       scale=HD ** -0.5, accum_out=sm[:, 2, h:h + 1]).then_inc(probs_ready, 1)
                    act.activation(sm[:, 3, :], sm[:, 3, :], ACT.Exp).then_inc(probs_ready, 1)
                elif kind == "probs_turn":
                    n = st[1]
                    for i in range(1, 4, 2):
                        act.wait_ge(probs_turned, 4 * n + i + 1)
                        if n == 0:
                            act.activation(probsT[:, 2 * i:2 * i + 2, 1, :],
                                           ps[3 + i][:, :].rearrange("p (h c q) -> p h c q", h=2, c=2)[:, :, 1, :],
                                           ACT.Copy).then_inc(probs_copied, 1)
                        else:
                            act.activation(probsT[:, 2 * i:2 * i + 2, :, :],
                                           ps[3 + i][:, :].rearrange("p (h c q) -> p h c q", h=2, c=2),
                                           ACT.Copy).then_inc(probs_copied, 1)
                elif kind == "gla_decay":
                    n = st[1]
                    act.wait_ge(gla_logs, n + 1)
                    if n >= 1:
                        act.wait_ge(gla_ops, n)
                        act.wait_ge(gla_state, 2 * n * GH)
                    else:
                        act.wait_ge(turn_ready, TURN[("proj", 2, 3)] + 1)
                    act.activation(ebr, ps[2][:, :], ACT.Exp).then_inc(gla_exps, 1)
                    act.activation(enb, ps[2][:, 0:256], ACT.Exp, scale=-1.0).then_inc(gla_exps, 1)
                    src = ps[7][:, 0:4].rearrange("p (i c) -> p i c", c=2)
                    for odd in range(2):
                        for ch in range(2):
                            act.activation(dec[ch * DK:(ch + 1) * DK, :].rearrange("p (i o c) -> p i o c", i=2, o=2)
                                           [:, :, odd, ch], src[odd * DK:(odd + 1) * DK, :, ch], ACT.Exp)\
                                .then_inc(gla_exps, 1)
                elif kind == "gla_operands":
                    n = st[1]
                    act.wait_ge(gla_turned, n + 1)
                    if n >= 1:
                        act.wait_ge(gla_out, n)
                    act.activation(gqT[:, :, :], ps[2][:, :].rearrange("p (h t) -> p h t", h=GH), ACT.Copy,
                                   scale=DK ** -0.5).then_inc(gla_q_copied, 1)
                elif kind == "gate":
                    b = st[1]
                    act.wait_ge(turn_free, TURN[("proj", 4, b)] + 1)
                    act.activation(proj[:, b, CG:CA], proj[:, b, CG:CA], ACT.Silu).then_inc(gate_ready, 1)
                elif kind == "mix_turn":
                    b = st[1]
                    act.wait_ge(mix_turned, 2 * b + 2)
                    act.activation(mixT[b % 2][:, 4:8, :], ps[4][:, :].rearrange("p (k t) -> p k t", k=4), ACT.Copy)\
                        .then_inc(mix_copied, 1)
                elif kind == "out_proj":
                    b, i = st[1:]
                    cols = slice(512 * i, 512 * (i + 1))
                    act.wait_ge(x1_done, 2 * b + i + 1)
                    act.activation(sq2t[:, cols], xres[:, b, cols], ACT.Square, scale=D ** -0.5,
                                   accum_out=ssq[:, 8 + 4 * i + b:9 + 4 * i + b]).then_inc(squares2, 1)
                elif kind == "h_turn":
                    b = st[1]
                    for i in range(2):
                        act.wait_ge(h_turned, 2 * b + i + 1)
                        act.activation(hcT[:, 4 * i:4 * i + 4, :], ps[i][:, :].rearrange("p (k t) -> p k t", k=4),
                                       ACT.Copy).then_inc(h_col, 1)
                elif kind == "gla_output":
                    n = st[1]
                    act.wait_ge(gla_out, n + 1)
                    if n >= 1:
                        act.wait_ge(gla_mean, n)
                    act.activation(osq, ps[2][:, :], ACT.Square).then_inc(gla_squared, 1)
            act.wait_ge(router_step, 1)
            act.activation(rt[:, 0:16], rt[:, 0:16], ACT.Exp).then_inc(router_exps, 1)
            act.wait_ge(router_step, 2)
            act.activation(rt[:, 32:36], rt[:, 32:36], ACT.Exp).then_inc(router_exps, 1)

            def turn(e, u):
                act.wait_ge(e_turned, e + 1)
                act.activation(heT[u % 2][:, 4:8, :], ps[1][:, 0:4 * CAP].rearrange("p (k t) -> p k t", k=4),
                               ACT.Copy).then_inc(e_tokens_act, 1)

            def silu(e, u):
                act.wait_ge(e_gate_up, e + 1)
                act.activation(sg[u % 2], ps[2 + u % 2][:, 0:FC * CAP], ACT.Silu).then_inc(e_silu, 1)

            def group(j, first=False, last=False):
                for u in range(SLOTS):
                    e = SLOTS * j + u
                    silu(e, u)
                    if not (last and u == SLOTS - 1):
                        turn(e + 1, u + 1)
            turn(0, 0)
            group(0, first=True)
            with act.Fori(1, NE // SLOTS - 1) as j:
                group(j)
            group(NE // SLOTS - 1, last=True)

            act.wait_ge(router_step, 3)
            extra = act.value_load(extra_i[0:1, 0:1], min_val=0, max_val=EXTRA)
            with act.If(extra > 0):
                with act.Fori(0, extra) as m:
                    with act.Fori(0, NE) as e:
                        n = m * NE + e
                        act.wait_ge(ov_turned, n + 1)
                        act.activation(heT[0][:, 4:8, :], ps[1][:, 0:4 * CAP].rearrange("p (k t) -> p k t", k=4),
                                       ACT.Copy).then_inc(ov_copied, 1)
                        act.wait_ge(ov_gate_up, n + 1)
                        act.activation(sg[0], ps[2][:, 0:FC * CAP], ACT.Silu).then_inc(ov_silu, 1)
            act.wait_ge(h_ready, 2 * NB)
            act.dma_start(fin_g[:, :], final_norm_g.unsqueeze(0).broadcast_to([P, D])).then_inc(fg_in, 16)
            for b in range(NB):
                for i in range(2):
                    cols = slice(512 * i, 512 * (i + 1))
                    act.wait_ge(y2_added, 2 * b + i + 1)
                    act.activation(y_sb[b][0][:, cols], xres[:, b, cols], ACT.Square, scale=D ** -0.5,
                                   accum_out=ssq[:, 8 + 4 * i + b:9 + 4 * i + b]).then_inc(y_squared, 1)

        @block.vector
        def _(dve):
            links = [0]

            def link(ins):
                links[0] += 1
                ins.then_inc(chain, 1)
                dve.wait_ge(chain, links[0])

            dve.wait_ge(silu_e, 1)
            link(dve.tensor_scalar(csil[:, :], csil[:, :], 1.0, None, ALU.add))
            link(dve.reciprocal(csil[:, :], csil[:, :]))
            link(dve.tensor_tensor(csil[:, :], csil[:, :], ccol[:, :], ALU.mult))
            ada_sem = [ada_in0, ada_in1, ada_in2]

            def piece(i):
                n = FIRST.index(i)
                a = acc[:, n % 2, :]
                if i >= 6:
                    dve.wait_ge(turn_ready, TURN[("mod", i - 2)] + 1)
                elif n >= 2:
                    dve.wait_ge(mod_col, n - 1)
                for k in range(KD):
                    q = 2 * n + k // KH
                    if k % KH == 0:
                        dve.wait_ge(ada_sem[q % 3], 16 * (q // 3 + 1))
                    w = ada_sb[q % 3][:, k % KH, :]
                    to = a if k % 2 == 0 else acc2
                    if k == 1 and n >= 1:
                        dve.wait_ge(acc_ready, n)
                    if k < 2:
                        dve.tensor_scalar(to, w, csil[:, k:k + 1], None, ALU.mult).then_inc(ada_rows, 1)
                    else:
                        dve.wait_ge(ada_rows, KD * n + k - 1)
                        dve.scalar_tensor_tensor(out=to, in0=w, scalar=csil[:, k:k + 1], in1=to,
                                                 op0=ALU.mult, op1=ALU.add).then_inc(ada_rows, 1)
                dve.wait_ge(brow_in, 16 * (n + 1))
                dve.wait_ge(ada_rows, KD * n + KD - 1)
                dve.tensor_tensor(a[0:1, :], a[0:1, :], brow, ALU.add).then_inc(bias_added, 1)
                dve.wait_ge(ada_rows, KD * (n + 1))
                dve.wait_ge(bias_added, n + 1)
                dve.tensor_tensor(a, a, acc2, ALU.add).then_inc(acc_ready, 1)

            piece(0)
            dve.wait_ge(ssq_ready, NB)
            dve.tensor_scalar(ssq[:, 0:NB], ssq[:, 0:NB], 1.0 / D, EPS, ALU.mult, ALU.add).then_inc(mean1_ready, 1)
            for half in range(2):
                if half == 0:
                    piece(2)
                    dve.wait_ge(gain_in, 16)
                else:
                    piece(1)
                    piece(3)
                cols = slice(4 * half, 4 * half + 4)
                dve.wait_ge(mod_col, 2 * half + 2)
                link(dve.tensor_copy(mcol[:, 0:2, cols],
                                     ps[7][:, 0:2 * KD].rearrange("p (a k) -> p a k", a=2)[:, :, cols]))
                dve.scalar_tensor_tensor(out=mcol[:, 3, cols], in0=mcol[:, 0, cols], scalar=1.0, in1=mcol[:, 2, cols],
                                         op0=ALU.add, op1=ALU.mult).then_inc(col_vec, 1)
                dve.wait_ge(col_vec, half + 1)
                for k in (4 * half, 4 * half + 2):
                    dve.wait_ge(x_turned, k + 1)
                    dve.tensor_scalar(hT[:, k, :], ps[X_BANK[k]][:, :], mcol[:, 3, k:k + 1], mcol[:, 1, k:k + 1],
                                      ALU.mult, ALU.add).then_inc(h_dve, 1)
            dve.wait_ge(consts, CONSTS)
            dve.wait_ge(pos_in, 16)
            a3 = [ang[:, i, :].rearrange("p (b d) -> p b d", b=NB) for i in range(3)]
            link(dve.tensor_copy(trig[:, 0, 0:NB], posi[:, :]))
            link(dve.tensor_tensor(a3[0], trig[:, 0, 0:NB].unsqueeze(2).broadcast_to([P, NB, HALF]),
                                   freq[:, :].unsqueeze(1).broadcast_to([P, NB, HALF]), ALU.mult))
            magic = 1.5 * 2 ** 23
            link(dve.tensor_scalar(ang[:, 1, :], ang[:, 0, :], float(1 / (2 * np.pi)), magic, ALU.mult, ALU.add))
            link(dve.tensor_scalar(ang[:, 1, :], ang[:, 1, :], -magic, None, ALU.add))
            for part in (6.25, 0.03125, 0.001953125, float(2 * np.pi - 6.283203125)):
                link(dve.scalar_tensor_tensor(out=ang[:, 0, :], in0=ang[:, 1, :], scalar=-part, in1=ang[:, 0, :],
                                              op0=ALU.mult, op1=ALU.add))
            link(dve.tensor_scalar(ang[:, 0, :], ang[:, 0, :], 3.1415925, -3.1415925, ALU.min, ALU.max))
            link(dve.tensor_scalar(ang[:, 1, :], ang[:, 0, :], -1.0, None, ALU.mult))
            link(dve.tensor_tensor(ang[:, 1, :], ang[:, 1, :], ang[:, 0, :], ALU.min))
            dve.tensor_scalar(ang[:, 1, :], ang[:, 1, :], float(np.pi / 2), None, ALU.add).then_inc(ang_ready, 1)
            col = lambda o: rt[:, o:o + NB]
            by_block = lambda o: rt[:, o:o + NB * NE].rearrange("p (b n) -> p b n", b=NB)
            eg = rt[:, 0:NB * NG].rearrange("p (b n) -> p b n", b=NB)
            gmax, gate, t1, t2, e12 = col(16), col(20), col(24), col(28), col(32)
            cnt, oh1, oh2 = by_block(64), by_block(192), by_block(320)
            M, key = rt[:, 448:448 + NE], rt[:, 480:480 + NE]
            two = rt[:, 512:512 + 2 * NE].rearrange("p (r n) -> p r n", r=2)
            gk, kmax = rt[:, 576:576 + NG], rt[:, 608:609]

            def best(values, top, keys, key_t):
                link(dve.tensor_reduce(top, values, AX, ALU.max))
                link(dve.scalar_tensor_tensor(out=key_t, in0=values, scalar=top, in1=keys,
                                              op0=ALU.is_equal, op1=ALU.mult))
                link(dve.tensor_reduce(kmax, key_t, AX, ALU.max))

            for st in MIXER_ORDER:
                kind = st[0]
                if kind == "ada_sum":
                    piece(st[1])
                elif kind == "amp":
                    dve.wait_ge(small_in, SMALL)
                    dve.wait_ge(turn_free, TURN[("mod", 7)] + 1)
                    dve.scalar_tensor_tensor(out=amp_f[:, :], in0=gt_f[:, :], scalar=1.0,
                                             in1=amp_f[:, :], op0=ALU.add, op1=ALU.mult).then_inc(amp_ready, 1)
                elif kind == "rope":
                    dve.wait_ge(turn_free, TURN[("proj", 1, NB - 1)] + 1)
                    dve.wait_ge(trig_ready, 2)
                    qk = proj[:, :, CSQ:CSV].rearrange("p b (h d) -> p b h d", h=10)
                    x1, x2 = qk[:, :, :, 0:HALF], qk[:, :, :, HALF:ROPE]
                    t = [ropet[:, f] for f in range(4)]
                    dve.tensor_tensor(t[0], x1, trig_b(1), ALU.mult)
                    dve.tensor_tensor(t[1], x2, trig_b(0), ALU.mult)
                    dve.tensor_tensor(t[2], x2, trig_b(1), ALU.mult)
                    link(dve.tensor_tensor(t[3], x1, trig_b(0), ALU.mult))
                    link(dve.tensor_tensor(x1, t[0], t[1], ALU.subtract))
                    dve.tensor_tensor(x2, t[2], t[3], ALU.add).then_inc(rope_done, 1)
                elif kind == "log_sigmoid":
                    dve.wait_ge(logit_copied, 2)
                    dve.scalar_tensor_tensor(out=lexp, in0=loga, scalar=-1.0, in1=loga, op0=ALU.mult, op1=ALU.min)\
                        .then_inc(negabs_ready, 1)
                elif kind == "decay":
                    dve.wait_ge(ln_ready, 1)
                    dve.scalar_tensor_tensor(out=loga, in0=loga, scalar=0.0, in1=lexp, op0=ALU.min,
                                             op1=ALU.subtract).then_inc(loga_ready, 1)
                elif kind == "attn_score":
                    n = st[1]
                    lo = 0 if n else P
                    if n >= 1:
                        dve.wait_ge(probs_turned, 4 * n)
                    else:
                        dve.wait_ge(rope_done, 1)
                    for h in range(SH):
                        bank, o = score_place(h)
                        dve.wait_ge(scores_ready, 4 * n + bank - 2)
                        dve.tensor_tensor_reduce(out=probs[:, h, lo:], in0=ps[bank][:, o + lo:o + 256],
                                                 in1=band[:, lo:], scale=1.0, scalar=-BIG, op0=ALU.add, op1=ALU.max,
                                                 accum_out=sm[:, 0, h:h + 1]).then_inc(scores_masked, 1)
                    dve.wait_ge(scores_masked, SH * (n + 1))
                    link(dve.scalar_tensor_tensor(out=sm[:, 0, :], in0=sm[:, 0, :], scalar=HD ** -0.5, in1=sinks[:, :],
                                                  op0=ALU.mult, op1=ALU.max))
                    link(dve.tensor_scalar(sm[:, 1, :], sm[:, 0, :], -1.0, None, ALU.mult))
                    dve.tensor_tensor(sm[:, 3, :], sinks[:, :], sm[:, 0, :], ALU.subtract).then_inc(rowmax_ready, 1)
                elif kind == "probs_turn":
                    n = st[1]
                    dve.wait_ge(probs_ready, (SH + 1) * (n + 1))
                    link(dve.tensor_tensor(sm[:, 4, :], sm[:, 2, :], sm[:, 3, :], ALU.add))
                    dve.reciprocal(sm[:, 5, :], sm[:, 4, :]).then_inc(sums_ready, 1)
                    for i in range(0, 4, 2):
                        dve.wait_ge(probs_turned, 4 * n + i + 1)
                        src = ps[3 + i][:, :].rearrange("p (h c q) -> p h c q", h=2, c=2)
                        if n == 0:
                            dve.tensor_copy(probsT[:, 2 * i:2 * i + 2, 1, :], src[:, :, 1, :])\
                                .then_inc(probs_copied, 1)
                        else:
                            dve.tensor_copy(probsT[:, 2 * i:2 * i + 2, :, :], src).then_inc(probs_copied, 1)
                elif kind == "attn_value":
                    n = st[1]
                    dve.wait_ge(values_ready, n + 1)
                    dve.wait_ge(sums_ready, n + 1)
                    dve.tensor_tensor(proj[:, n, CSQ:CSK].rearrange("p (h d) -> p h d", h=SH),
                                      ps[3][:, :].rearrange("p (h d) -> p h d", h=SH),
                                      sm[:, 5, :].unsqueeze(2).broadcast_to([P, SH, HD]), ALU.mult)\
                                          .then_inc(attn_out, 1)
                elif kind == "gla_decay":
                    if st[1] == 0:
                        dve.wait_ge(turn_ready, TURN[("proj", 2, 3)] + 1)
                        dve.memset(aT, 0.0)
                        link(dve.memset(state, 0.0))
                elif kind == "gla_operands":
                    n = st[1]
                    dve.wait_ge(gla_exps, 6 * (n + 1))
                    if n >= 1:
                        dve.wait_ge(gla_kv, n)
                        dve.wait_ge(gla_turned, n)
                    q3 = proj[:, n, CQ:CK].rearrange("p (h d) -> p h d", h=GH).unsqueeze(2).broadcast_to([P, GH, 2, DK])
                    e3 = ebr[:, 0:256].rearrange("p (h d) -> p h d", h=GH).unsqueeze(2).broadcast_to([P, GH, 2, DK])
                    dve.tensor_tensor(qdup, q3, e3, ALU.mult)
                    dve.tensor_tensor(kdec, proj[:, n, CK:CV], enb, ALU.mult)
                    link(dve.tensor_tensor(krem, proj[:, n, CK:CV], ebr[:, 256:512], ALU.mult))
                    k3 = krem.rearrange("p (h d) -> p h d", h=GH).unsqueeze(2).broadcast_to([P, GH, 2, DK])
                    m3 = blockm[:, :].rearrange("p (c d) -> p c d", c=2).unsqueeze(1).broadcast_to([P, GH, 2, DK])
                    dve.tensor_tensor(krm, k3, m3, ALU.mult).then_inc(gla_ops, 1)
                    dve.wait_ge(gla_turned, n + 1)
                    if n >= 1:
                        dve.wait_ge(gla_scored, 2 * n)
                        dve.wait_ge(gla_out, n)
                    dve.tensor_copy(gkT, ps[7][:, 256:512].rearrange("p (h t) -> p h t", h=2))\
                        .then_inc(gla_k_copied, 1)
                    dve.wait_ge(gla_q_copied, n + 1)
                    dve.tensor_tensor(gqTm, gqT, blockm[:, :].unsqueeze(1).broadcast_to([P, GH, P]), ALU.mult)\
                        .then_inc(gla_k_copied, 1)
                elif kind == "gla_scores":
                    n = st[1]
                    dve.wait_ge(gla_scored, 2 * (n + 1))
                    if n >= 1:
                        dve.wait_ge(gla_out, n)
                    dve.copy_predicated(out=aT, mask=causal[:, :].bitcast(U32).unsqueeze(1).broadcast_to([P, GH, P]),
                                        data=ps[2][:, :].rearrange("p (h t) -> p h t", h=GH)).then_inc(gla_masked, 1)
                    dve.wait_ge(gla_kv, n + 1)
                    kv = ps[7][:, :].rearrange("p (h v) -> p h v", h=GH)
                    for h in range(GH):
                        dve.scalar_tensor_tensor(out=state[CHUNK:P, h, :], in0=state[0:CHUNK, h, :],
                                                 scalar=dec[0:CHUNK, 2 * h:2 * h + 1], in1=kv[0:CHUNK, h, :],
                                                 op0=ALU.mult, op1=ALU.add).then_inc(gla_state, 1)
                elif kind == "gate_scale":
                    b = st[1]
                    dve.wait_ge(gate_ready, b + 1)
                    link(dve.tensor_tensor(proj[:, b, CG:CA], proj[:, b, CG:CA], gla_g[:, :], ALU.mult))
                    dve.wait_ge(gla_normed, b + 1)
                    dve.tensor_tensor(proj[:, b, CV:CG], proj[:, b, CV:CG], proj[:, b, CG:CA], ALU.mult)\
                        .then_inc(gate_scaled, 1)
                elif kind == "mix_turn":
                    b = st[1]
                    dve.wait_ge(mix_turned, 2 * b + 1)
                    dve.tensor_copy(mixT[b % 2][:, 0:4, :], ps[3][:, :].rearrange("p (k t) -> p k t", k=4))\
                        .then_inc(mix_copied, 1)
                elif kind == "out_proj":
                    b, i = st[1:]
                    dve.wait_ge(out_proj_done, 2 * b + i + 1)
                    dve.wait_ge(turn_free, len(TURN))
                    cols = slice(512 * i, 512 * (i + 1))
                    t = mo_t[:, cols]
                    link(dve.tensor_tensor(t, ps[5 + i][:, :], gt_a[:, cols], ALU.mult))
                    dve.tensor_tensor(xres[:, b, cols], xres[:, b, cols], t, ALU.add).then_inc(x1_done, 1)
                elif kind == "norm2":
                    b = st[1]
                    dve.wait_ge(squares2, 2 * b + 2)
                    dve.scalar_tensor_tensor(out=ssq[:, 8 + b:9 + b], in0=ssq[:, 8 + b:9 + b], scalar=EPS,
                                             in1=ssq[:, 12 + b:13 + b], op0=ALU.add, op1=ALU.add).then_inc(mean2, 1)
                    dve.wait_ge(rstd2, b + 1)
                    if b >= 2:
                        dve.wait_ge(h_stored[b - 2], 2 * 16)
                        dve.wait_ge(h_turned, 2 * (b - 1))
                    for i in range(2):
                        cols = slice(512 * i, 512 * (i + 1))
                        link(dve.scalar_tensor_tensor(out=hb[:, b % 2, cols], in0=xres[:, b, cols],
                                                      scalar=rstd[:, 8 + b:9 + b], in1=amp_f[:, cols],
                                                      op0=ALU.mult, op1=ALU.mult))
                        dve.tensor_tensor(hb[:, b % 2, cols], hb[:, b % 2, cols], sh_f[:, cols], ALU.add)\
                            .then_inc(h_ready, 1)
                elif kind == "router":
                    b = st[1]
                    dve.wait_ge(logits_ready, b + 1)
                    dve.tensor_tensor(lg[:, b, :], ps[0][:, 0:NR], br[:, :], ALU.add).then_inc(logits_read, 1)
                    dve.wait_ge(logits_read, b + 1)
                    best(lg[:, b, 0:NG], gmax[:, b:b + 1], gkey[:, :], gk)
                    link(dve.tensor_scalar(gk, gk, kmax, -BIG, ALU.is_lt, ALU.mult))
                    link(dve.tensor_tensor(M.rearrange("p (g e) -> p g e", g=NG),
                                           lg[:, b, NG:].rearrange("p (g e) -> p g e", g=NG),
                                           gk.unsqueeze(2).broadcast_to([P, NG, EPG]), ALU.add))
                    best(M, t1[:, b:b + 1], ekey[:, :], key)
                    link(dve.tensor_scalar(oh1[:, b, :], key, kmax, None, ALU.is_ge))
                    link(dve.scalar_tensor_tensor(out=M, in0=oh1[:, b, :], scalar=-3.0 * BIG, in1=M,
                                                  op0=ALU.mult, op1=ALU.add))
                    best(M, t2[:, b:b + 1], ekey[:, :], key)
                    link(dve.tensor_scalar(oh2[:, b, :], key, kmax, None, ALU.is_ge))
                    dve.tensor_tensor(cnt[:, b, :], oh1[:, b, :], oh2[:, b, :], ALU.add).then_inc(pairs_marked, 1)
                elif kind == "places":
                    b = st[1]
                    dve.wait_ge(places_ready, b + 1)
                    link(dve.scalar_tensor_tensor(out=M, in0=ps[place_bank(b)][:, 0:NE], scalar=float(NE),
                                                  in1=eidx[:, :], op0=ALU.mult, op1=ALU.add))
                    dve.tensor_tensor(two[:, 0, :], oh1[:, b, :], M, ALU.mult)
                    link(dve.tensor_tensor(two[:, 1, :], oh2[:, b, :], M, ALU.mult))
                    place = rt[:, 40:48].rearrange("p (r b) -> p b r", r=2)[:, b, :]
                    link(dve.tensor_reduce(place, two, AX, ALU.add))
                    dve.tensor_copy(slot_i[:, :].rearrange("p (r b) -> p b r", r=2)[:, b, :], place)\
                        .then_inc(slot_ready, 1)
                elif kind == "gla_output":
                    n = st[1]
                    dve.wait_ge(gla_out, n + 1)
                    kv = ps[7][:, :].rearrange("p (h v) -> p h v", h=GH)
                    for h in range(GH):
                        dve.scalar_tensor_tensor(out=state[0:CHUNK, h, :], in0=state[CHUNK:P, h, :],
                                                 scalar=dec[CHUNK:P, 2 * h + 1:2 * h + 2], in1=kv[CHUNK:P, h, :],
                                                 op0=ALU.mult, op1=ALU.add).then_inc(gla_state, 1)
                    dve.wait_ge(gla_squared, n + 1)
                    link(dve.tensor_reduce(ssq[:, 4:8], osq.rearrange("p (h v) -> p h v", h=GH), AX, ALU.add))
                    dve.tensor_scalar(ssq[:, 4:8], ssq[:, 4:8], 1.0 / DV, EPS, ALU.mult, ALU.add)\
                        .then_inc(gla_mean, 1)
                    dve.wait_ge(gla_rstd, n + 1)
                    dve.tensor_tensor(proj[:, n, CV:CG].rearrange("p (h v) -> p h v", h=GH),
                                      ps[2][:, :].rearrange("p (h v) -> p h v", h=GH),
                                      rstd[:, 4:8].unsqueeze(2).broadcast_to([P, GH, DV]), ALU.mult)\
                                          .then_inc(gla_normed, 1)
            dve.tensor_tensor(eg, lg[:, :, 0:NG], gmax.unsqueeze(2).broadcast_to([P, NB, NG]), ALU.subtract)\
                .then_inc(router_step, 1)
            dve.tensor_tensor(e12, t2, t1, ALU.subtract).then_inc(router_step, 1)
            dve.wait_ge(places_ready, NB + 1)
            link(dve.tensor_reduce(col(48)[:, 0:1], ps[2][:, 0:NE], AX, ALU.max))
            link(dve.tensor_scalar(rt[:, 52:52 + EXTRA], steps[:, :], col(48)[:, 0:1], None, ALU.is_lt))
            link(dve.tensor_reduce(col(60)[:, 0:1], rt[:, 52:52 + EXTRA], AX, ALU.add))
            dve.tensor_copy(extra_i[:, :], col(60)[:, 0:1]).then_inc(router_step, 1)
            dve.wait_ge(router_exps, 2)
            link(dve.tensor_reduce(gate, eg, AX, ALU.add))
            link(dve.tensor_scalar(col(36), e12, 1.0, None, ALU.add))
            link(dve.tensor_tensor(col(36), col(36), gate, ALU.mult))
            link(dve.reciprocal(topw[:, 0, :], col(36)))
            dve.tensor_tensor(topw[:, 1, :], topw[:, 0, :], e12, ALU.mult)

            def turn(e, u):
                dve.wait_ge(e_turned, e + 1)
                dve.tensor_copy(heT[u % 2][:, 0:4, :], ps[0][:, 0:4 * CAP].rearrange("p (k t) -> p k t", k=4))\
                    .then_inc(e_tokens_dve, 1)

            def product(e, u):
                dve.wait_ge(e_silu, e + 1)
                dve.tensor_tensor(eact[u % 2], sg[u % 2].rearrange("p (c t) -> p c t", c=FC),
                                  ps[2 + u % 2][:, FC * CAP:2 * FC * CAP].rearrange("p (c t) -> p c t", c=FC),
                                  ALU.mult).then_inc(e_act, 1)

            def give(e, u, j, first):
                dve.wait_ge(e_down, e + 1)
                if not (first and u < 2):
                    dve.wait_ge(scat[(u + 2) % 4], 16 * (j if u < 2 else j + 1))
                for i in range(2):
                    cols = slice(512 * i, 512 * (i + 1))
                    dve.tensor_tensor(eo[u % 2][:, cols], ps[4 + 2 * (u % 2) + i][0:CAP, :], gt_f[0:CAP, cols],
                                      ALU.mult).then_inc(e_out, 1)

            def group(j, first=False, last=False):
                for u in range(SLOTS):
                    e = SLOTS * j + u
                    product(e, u)
                    if not (last and u == SLOTS - 1):
                        turn(e + 1, u + 1)
                    if not (first and u == 0):
                        give(e - 1, (u + 3) % 4, j - 1 if u == 0 else j, first)
            turn(0, 0)
            group(0, first=True)
            with dve.Fori(1, NE // SLOTS - 1) as j:
                group(j)
            group(NE // SLOTS - 1, last=True)
            give(NE - 1, 3, NE // SLOTS - 1, False)

            dve.wait_ge(router_step, 3)
            extra = dve.value_load(extra_i[0:1, 0:1], min_val=0, max_val=EXTRA)
            with dve.If(extra > 0):
                with dve.Fori(0, extra) as m:
                    with dve.Fori(0, NE) as e:
                        n = m * NE + e
                        dve.wait_ge(ov_turned, n + 1)
                        dve.tensor_copy(heT[0][:, 0:4, :], ps[0][:, 0:4 * CAP].rearrange("p (k t) -> p k t", k=4))\
                            .then_inc(ov_copied, 1)
                        dve.wait_ge(ov_silu, n + 1)
                        dve.tensor_tensor(eact[0], sg[0].rearrange("p (c t) -> p c t", c=FC),
                                          ps[2][:, FC * CAP:2 * FC * CAP].rearrange("p (c t) -> p c t", c=FC),
                                          ALU.mult).then_inc(ov_act, 1)
                        dve.wait_ge(ov_down, n + 1)
                        for i in range(2):
                            cols = slice(512 * i, 512 * (i + 1))
                            dve.tensor_tensor(eo[0][:, cols], ps[4 + i][0:CAP, :], gt_f[0:CAP, cols], ALU.mult)\
                                .then_inc(ov_out, 1)

            def add_experts(b):
                y1, y2 = y_sb[b]
                dve.wait_ge(y_in[0][b], 16)
                for i in range(2):
                    cols = slice(512 * i, 512 * (i + 1))
                    dve.scalar_tensor_tensor(out=y1[:, cols], in0=y1[:, cols], scalar=topw[:, 0, b:b + 1],
                                             in1=xres[:, b, cols], op0=ALU.mult, op1=ALU.add).then_inc(y1_added, 1)
                for i in range(2):
                    cols = slice(512 * i, 512 * (i + 1))
                    dve.wait_ge(y1_added, 2 * b + i + 1)
                    if i == 0:
                        dve.wait_ge(y_in[1][b], 2 * 16)
                    dve.scalar_tensor_tensor(out=xres[:, b, cols], in0=y2[:, cols], scalar=topw[:, 1, b:b + 1],
                                             in1=y1[:, cols], op0=ALU.mult, op1=ALU.add).then_inc(y2_added, 1)

            def finish(b):
                dve.wait_ge(y_squared, 2 * b + 2)
                dve.scalar_tensor_tensor(out=ssq[:, 8 + b:9 + b], in0=ssq[:, 8 + b:9 + b], scalar=EPS,
                                         in1=ssq[:, 12 + b:13 + b], op0=ALU.add, op1=ALU.add).then_inc(y_mean, 1)
                dve.wait_ge(y_rstd, b + 1)
                if b == 0:
                    dve.wait_ge(fg_in, 16)
                for i in range(2):
                    cols = slice(512 * i, 512 * (i + 1))
                    dve.scalar_tensor_tensor(out=xres[:, b, cols], in0=xres[:, b, cols], scalar=rstd[:, 8 + b:9 + b],
                                             in1=fin_g[:, cols], op0=ALU.mult, op1=ALU.mult).then_inc(ynorm, 1)

            for b in range(NB):
                add_experts(b)
                if b >= 1:
                    finish(b - 1)
            finish(NB - 1)

        @block.tensor
        def _(pe):
            pe.wait_ge(consts, CONSTS)
            def turn_x(k):
                for b in range(NB):
                    mm = pe.transpose(ps[X_BANK[k]][:, b * P:(b + 1) * P], scm[:, b, k * P:(k + 1) * P], ident[:, :])
                mm.then_inc(x_turned, 1)

            def sum_columns(i):
                n = FIRST.index(i)
                pe.wait_ge(acc_ready, n + 1)
                for j in range(4):
                    o = (i // 2) * KD + (i % 2) * 4 + j
                    mm = pe.matmul(ps[7][:, o:o + 1], acc[:, n % 2, j * P:(j + 1) * P], ones[:, 0:1],
                                   start=True, stop=True)
                mm.then_inc(mod_col, 1)

            def project(st, ks):
                ch, b = st[1:]
                for k in ks:
                    mm = pe.matmul(ps[bank_of(st)][:, 0:CW[ch]], hT[:, k, b * P:(b + 1) * P], win_sb[ch][:, k, :],
                                   start=k == 0, stop=k == KD - 1)
                return mm

            sum_columns(0)
            pe.wait_ge(xs_ready, NB)
            for k in range(4):
                turn_x(k)
            sum_columns(2)
            pe.wait_ge(h_dve, 2)
            pe.wait_ge(h_act, 2)
            pe.wait_ge(win_in0, 16)
            for b in range(NB - 1):
                project(("proj", 0, b), range(4))
            for k in range(4, 7):
                turn_x(k)
            sum_columns(1)
            sum_columns(3)
            project(("proj", 0, NB - 1), range(4))
            pe.wait_ge(h_dve, 3)
            turn_x(7)
            pe.wait_ge(h_dve, 4)
            pe.wait_ge(h_act, 3)
            project(("proj", 0, 0), range(4, 7))
            pe.wait_ge(h_act, 4)

            for st in MIXER_ORDER:
                kind = st[0]
                if kind == "proj":
                    ch, b = st[1:]
                    r = TURN[st]
                    if b == 0 and ch >= 1:
                        pe.wait_ge([win_in0, win_in1, win_in2, win_in3, win_in4][ch], 16)
                    if r >= 2 and ch >= 1:
                        pe.wait_ge(turn_free, r - 1)
                    done = 0 if ch else 4 if b else 7
                    project(st, range(done, KD)).then_inc(turn_ready, 1)
                elif kind == "mod":
                    r = TURN[st]
                    pe.wait_ge(acc_ready, st[1] + 1)
                    pe.wait_ge(turn_free, r - 1)
                    pe.matmul(ps[bank_of(st)][:, :], ones[:, :], acc[:, st[1] % 2, :], start=True, stop=True)\
                        .then_inc(turn_ready, 1)
                elif kind == "low_turn":
                    pe.wait_ge(turn_free, TURN[("proj", 0, NB - 1)] + 1)
                    for b in range(NB):
                        mm = pe.transpose(ps[7][0:RANK, b * P:(b + 1) * P], proj[:, b, CA:CA + RANK], ident[:, :])
                    mm.then_inc(low_turned, 1)
                elif kind == "decay_logit":
                    pe.wait_ge(small_in, SMALL)
                    pe.wait_ge(low_ready, 1)
                    for b in range(NB):
                        mm = pe.matmul(ps[2 if b < 2 else 7][:, (b % 2) * 256:(b % 2) * 256 + 256],
                                       lowT[0:RANK + 1, b * P:(b + 1) * P], wa2[:, :], start=True, stop=True)
                    mm.then_inc(logit_ready, 1)
                elif kind == "attn_turn":
                    n = st[1]
                    pe.wait_ge(rope_done, 1)
                    if n >= 1:
                        pe.wait_ge(probs_copied, 4 * n)
                        if n >= 2:
                            pe.wait_ge(attn_out, n - 1)
                    for i in range(4):
                        pe.transpose(ps[3][:, i * P:(i + 1) * P], proj[:, n, CSQ + i * P:CSQ + (i + 1) * P],
                                     ident[:, :])
                    pe.transpose(ps[4][:, 0:P], proj[:, n, CSK:CSV], ident[:, :]).then_inc(attn_turned, 1)
                elif kind == "attn_score":
                    n = st[1]
                    pe.wait_ge(attn_copied, 5 * (n + 1))
                    if n >= 1:
                        pe.wait_ge(probs_copied, 4 * n)
                        pe.wait_ge(attn_out, n)
                    for h in range(SH):
                        kv, i = h // 4, h // 2
                        rows = slice((h % 2) * HD, (h % 2 + 1) * HD)
                        bank, o = score_place(h)
                        if n >= 1:
                            mm = pe.matmul(ps[bank][:, o:o + 256], sqT[rows, i, :],
                                           skT[rows, kv, n - 1:n + 1, :].rearrange("p b s -> p (b s)"),
                                           start=True, stop=True)
                        else:
                            mm = pe.matmul(ps[bank][:, o + P:o + 256], sqT[rows, i, :], skT[rows, kv, n, :],
                                           start=True, stop=True)
                        if h % 4 >= 2:
                            mm.then_inc(scores_ready, 1)
                elif kind == "probs_turn":
                    n = st[1]
                    pe.wait_ge(probs_ready, (SH + 1) * (n + 1))
                    if n >= 1:
                        pe.wait_ge(attn_out, n)
                    for h in range(SH):
                        for cc in range(0 if n else 1, 2):
                            mm = pe.transpose(ps[3 + h // 2][:, (h % 2) * 256 + cc * P:(h % 2) * 256 + (cc + 1) * P],
                                              probs[:, h, cc * P:(cc + 1) * P], ident[:, :])
                        if h % 2:
                            mm.then_inc(probs_turned, 1)
                elif kind == "attn_value":
                    n = st[1]
                    pe.wait_ge(probs_copied, 4 * (n + 1))
                    if n + 1 < NB:
                        pe.wait_ge(attn_copied, 5 * (n + 2))
                    for h in range(SH):
                        kv = h // 4
                        for cc in range(0 if n else 1, 2):
                            mm = pe.matmul(ps[3][:, h * HD:(h + 1) * HD], probsT[:, h, cc, :],
                                           proj[:, n - 1 + cc, CSV + kv * HD:CSV + (kv + 1) * HD],
                                           start=cc == (0 if n else 1), stop=cc == 1)
                    mm.then_inc(values_ready, 1)
                elif kind == "gla_decay":
                    n = st[1]
                    if n == 0:
                        pe.wait_ge(loga_ready, 1)
                    else:
                        pe.wait_ge(gla_normed, n)
                        pe.wait_ge(gla_state, 2 * GH * n)
                    pe.matmul(ps[2][:, 0:256], u16[:, :], loga[:, n, :], start=True, stop=True)
                    pe.matmul(ps[2][:, 256:512], r16[:, :], loga[:, n, :], start=True, stop=True)
                    for i in range(2):
                        mm = pe.matmul(ps[7][:, 2 * i:2 * i + 2], loga[:, n, i * P:(i + 1) * P], ind16[:, :],
                                       start=True, stop=True)
                    mm.then_inc(gla_logs, 1)
                elif kind == "gla_operands":
                    n = st[1]
                    pe.wait_ge(gla_ops, n + 1)
                    pe.wait_ge(gla_exps, 6 * (n + 1))
                    for h in range(GH):
                        pe.transpose(ps[2][:, h * P:(h + 1) * P], qdup[:, h].rearrange("p c d -> p (c d)"), ident[:, :])
                    for i in range(2):
                        mm = pe.transpose(ps[7][:, 256 + i * P:256 + (i + 1) * P], kdec[:, i * P:(i + 1) * P],
                                          ident[:, :])
                    mm.then_inc(gla_turned, 1)
                elif kind == "gla_scores":
                    n = st[1]
                    pe.wait_ge(gla_k_copied, 2 * (n + 1))
                    pe.wait_ge(gla_q_copied, n + 1)
                    for odd in range(2):
                        for h in range(odd, GH, 2):
                            rows = slice(odd * DK, (odd + 1) * DK)
                            mm = pe.matmul(ps[2][:, h * P:(h + 1) * P], gkT[rows, h // 2, :], gqT[rows, h, :],
                                           start=True, stop=True)
                        mm.then_inc(gla_scored, 1)
                        if odd == 0:
                            pe.wait_ge(gla_scored, 2 * n + 1)
                    pe.wait_ge(turn_free, TURN[("proj", 3, n)] + 1)
                    for h in range(GH):
                        mm = pe.matmul(ps[7][:, h * DV:(h + 1) * DV], krm[:, h].rearrange("p c d -> p (c d)"),
                                       proj[:, n, CV + h * DV:CV + (h + 1) * DV], start=True, stop=True)
                    mm.then_inc(gla_kv, 1)
                elif kind == "mix_turn":
                    b = st[1]
                    if b == 0:
                        pe.wait_ge(attn_out, NB)
                    else:
                        pe.wait_ge(mix_copied, 2 * b)
                    pe.wait_ge(gate_scaled, b + 1)
                    for i in range(2):
                        for k in range(4 * i, 4 * i + 4):
                            lo = (CV if i == 0 else CSQ) + (k % 4) * P
                            mm = pe.transpose(ps[3 + i][:, (k % 4) * P:(k % 4 + 1) * P], proj[:, b, lo:lo + P],
                                              ident[:, :])
                        mm.then_inc(mix_turned, 1)
                elif kind == "out_proj":
                    b, i = st[1:]
                    if b == 0:
                        pe.wait_ge(wout_in, 16)
                    else:
                        pe.wait_ge(x1_done, 2 * b - 1 + i)
                    pe.wait_ge(mix_copied, 2 * b + 2)
                    for k in range(KD):
                        mm = pe.matmul(ps[5 + i][:, :], mixT[b % 2][:, k, :], wout_sb[:, k, 512 * i:512 * (i + 1)],
                                       start=k == 0, stop=k == KD - 1)
                    mm.then_inc(out_proj_done, 1)
                elif kind == "h_turn":
                    b = st[1]
                    pe.wait_ge(turn_free, len(TURN))
                    if b >= 1:
                        pe.wait_ge(logits_read, b)
                    for i in range(2):
                        pe.wait_ge(h_ready, 2 * b + i + 1)
                        for k in range(4 * i, 4 * i + 4):
                            mm = pe.transpose(ps[i][:, (k % 4) * P:(k % 4 + 1) * P], hb[:, b % 2, k * P:(k + 1) * P],
                                              ident[:, :])
                        mm.then_inc(h_turned, 1)
                elif kind == "router":
                    b = st[1]
                    pe.wait_ge(h_col, 2 * b + 2)
                    for k in range(KD):
                        mm = pe.matmul(ps[0][:, 0:NR], hcT[:, k, :], wr[:, k, :], start=k == 0, stop=k == KD - 1)
                    mm.then_inc(logits_ready, 1)
                elif kind == "gla_output":
                    n = st[1]
                    pe.wait_ge(gla_masked, n + 1)
                    pe.wait_ge(gla_state, 2 * GH * n + GH)
                    for h in range(GH):
                        o = ps[2][:, h * DV:(h + 1) * DV]
                        pe.matmul(o, aT[:, h, :], proj[:, n, CV + h * DV:CV + (h + 1) * DV], start=True, stop=False)
                        mm = pe.matmul(o, gqTm[:, h, :], state[:, h, :], start=False, stop=True)
                    mm.then_inc(gla_out, 1)
                elif kind == "places":
                    b = st[1]
                    pe.wait_ge(pairs_marked, b + 1)
                    pe.wait_ge(gla_normed, NB)
                    if b >= 2:
                        pe.wait_ge(slot_ready, b - 1)
                    cnt = rt[:, 64:64 + NB * NE].rearrange("p (b n) -> p b n", b=NB)
                    here = ps[place_bank(b)][:, 0:NE]
                    for a in range(b):
                        pe.matmul(here, ones[:, :], cnt[:, a, :], start=a == 0, stop=False)
                    pe.matmul(here, ustrict[:, :], cnt[:, b, :], start=b == 0, stop=True).then_inc(places_ready, 1)
                    if b == NB - 1:
                        pe.wait_ge(slot_ready, b)
                        for a in range(NB):
                            mm = pe.matmul(ps[2][:, 0:NE], ones[:, :], cnt[:, a, :],
                                           start=a == 0, stop=a == NB - 1)
                        mm.then_inc(places_ready, 1)

            def turn_tile(src, done):
                for i in range(2):
                    for k in range(4 * i, 4 * i + 4):
                        rows = src.rearrange("t (p k) -> t k p", k=KD)[:, k, :]
                        mm = pe.transpose(ps[i][:, (k % 4) * CAP:(k % 4 + 1) * CAP], rows, ident[0:CAP, 0:CAP])
                mm.then_inc(done, 1)

            def gate_up(bank, w, u, hx, done):
                for m, wt in enumerate((wg_sb[w], wu_sb[w])):
                    for f in range(FC):
                        o = (m * FC + f) * CAP
                        for k in range(KD):
                            mm = pe.matmul(ps[bank][:, o:o + CAP], wt[:, k, f * P:(f + 1) * P], hx[:, k, :],
                                           start=k == 0, stop=k == KD - 1)
                mm.then_inc(done, 1)

            def down_tile(bank, w, a, done):
                for i in range(2):
                    for f in range(FC):
                        mm = pe.matmul(ps[bank + i][0:CAP, :], a[:, f, :], wd_sb[w][:, f, 512 * i:512 * (i + 1)],
                                       start=f == 0, stop=f == FC - 1)
                mm.then_inc(done, 1)

            def turn(e, u, j):
                pe.wait_ge(gath[u], 16 * (j + 1))
                turn_tile(hg[u], e_turned)

            def down(e, u, j, first):
                pe.wait_ge(e_act, e + 1)
                pe.wait_ge(wd_sem[u], 16 * (j + 1))
                if not (first and u < 2):
                    pe.wait_ge(e_out, 2 * (e - 1))
                down_tile(4 + 2 * (u % 2), u, eact[u % 2], e_down)

            def group(j, first=False, last=False):
                for u in range(SLOTS):
                    e = SLOTS * j + u
                    pe.wait_ge(e_tokens_act, e + 1)
                    pe.wait_ge(e_tokens_dve, e + 1)
                    pe.wait_ge(w_sem[u], 32 * (j + 1))
                    if not (first and u < 2):
                        pe.wait_ge(e_act, e - 1)
                    gate_up(2 + u % 2, u, u, heT[u % 2], e_gate_up)
                    if not (last and u == SLOTS - 1):
                        turn(e + 1, (u + 1) % 4, j + 1 if u == SLOTS - 1 else j)
                    if not (first and u == 0):
                        down(e - 1, (u + 3) % 4, j - 1 if u == 0 else j, first)
            pe.wait_ge(slot_ready, NB)
            pe.wait_ge(router_step, 3)
            turn(0, 0, 0)
            group(0, first=True)
            with pe.Fori(1, NE // SLOTS - 1) as j:
                group(j)
            group(NE // SLOTS - 1, last=True)
            down(NE - 1, 3, NE // SLOTS - 1, False)

            extra = pe.value_load(extra_i[0:1, 0:1], min_val=0, max_val=EXTRA)
            with pe.If(extra > 0):
                pe.wait_ge(e_out, 2 * NE)
                with pe.Fori(0, extra) as m:
                    with pe.Fori(0, NE) as e:
                        n = m * NE + e
                        pe.wait_ge(ov_gath, (n + 1) * 16)
                        turn_tile(hg[0], ov_turned)
                        pe.wait_ge(ov_copied, (n + 1) * 2)
                        pe.wait_ge(ov_w, (n + 1) * 48)
                        gate_up(2, 0, 0, heT[0], ov_gate_up)
                        pe.wait_ge(ov_act, n + 1)
                        down_tile(4, 0, eact[0], ov_down)


_INS = ["x", "c", "positions", "ada_w", "ada_b", "norm_mix_g", "w_in", "gla_w_a2", "gla_b_a2", "gla_norm_g",
        "swa_sinks", "w_out", "norm_ffn_g", "w_grp", "b_grp", "w_exp", "b_exp", "w_gate", "w_up", "w_down",
        "final_norm_g"]


def kernel(**inputs):
    import concourse.bacc as bacc
    from concourse.bass_utils import run_bass_kernel_spmd

    nc = bacc.Bacc("TRN2", target_bir_lowering=False, num_devices=1)
    arrays, args = {}, []
    for name in _INS:
        a = np.ascontiguousarray(inputs[name])
        arrays[f"in_{name}"] = a
        args.append(nc.dram_tensor(f"in_{name}", a.shape, mybir.dt.from_np(a.dtype), kind="ExternalInput").ap())
    out = nc.dram_tensor("out_x", [1, SEQ, D], F32, kind="ExternalOutput").ap()
    layer_kernel(nc, *args, out)
    r = run_bass_kernel_spmd(nc, [arrays], core_ids=[0])
    return r.results[0]["out_x"]
```
